# Optimizing a Trainium2 kernel written in Bass

```python
import math
import jax, jax.numpy as jnp
from jax import lax
import numpy as np

D_MODEL = 1024
BATCH = 1
SEQ = 256
DEPTH = 1

GRID_W = 64
CTX_LEN = 256
N_MIXERS = 2
N_CONV_LAYERS = (DEPTH + N_MIXERS - 1) // N_MIXERS
N_DELTA_LAYERS = DEPTH // N_MIXERS
CONV_WIDTH = 31
DN_HEADS = 8
DN_HEAD_DIM = D_MODEL // DN_HEADS
DN_SHORT_CONV = 5
DN_CHUNK = 64
N_DIRS = 2
DN_QKV = 3 * D_MODEL
DN_IN = 4 * D_MODEL + 2 * N_DIRS * DN_HEADS
FFN_HIDDEN = 4 * D_MODEL
EPS = 1e-6


def rms_norm(x, g):
    xf = x.astype(jnp.float32)
    y = xf * lax.rsqrt(jnp.mean(xf * xf, axis=-1, keepdims=True) + EPS)
    return (y * g.astype(jnp.float32)).astype(x.dtype)

def layer_norm(x, g, b):
    xf = x.astype(jnp.float32)
    mu = jnp.mean(xf, axis=-1, keepdims=True)
    xc = xf - mu
    y = xc * lax.rsqrt(jnp.mean(xc * xc, axis=-1, keepdims=True) + EPS)
    return (y * g.astype(jnp.float32) + b.astype(jnp.float32)).astype(x.dtype)

def l2_norm(x):
    xf = x.astype(jnp.float32)
    return xf * lax.rsqrt(jnp.sum(xf * xf, axis=-1, keepdims=True) + EPS)

def modulate(h, shift, scale):
    return h * (1.0 + scale) + shift

def dwconv(x, w):
    K, C = w.shape
    return lax.conv_general_dilated(
        x, w[:, None, :].astype(x.dtype), window_strides=(1,),
        padding=[(K // 2, K // 2)], dimension_numbers=('NWC', 'WIO', 'NWC'),
        feature_group_count=C)

def conformer_conv(h, n_seg, w_pw1, b_pw1, w_dw, b_dw, ln_g, ln_b, w_pw2, b_pw2):
    B, L, D = h.shape
    u = h @ w_pw1 + b_pw1
    a, gate = jnp.split(u, 2, axis=-1)
    u = a * jax.nn.sigmoid(gate)
    u = dwconv(u.reshape(B * n_seg, L // n_seg, D), w_dw).reshape(B, L, D) + b_dw
    u = jax.nn.silu(layer_norm(u, ln_g, ln_b))
    return u @ w_pw2 + b_pw2

def gated_delta_chunked(q, k, v, g, beta, state):
    B, H, L, DK = q.shape
    DV = v.shape[-1]
    C = DN_CHUNK
    NC = L // C
    q = q.reshape(B, H, NC, C, DK)
    k = k.reshape(B, H, NC, C, DK)
    v = v.reshape(B, H, NC, C, DV)
    g = g.reshape(B, H, NC, C)
    beta = beta.reshape(B, H, NC, C)
    G = jnp.cumsum(g, axis=-1)
    lower = jnp.tril(jnp.ones((C, C), dtype=bool))
    strict = jnp.tril(jnp.ones((C, C), dtype=bool), -1)
    decay = jnp.exp(jnp.where(lower, G[..., :, None] - G[..., None, :], -jnp.inf))
    kk = jnp.einsum('bhncd,bhnsd->bhncs', k, k)
    a_mat = jnp.where(strict, beta[..., :, None] * kk * decay, 0.0)
    eye = jnp.broadcast_to(jnp.eye(C, dtype=q.dtype), a_mat.shape)
    rhs = jnp.concatenate([beta[..., None] * v, (beta * jnp.exp(G))[..., None] * k], axis=-1)
    sol = lax.linalg.triangular_solve(a_mat + eye, rhs, left_side=True, lower=True,
                                      unit_diagonal=True)
    u, w = sol[..., :DV], sol[..., DV:]
    qk = jnp.einsum('bhncd,bhnsd->bhncs', q, k) * decay
    qg = q * jnp.exp(G)[..., None]
    kd = k * jnp.exp(G[..., -1:] - G)[..., None]
    chunk_decay = jnp.exp(G[..., -1])
    xs = tuple(jnp.moveaxis(t, 2, 0) for t in (u, w, qg, qk, kd, chunk_decay))

    def step(S, inp):
        u_c, w_c, qg_c, qk_c, kd_c, cd_c = inp
        v_new = u_c - jnp.einsum('bhcd,bhde->bhce', w_c, S)
        o_c = (jnp.einsum('bhcd,bhde->bhce', qg_c, S)
               + jnp.einsum('bhcs,bhse->bhce', qk_c, v_new))
        S = S * cd_c[..., None, None] + jnp.einsum('bhcd,bhce->bhde', kd_c, v_new)
        return S, o_c

    state, o = lax.scan(step, state, xs)
    o = jnp.moveaxis(o, 0, 2).reshape(B, H, L, DV)
    return o, state

def gdn_project(h, w_in, conv_w, a_log, dt_bias):
    B, L, _ = h.shape
    p = h @ w_in
    qkv = jax.nn.silu(dwconv(p[..., :DN_QKV], conv_w))
    z = p[..., DN_QKV:4 * D_MODEL].reshape(B, L, DN_HEADS, DN_HEAD_DIM)
    ab = p[..., 4 * D_MODEL:].astype(jnp.float32).reshape(B, L, 2, N_DIRS, DN_HEADS)
    to_heads = lambda t: t.reshape(B, L, DN_HEADS, DN_HEAD_DIM).transpose(0, 2, 1, 3)
    q, k, v = jnp.split(qkv, 3, axis=-1)
    q = l2_norm(to_heads(q)) * (DN_HEAD_DIM ** -0.5)
    k = l2_norm(to_heads(k))
    v = to_heads(v).astype(jnp.float32)
    g = -jnp.exp(a_log.astype(jnp.float32)) * jax.nn.softplus(ab[:, :, 0] + dt_bias.astype(jnp.float32))
    beta = jax.nn.sigmoid(ab[:, :, 1])
    return q, k, v, z, jnp.transpose(g, (2, 0, 3, 1)), jnp.transpose(beta, (2, 0, 3, 1))

def gdn_output(o, z, norm_g, w_o, dtype):
    B, H, L, DV = o.shape
    o = rms_norm(o.transpose(0, 2, 1, 3), norm_g) * jax.nn.silu(z.astype(jnp.float32))
    return o.reshape(B, L, H * DV).astype(dtype) @ w_o

def gated_deltanet_bidir(hc, hl, w_in, conv_w, a_log, dt_bias, norm_g, w_o):
    qc, kc, vc, zc, gc, bc = gdn_project(hc, w_in, conv_w, a_log, dt_bias)
    ql, kl, vl, zl, gl, bl = gdn_project(hl, w_in, conv_w, a_log, dt_bias)
    B = hl.shape[0]
    s0 = jnp.zeros((B, DN_HEADS, DN_HEAD_DIM, DN_HEAD_DIM), jnp.float32)
    fl = lambda t: jnp.flip(t, axis=2)
    oc_f, sc_f = gated_delta_chunked(qc, kc, vc, gc[0], bc[0], s0)
    ol_f, _ = gated_delta_chunked(ql, kl, vl, gl[0], bl[0], sc_f)
    oc_b, sc_b = gated_delta_chunked(fl(qc), fl(kc), fl(vc), fl(gc[1]), fl(bc[1]), s0)
    ol_b, _ = gated_delta_chunked(fl(ql), fl(kl), fl(vl), fl(gl[1]), fl(bl[1]), sc_b)
    yc = gdn_output(oc_f + fl(oc_b), zc, norm_g, w_o, hc.dtype)
    yl = gdn_output(ol_f + fl(ol_b), zl, norm_g, w_o, hl.dtype)
    return yc, yl

def sq_relu_mlp(h, w1, w2):
    return jnp.square(jax.nn.relu(h @ w1)) @ w2

def first_inputs(seed: int = 0) -> dict:
    key = jax.random.key(seed)
    ks = jax.random.split(key, 26)
    D = D_MODEL
    NA, NB = N_CONV_LAYERS, N_DELTA_LAYERS
    nrm = lambda k, shape, s: jax.random.normal(k, shape, jnp.float32) * s
    dt = jnp.exp(jax.random.uniform(ks[20], (NB, N_DIRS, DN_HEADS), jnp.float32,
                                    minval=math.log(1e-3), maxval=math.log(1e-1)))
    return {
        "x": nrm(ks[0], (BATCH, SEQ, D), 1.0),
        "c": nrm(ks[1], (BATCH, D), 1.0),
        "ctx": nrm(ks[2], (BATCH, CTX_LEN, D), 1.0),
        "c_ctx": nrm(ks[3], (D,), 1.0),
        "w_mod": nrm(ks[4], (DEPTH, D, 6 * D), 0.5 * D ** -0.5),
        "b_mod": nrm(ks[5], (DEPTH, 6 * D), 0.02),
        "norm1_g": 1.0 + nrm(ks[6], (DEPTH, D), 0.02),
        "norm2_g": 1.0 + nrm(ks[7], (DEPTH, D), 0.02),
        "final_g": 1.0 + nrm(ks[8], (D,), 0.02),
        "conv_w_pw1": nrm(ks[9], (NA, D, 2 * D), D ** -0.5),
        "conv_b_pw1": nrm(ks[10], (NA, 2 * D), 0.02),
        "conv_w_dw": nrm(ks[11], (NA, CONV_WIDTH, D), CONV_WIDTH ** -0.5),
        "conv_b_dw": nrm(ks[12], (NA, D), 0.02),
        "conv_ln_g": 1.0 + nrm(ks[13], (NA, D), 0.02),
        "conv_ln_b": nrm(ks[14], (NA, D), 0.02),
        "conv_w_pw2": nrm(ks[15], (NA, D, D), D ** -0.5),
        "conv_b_pw2": nrm(ks[16], (NA, D), 0.02),
        "dn_w_in": nrm(ks[17], (NB, D, DN_IN), D ** -0.5),
        "dn_conv_w": nrm(ks[18], (NB, DN_SHORT_CONV, DN_QKV), DN_SHORT_CONV ** -0.5),
        "dn_a_log": jnp.log(jax.random.uniform(ks[19], (NB, N_DIRS, DN_HEADS), jnp.float32,
                                               minval=1.0, maxval=16.0)),
        "dn_dt_bias": dt + jnp.log(-jnp.expm1(-dt)),
        "dn_norm_g": 1.0 + nrm(ks[21], (NB, DN_HEAD_DIM), 0.02),
        "dn_w_o": nrm(ks[22], (NB, D, D), D ** -0.5),
        "mlp_w1": nrm(ks[23], (DEPTH, D, FFN_HIDDEN), D ** -0.5),
        "mlp_w2": nrm(ks[24], (DEPTH, FFN_HIDDEN, D), FFN_HIDDEN ** -0.5),
    }

def first_block(x, c, ctx, c_ctx, w_mod, b_mod, norm1_g, norm2_g, final_g,
              conv_w_pw1, conv_b_pw1, conv_w_dw, conv_b_dw, conv_ln_g, conv_ln_b,
              conv_w_pw2, conv_b_pw2, dn_w_in, dn_conv_w, dn_a_log, dn_dt_bias,
              dn_norm_g, dn_w_o, mlp_w1, mlp_w2):
    rows = x.shape[1] // GRID_W
    xl, xc = x, ctx
    sc_l = jax.nn.silu(c)
    sc_c = jax.nn.silu(c_ctx)
    for i in range(DEPTH):
        last = i == DEPTH - 1
        j = i // N_MIXERS
        mod_l = (sc_l @ w_mod[i] + b_mod[i])[:, None, :]
        mod_c = (sc_c @ w_mod[i] + b_mod[i])[None, None, :]
        sh1_l, s1_l, g1_l, sh2_l, s2_l, g2_l = jnp.split(mod_l, 6, axis=-1)
        sh1_c, s1_c, g1_c, sh2_c, s2_c, g2_c = jnp.split(mod_c, 6, axis=-1)
        hl = modulate(rms_norm(xl, norm1_g[i]), sh1_l, s1_l)
        hc = modulate(rms_norm(xc, norm1_g[i]), sh1_c, s1_c)
        if i % N_MIXERS == 0:
            conv_p = (conv_w_pw1[j], conv_b_pw1[j], conv_w_dw[j], conv_b_dw[j],
                      conv_ln_g[j], conv_ln_b[j], conv_w_pw2[j], conv_b_pw2[j])
            yl = conformer_conv(hl, rows, *conv_p)
            if not last:
                yc = conformer_conv(hc, 1, *conv_p)
        else:
            yc, yl = gated_deltanet_bidir(hc, hl, dn_w_in[j], dn_conv_w[j], dn_a_log[j],
                                          dn_dt_bias[j], dn_norm_g[j], dn_w_o[j])
        xl = xl + g1_l * yl
        xl = xl + g2_l * sq_relu_mlp(modulate(rms_norm(xl, norm2_g[i]), sh2_l, s2_l),
                                     mlp_w1[i], mlp_w2[i])
        if not last:
            xc = xc + g1_c * yc
            xc = xc + g2_c * sq_relu_mlp(modulate(rms_norm(xc, norm2_g[i]), sh2_c, s2_c),
                                         mlp_w1[i], mlp_w2[i])
    return rms_norm(xl, final_g)


DEPTH_2 = 2

BLOCK_Q = 128
MLA_HEADS = 6
MLA_Q_LORA = 384
MLA_KV_LORA = 256
MLA_NOPE = 64
MLA_ROPE = 32
MLA_V = 64
ROPE_THETA = 10000.0
DSA_HEADS = 5
DSA_DIM = 64
IDX_HEADS = 8
IDX_DIM = 64
DSA_TOPK = 256
SB_HEADS = 5
SB_DIM = 64
REL_BUCKETS = 32
REL_MAX_DIST = 128
D_FF = -(-8 * D_MODEL // (3 * 256)) * 256
PLE_DIM = 256

MIX_WIDTH = MLA_HEADS * MLA_V + DSA_HEADS * DSA_DIM + SB_HEADS * SB_DIM
IN_SPLITS = (MLA_Q_LORA, MLA_KV_LORA, MLA_ROPE,
             DSA_HEADS * DSA_DIM, DSA_DIM, DSA_DIM,
             IDX_HEADS * IDX_DIM, IDX_DIM, IDX_HEADS,
             SB_HEADS * SB_DIM, SB_HEADS * SB_DIM, SB_HEADS * SB_DIM)
D_IN = sum(IN_SPLITS)


def rms_norm_2(x, g):
    xf = x.astype(jnp.float32)
    y = xf * lax.rsqrt(jnp.mean(xf * xf, axis=-1, keepdims=True) + EPS)
    return (y * g.astype(jnp.float32)).astype(x.dtype)

def apply_rope(x, pos):
    half = x.shape[-1] // 2
    inv = ROPE_THETA ** (-jnp.arange(half, dtype=jnp.float32) / half)
    ang = pos.astype(jnp.float32)[:, None] * inv[None, :]
    cos = jnp.cos(ang)[None, :, None, :].astype(x.dtype)
    sin = jnp.sin(ang)[None, :, None, :].astype(x.dtype)
    x1, x2 = x[..., :half], x[..., half:]
    return jnp.concatenate([x1 * cos - x2 * sin, x1 * sin + x2 * cos], axis=-1)

def t5_bucket(dist):
    max_exact = REL_BUCKETS // 2
    d = jnp.maximum(dist, 1).astype(jnp.float32)
    large = max_exact + (jnp.log(d / max_exact) / math.log(REL_MAX_DIST / max_exact)
                         * (REL_BUCKETS - max_exact)).astype(jnp.int32)
    large = jnp.minimum(large, REL_BUCKETS - 1)
    return jnp.where(dist < max_exact, dist, large)

def mixer_block(q0, pos, mla_q, mla_k, mla_v, dsa_q, dsa_k, dsa_v,
                idx_q, idx_k, idx_w, sb_q, sb_k, sb_v, rel_bias, topk):
    B = mla_q.shape[0]
    sl = lambda a: lax.dynamic_slice_in_dim(a, q0, BLOCK_Q, axis=1)
    qpos = q0 + jnp.arange(BLOCK_Q, dtype=jnp.int32)
    causal = pos[None, :] <= qpos[:, None]
    strict = pos[None, :] < qpos[:, None]

    s = jnp.einsum('bqhd,bkhd->bhqk', sl(mla_q), mla_k).astype(jnp.float32) * (MLA_NOPE + MLA_ROPE) ** -0.5
    s = jnp.where(causal[None, None], s, -jnp.inf)
    pr = jax.nn.softmax(s, axis=-1).astype(mla_v.dtype)
    o_mla = jnp.einsum('bhqk,bkhd->bqhd', pr, mla_v).reshape(B, BLOCK_Q, MLA_HEADS * MLA_V)

    ilog = jnp.einsum('bqhd,bkd->bqhk', sl(idx_q), idx_k) * IDX_DIM ** -0.5
    isc = jnp.einsum('bqhk,bqh->bqk', jax.nn.relu(ilog), sl(idx_w)).astype(jnp.float32)
    isc = jnp.where(causal[None], isc, -jnp.inf)
    _, sel = lax.top_k(isc, topk)
    valid = sel <= qpos[None, :, None]
    gather = jax.vmap(lambda a, i: a[i])
    kg = gather(dsa_k, sel)
    vg = gather(dsa_v, sel)
    bias = rel_bias[t5_bucket(jnp.maximum(qpos[None, :, None] - sel, 0))]
    a = (jnp.einsum('bqhd,bqjd->bhqj', sl(dsa_q), kg).astype(jnp.float32) * DSA_DIM ** -0.5
         + jnp.transpose(bias, (0, 3, 1, 2)).astype(jnp.float32))
    a = jnp.where(valid[:, None], a, -jnp.inf)
    pa = jax.nn.softmax(a, axis=-1).astype(vg.dtype)
    o_dsa = jnp.einsum('bhqj,bqjd->bqhd', pa, vg).reshape(B, BLOCK_Q, DSA_HEADS * DSA_DIM)

    z = jnp.einsum('bqhd,bkhd->bhqk', sl(sb_q), sb_k).astype(jnp.float32) * SB_DIM ** -0.5
    m = strict[None, None]
    l1m = jnp.where(m, jax.nn.log_sigmoid(-z), 0.0)
    suffix = lax.cumsum(l1m, axis=3, reverse=True) - l1m
    w = jnp.where(m, jnp.exp(jax.nn.log_sigmoid(z) + suffix), 0.0).astype(sb_v.dtype)
    o_sb = jnp.einsum('bhqk,bkhd->bqhd', w, sb_v).reshape(B, BLOCK_Q, SB_HEADS * SB_DIM)

    return jnp.concatenate([o_mla, o_dsa, o_sb], axis=-1)

def second_inputs(seed: int = 0) -> dict:
    key = jax.random.key(seed)
    ks = jax.random.split(key, 18)
    f32 = jnp.float32
    nrm = lambda k, shape, scale: jax.random.normal(k, shape, f32) * scale
    gain = lambda k, shape: 1.0 + 0.05 * jax.random.normal(k, shape, f32)
    return {
        "x": nrm(ks[0], (BATCH, SEQ, D_MODEL), 1.0),
        "p": nrm(ks[1], (DEPTH_2, BATCH, SEQ, PLE_DIM), 1.0),
        "w_in": nrm(ks[2], (DEPTH_2, D_MODEL, D_IN), D_MODEL ** -0.5),
        "attn_norm": gain(ks[3], (DEPTH_2, D_MODEL)),
        "mla_q_norm": gain(ks[4], (DEPTH_2, MLA_Q_LORA)),
        "mla_w_uq": nrm(ks[5], (DEPTH_2, MLA_Q_LORA, MLA_HEADS * (MLA_NOPE + MLA_ROPE)), MLA_Q_LORA ** -0.5),
        "mla_kv_norm": gain(ks[6], (DEPTH_2, MLA_KV_LORA)),
        "mla_w_ukv": nrm(ks[7], (DEPTH_2, MLA_KV_LORA, MLA_HEADS * (MLA_NOPE + MLA_V)), MLA_KV_LORA ** -0.5),
        "rel_bias": nrm(ks[8], (REL_BUCKETS, DSA_HEADS), 0.5),
        "w_o": nrm(ks[9], (DEPTH_2, MIX_WIDTH, D_MODEL), MIX_WIDTH ** -0.5),
        "ffn_norm": gain(ks[10], (DEPTH_2, D_MODEL)),
        "w_gate": nrm(ks[11], (DEPTH_2, D_MODEL, D_FF), D_MODEL ** -0.5),
        "w_up": nrm(ks[12], (DEPTH_2, D_MODEL, D_FF), D_MODEL ** -0.5),
        "w_down": nrm(ks[13], (DEPTH_2, D_FF, D_MODEL), D_FF ** -0.5),
        "ple_norm": gain(ks[14], (DEPTH_2, D_MODEL)),
        "w_ple_gate": nrm(ks[15], (DEPTH_2, D_MODEL, D_MODEL), D_MODEL ** -0.5),
        "w_ple_proj": nrm(ks[16], (DEPTH_2, PLE_DIM, D_MODEL), PLE_DIM ** -0.5),
        "final_norm": gain(ks[17], (D_MODEL,)),
    }

def second_block(x, p, w_in, attn_norm, mla_q_norm, mla_w_uq, mla_kv_norm, mla_w_ukv,
              rel_bias, w_o, ffn_norm, w_gate, w_up, w_down, ple_norm, w_ple_gate,
              w_ple_proj, final_norm):
    B, S, _ = x.shape
    n_blk = S // BLOCK_Q
    topk = min(DSA_TOPK, S // 4)
    pos = jnp.arange(S, dtype=jnp.int32)
    offsets = [int(o) for o in np.cumsum(IN_SPLITS)[:-1]]
    starts = jnp.arange(n_blk, dtype=jnp.int32) * BLOCK_Q
    h = x
    for i in range(DEPTH_2):
        hn = rms_norm_2(h, attn_norm[i])
        proj = hn @ w_in[i]
        (c_q, c_kv, k_rope, dq, dk, dv, iq, ik, iw, sq, sk, sv) = jnp.split(proj, offsets, axis=-1)

        q = (rms_norm_2(c_q, mla_q_norm[i]) @ mla_w_uq[i]).reshape(B, S, MLA_HEADS, MLA_NOPE + MLA_ROPE)
        q = jnp.concatenate([q[..., :MLA_NOPE], apply_rope(q[..., MLA_NOPE:], pos)], axis=-1)
        kv = (rms_norm_2(c_kv, mla_kv_norm[i]) @ mla_w_ukv[i]).reshape(B, S, MLA_HEADS, MLA_NOPE + MLA_V)
        kr = apply_rope(k_rope[:, :, None, :], pos)
        mla_k = jnp.concatenate([kv[..., :MLA_NOPE],
                                 jnp.broadcast_to(kr, (B, S, MLA_HEADS, MLA_ROPE))], axis=-1)
        mla_v = kv[..., MLA_NOPE:]

        dsa_q = dq.reshape(B, S, DSA_HEADS, DSA_DIM)
        idx_q = iq.reshape(B, S, IDX_HEADS, IDX_DIM)
        idx_w = iw * IDX_HEADS ** -0.5

        sb_q = sq.reshape(B, S, SB_HEADS, SB_DIM)
        sb_k = sk.reshape(B, S, SB_HEADS, SB_DIM)
        sb_v = sv.reshape(B, S, SB_HEADS, SB_DIM)

        blocks = lax.map(lambda q0: mixer_block(q0, pos, q, mla_k, mla_v, dsa_q, dk, dv,
                                                idx_q, ik, idx_w, sb_q, sb_k, sb_v,
                                                rel_bias, topk), starts)
        mix = jnp.transpose(blocks, (1, 0, 2, 3)).reshape(B, S, MIX_WIDTH)
        h = h + mix @ w_o[i]

        hf = rms_norm_2(h, ffn_norm[i])
        h = h + (jax.nn.silu(hf @ w_gate[i]) * (hf @ w_up[i])) @ w_down[i]

        g = jax.nn.sigmoid(rms_norm_2(h, ple_norm[i]) @ w_ple_gate[i])
        h = h + g * (p[i] @ w_ple_proj[i])
    return rms_norm_2(h, final_norm)


def setup_inputs(seed=0):
    out = dict(first_inputs(seed))
    for name, value in second_inputs(seed + 1).items():
        if name != "x":
            out[name + "_2"] = value
    return out


def reference(
    x, c, ctx, c_ctx, w_mod, b_mod, norm1_g, norm2_g, final_g, conv_w_pw1, conv_b_pw1,
    conv_w_dw, conv_b_dw, conv_ln_g, conv_ln_b, conv_w_pw2, conv_b_pw2, dn_w_in, dn_conv_w,
    dn_a_log, dn_dt_bias, dn_norm_g, dn_w_o, mlp_w1, mlp_w2, p_2, w_in_2, attn_norm_2,
    mla_q_norm_2, mla_w_uq_2, mla_kv_norm_2, mla_w_ukv_2, rel_bias_2, w_o_2, ffn_norm_2,
    w_gate_2, w_up_2, w_down_2, ple_norm_2, w_ple_gate_2, w_ple_proj_2, final_norm_2,
):
    x = first_block(
        x, c, ctx, c_ctx, w_mod, b_mod, norm1_g, norm2_g, final_g, conv_w_pw1, conv_b_pw1,
        conv_w_dw, conv_b_dw, conv_ln_g, conv_ln_b, conv_w_pw2, conv_b_pw2, dn_w_in, dn_conv_w,
        dn_a_log, dn_dt_bias, dn_norm_g, dn_w_o, mlp_w1, mlp_w2,
    )
    return second_block(
        x, p_2, w_in_2, attn_norm_2, mla_q_norm_2, mla_w_uq_2, mla_kv_norm_2, mla_w_ukv_2,
        rel_bias_2, w_o_2, ffn_norm_2, w_gate_2, w_up_2, w_down_2, ple_norm_2, w_ple_gate_2,
        w_ple_proj_2, final_norm_2,
    )


_drawn_inputs = setup_inputs


def setup_inputs(seed=0):
    import zlib

    import numpy as np

    out = dict(_drawn_inputs(seed))
    spreads = {}
    factors = {'norm1_g': 5.307,
     'norm2_g': 3.363,
     'conv_b_pw1': 5.529,
     'conv_b_dw': 3.539,
     'conv_ln_g': 4.745,
     'conv_ln_b': 5.328,
     'conv_b_pw2': 4.036,
     'mla_q_norm_2': 7.229,
     'mla_kv_norm_2': 3.897,
     'ple_norm_2': 4.545}
    for name, (base, spread) in spreads.items():
        noise = np.random.default_rng([zlib.crc32(name.encode()), seed]).standard_normal(out[name].shape)
        drawn = base * np.exp(spread * noise) if base else spread * noise
        out[name] = __import__('jax').numpy.asarray(drawn.astype(out[name].dtype))
    for name, factor in factors.items():
        out[name] = (out[name] * factor).astype(out[name].dtype)
    return out
```

```python
from contextlib import ExitStack

import numpy as np

import concourse.bass as bass
from concourse import mybir

F32 = mybir.dt.float32
F32R = mybir.dt.float32r
BF16 = mybir.dt.bfloat16
ALU = mybir.AluOpType
ACT = mybir.ActivationFunctionType
AX = mybir.AxisListType

P = 128
D = 1024
KT = D // P
SEQ = 256
NB = SEQ // P
EPS = 1e-6
LAYERS = 2

SEG = 64
SEGS = SEQ // SEG
TAPS = 31
HALO = TAPS // 2
PADDED = SEG + 2 * HALO
FFN1 = 4 * D
MLP_CHUNK = 512
MLP_CHUNKS = FFN1 // MLP_CHUNK

HM, NOPE, ROPE, VD = 6, 64, 32, 64
HALF = ROPE // 2
QK = NOPE + ROPE
QL, KVL = 384, 256
HD = 5
HI = 8
HS = 5
DH = 64
TOPK = 64
BUCKETS, MAX_DIST = 32, 128
DFF = 2816
FF_CHUNK = 256
FF_CHUNKS = DFF // FF_CHUNK
PLE = 256

SLOT = 2048
RAW_SLOTS = 4
SPLIT_SLOTS = 3
LOOKAHEAD = SPLIT_SLOTS - 1
NEG = -1.0e30
TAKEN = -3.0e38

IDX_COLS = HI * DH + DH + HI
MLA_COLS = QL + KVL + ROPE
DSA_COLS = (HD + 2) * DH
SB_COLS = 2 * HS * DH
SV_COLS = HS * DH
UQ_COLS = HM * QK
UKV_COLS = HM * (NOPE + VD)

ORDER5 = [0, 2, 1, 3, 4]
ORDER8 = [0, 2, 1, 3, 4, 6, 5, 7]
ORDER8_B0 = [0, 2, 4, 6, 1, 3, 5, 7]


def plan_units():
    units = []

    def add(stage, n, kts, cols, split=True):
        k0 = 0
        for i, k in enumerate(kts):
            units.append(dict(stage=stage, n=n, part=i, k0=k0, kts=k, cols=cols, split=split))
            k0 += k

    for v in range(2):
        for q in range(4):
            add(("mod", v), q, [KT], 256, split=False)
    for f in range(KT):
        add("pw1", f, [KT], 256)
    for v in range(2, 6):
        for q in range(4):
            add(("mod", v), q, [KT], 256, split=False)
    add("pw2", 0, [2] * 4, D)
    for j in range(MLP_CHUNKS + 1):
        if j < MLP_CHUNKS:
            add("w1", j, [4, 4], MLP_CHUNK)
        if j:
            add("w2", j - 1, [2, 2], D)
    for layer in range(LAYERS):
        add(("idx", layer), 0, [3, 3, 2], IDX_COLS)
        add(("mla", layer), 0, [3, 3, 2], MLA_COLS)
        add(("dsa", layer), 0, [4, 4], DSA_COLS)
        add(("uq", layer), 0, [QL // P], UQ_COLS)
        add(("ukv", layer), 0, [KVL // P], UKV_COLS)
        add(("sb", layer), 0, [3, 3, 2], SB_COLS)
        add(("sv", layer), 0, [4, 4], SV_COLS)
        add(("wo", layer), 0, [2] * 4, D)
        for j in range(FF_CHUNKS + 1):
            if j < FF_CHUNKS:
                add(("gu", layer), j, [4, 4], 2 * FF_CHUNK)
            if j:
                add(("dn", layer), j - 1, [2], D)
        add(("proj", layer), 0, [PLE // P], D)
        add(("gate", layer), 0, [2] * 4, D)
    at, split, landed = 0, 0, [0] * RAW_SLOTS
    for i, u in enumerate(units):
        u["index"] = i
        u["offset"] = at
        at += P * u["kts"] * u["cols"]
        u["slot"] = i % RAW_SLOTS
        landed[u["slot"]] += 16
        u["landed"] = landed[u["slot"]]
        if u["split"]:
            u["s"] = split
            split += 1
    return units, at


UNITS, STREAM = plan_units()
SPLIT = [u for u in UNITS if u["split"]]


def units_of(stage, n=0):
    return [u for u in UNITS if u["stage"] == stage and u["n"] == n]


def last_of(stage, n=0):
    return units_of(stage, n)[-1]


C_ID, C_TRI, C_CAUSAL, C_STRICT, C_COS, C_SIN, C_HOT = 0, 128, 256, 384, 512, 544, 576
HOT = 3 * P
C_END = C_HOT + HOT

V_C, V_BPW1, V_BDW, V_LNG, V_LNB, V_DW = 0, 8, 24, 32, 40, 48
V_END = V_DW + KT * TAPS


def build(nc, stream, x, p_t, vectors, rows, rel, consts, out):
    ctx = ExitStack()
    with ctx:
        def sb(name, shape, dt=F32):
            return ctx.enter_context(nc.sbuf_tensor(name, shape, dt))

        def sem(name):
            return ctx.enter_context(nc.semaphore(name))

        raw = sb("raw", [P, RAW_SLOTS, SLOT])
        hi = sb("hi", [P, SPLIT_SLOTS, SLOT], F32R)
        lo = sb("lo", [P, SPLIT_SLOTS, SLOT], F32R)
        xh = sb("xh", [P, KT, SEQ], F32R)
        xl = sb("xl", [P, KT, SEQ], F32R)
        gh = sb("gh", [P, 5, SEQ], F32R)
        gl = sb("gl", [P, 5, SEQ], F32R)
        h = sb("h", [P, NB, D])
        xs = sb("xs", [P, NB, D])
        gain = sb("gain", [P, 2, D])
        lora_gain = sb("lora_gain", [P, QL + KVL])
        ident = sb("ident", [P, P])
        tri = sb("tri", [P, P])
        neg_ones = sb("neg_ones", [P, P])
        cmask = sb("cmask", [P, 2, P])
        strict = sb("strict", [P, P])
        cosines = sb("cosines", [P, NB, HALF])
        sines = sb("sines", [P, NB, HALF])
        ident16 = sb("ident16", [P, P], BF16)
        masks16 = sb("masks16", [P, 2, P], BF16)
        bias = sb("bias", [P, HD, 2 * P])
        ss = sb("ss", [P, 4])
        var = sb("var", [P, 4])
        rstd = sb("rstd", [P, 4])
        pow_half = sb("pow_half", [P, 4])
        lss = sb("lss", [P, NB, 2])
        lvar = sb("lvar", [P, NB, 2])
        lrstd = sb("lrstd", [P, NB, 2])
        top8 = sb("top8", [P, 8])
        neg_max = sb("neg_max", [P, 12])
        row_max = sb("row_max", [P, 12])
        row_sum = sb("row_sum", [P, 12])
        row_inv = sb("row_inv", [P, 12])
        iw = sb("iw", [P, NB, HI])
        scratch = sb("scratch", [P, 16512])

        ps = ctx.enter_context(nc.psum_tensor("ps", [P, 8, 512], F32))

        def carve(table, start=0):
            views, at = {}, start
            for name, size in table:
                views[name] = scratch[:, at:at + size]
                at += size
            assert at <= 16512, at
            return views

        one = carve([("upad", KT * SEGS * PADDED), ("sig", 2 * SEQ), ("cv", KT * SEQ), ("mu", SEQ),
                     ("rs", SEQ), ("sq", KT * SEQ), ("csb", KT * P), ("rowA", D), ("rowB", D),
                     ("g1", D), ("g2", D), ("bpw2", D), ("vec", V_END), ("ones", P), ("vr", SEQ), ("pw", SEQ)])
        upad = one["upad"].rearrange("p (f s t) -> p f s t", f=KT, s=SEGS)
        sig = one["sig"].rearrange("p (b t) -> p b t", b=2)
        cv = one["cv"].rearrange("p (f t) -> p f t", f=KT)
        sq = one["sq"].rearrange("p (f t) -> p f t", f=KT)
        csb = one["csb"].rearrange("p (k m) -> p k m", k=KT)
        vec = one["vec"]
        dw = vec[:, V_DW:V_END].rearrange("p (f k) -> p f k", f=KT)
        hid1 = one["sq"][:, 0:NB * MLP_CHUNK].rearrange("p (b c) -> p b c", b=NB)
        rbb = one["upad"][0:BUCKETS + 1, 0:HD * P].rearrange("p (h m) -> p h m", h=HD)
        rb = one["cv"][0:BUCKETS + 1, 0:HD]
        hot = one["cv"][0:BUCKETS + 1, 512:512 + HOT]
        toep = one["sq"][:, 0:HD * 3 * P].rearrange("p (h d) -> p h d", h=HD)
        craw = one["cv"][:, 1024:1024 + C_HOT]

        two = carve([("Z", 3072), ("X", 2304), ("Y", 2304), ("iqT", 4 * SEQ), ("ikT", SEQ), ("work", 3 * P),
                     ("dT", 3 * SEQ), ("dkT", SEQ), ("dv", NB * DH), ("sT", 6 * SEQ), ("sv", NB * SV_COLS),
                     ("mv", NB * HM * VD), ("qT", HM * SEQ), ("kT", HM * SEQ)])
        relu1 = two["Z"][:, 0:2048].rearrange("p (h k) -> p h k", h=HI)
        relu0 = two["Z"][:, 2048:3072].rearrange("p (h k) -> p h k", h=HI)
        kfull = two["Z"][:, 0:NB * HM * QK].rearrange("p (b h d) -> p b h d", b=NB, h=HM)
        sbt = two["Z"][:, 1152:1152 + HS * 384].rearrange("p (h k) -> p h k", h=HS)
        cn = two["X"][:, 0:NB * (QL + KVL)].rearrange("p (b c) -> p b c", b=NB)
        q7 = two["Y"][:, 0:NB * 7 * QK].rearrange("p (b h d) -> p b h d", b=NB, h=7)
        rt = two["Y"][:, 1344:1344 + 4 * 224].rearrange("p (i b h d) -> p i b h d", i=4, b=NB, h=7)
        ikd = two["Y"][:, 2048:2304].rearrange("p (b d) -> p b d", b=NB)
        pm = [two["X"][:, 1536:2304].rearrange("p (h k) -> p h k", h=HM),
              two["X"][:, 0:1536].rearrange("p (h k) -> p h k", h=HM)]
        pmT = [two["Y"][:, 1536:2304], two["Y"][:, 0:1536]]
        pd = [two["X"][:, 1280:1920].rearrange("p (h k) -> p h k", h=HD),
              two["X"][:, 0:1280].rearrange("p (h k) -> p h k", h=HD)]
        pdT = [two["Y"][:, 1280:1920], two["Y"][:, 0:1280]]
        iqT = two["iqT"].rearrange("p (t q) -> p t q", t=4)
        ikT = two["ikT"]
        work = [two["work"][:, 0:P], two["work"][:, P:3 * P]]
        dT = two["dT"].rearrange("p (t q) -> p t q", t=3)
        dkT = two["dkT"]
        dv = two["dv"].rearrange("p (b d) -> p b d", b=NB)
        sT = two["sT"].rearrange("p (t q) -> p t q", t=6)
        sv = two["sv"].rearrange("p (b c) -> p b c", b=NB)
        mv = two["mv"].rearrange("p (b h d) -> p b h d", b=NB, h=HM)
        qT = two["qT"].rearrange("p (h q) -> p h q", h=HM)
        kT = two["kT"].rearrange("p (h q) -> p h q", h=HM)

        three = carve([("pp", NB * D), ("sg", NB * D), ("hid", NB * FF_CHUNK), ("silu", NB * FF_CHUNK), ("pT", 2 * SEQ)])
        pp = three["pp"].rearrange("p (b c) -> p b c", b=NB)
        sg = three["sg"].rearrange("p (b c) -> p b c", b=NB)
        hid2 = three["hid"].rearrange("p (b c) -> p b c", b=NB)
        silu2 = three["silu"].rearrange("p (b c) -> p b c", b=NB)
        pT = three["pT"].rearrange("p (t q) -> p t q", t=2)

        skew = nc.dram_tensor("skew", (HD, P * 3 * P), F32, kind="Internal").ap()

        landed = [sem(f"landed{i}") for i in range(RAW_SLOTS)]
        names = """used hi_done lo_done in_consts in_vec in_x in_rows in_rel in_gain in_lora in_p in_skew out_skew
        init_v init_p silu_c csb_done relb_ps toep_done relb_done
        row_b mod_evac mod_mid
        sumsq var_done rstd_done h_ready xs_mid xs_ready xT_ps xh_ready xl_ready
        sig_done glu_done conv_step mean_ps mean_done cent_done sq_done var_ps lnvar lnvar2 lnrs ln_done silu_done yh_done yl_done
        pw2_ps res_step xprep
        w1_ps relu_done hid_done hidT_ps gh_done gl_done mlp_ps
        iqT_done ikd_done iw_done ikT_ps ikT_done isc_ps relu_i isc_step topk_step sel_done
        lora_sq lora_var lora_rstd cn_done kr_done cnT_ps
        dsa_evac q7_done kv_done sb_evac sv_evac
        rope_t rope_done kf_done qkT_ps qT_done kT_done
        m_sc m_max m_nm m_exp m_inv m_pT_ps m_pT m_o mix_m
        s_z s_abs s_e s_ln s_sp s_zs s_w s_o mix_s
        d_sc d_b d_s d_nm d_exp d_inv d_pT_ps d_pT d_o mix_d
        wo_ps gu_ps silu_g hid_g dn_ps ph_done pl_done proj_evac gate_ps sig_g gmul outs""".split()
        S = {n: sem(n) for n in names}

        block = ctx.enter_context(nc.Block())

        def product(eng, stage, n=0):
            eng.wait_ge(S["used"], last_of(stage, n)["index"] + 1)

        def block_product(eng, first, value, b, stage, n=0):
            if b == 0:
                eng.wait_ge(S[first], value)
            else:
                product(eng, stage, n)

        NORMS = 3 + 3 * LAYERS + 1
        LAST = NORMS - 1

        def nval(n, b):
            return 2 * n + b + 1

        def hval(n, b):
            return 2 * (n - 1) + b + 1

        def xsval(n, b):
            return 2 * (n if n < 2 else n - 1) + b + 1

        def tval(t, b):
            return 2 * t + b + 1

        def norm_of(t):
            return t if t < 2 else 3 + 3 * ((t - 2) // 4) + (0, None, 1, 2)[(t - 2) % 4]

        def before_T(t):
            if t == 0:
                return None
            if t == 1:
                return last_of("pw2")
            layer, k = (t - 2) // 4, (t - 2) % 4
            if k == 0:
                return last_of("w1", MLP_CHUNKS - 1) if layer == 0 else last_of(("gate", layer - 1))
            return (None, last_of(("sv", layer)), last_of(("wo", layer)), last_of(("gu", layer), FF_CHUNKS - 1))[k]

        GAIN_ROWS = ["norm1_g", "norm2_g", "final_g"] + [f"{k}{l}" for l in range(LAYERS) for k in ("attn", "ffn", "ple")] + ["final"]

        @block.sync
        def _(sp):
            def weights(units):
                for u in units:
                    if u["index"] >= RAW_SLOTS:
                        old = UNITS[u["index"] - RAW_SLOTS]
                        if old["split"]:
                            sp.wait_ge(S["lo_done"], old["s"] + 1)
                        else:
                            sp.wait_ge(S["used"], old["index"] + 1)
                    n = u["kts"] * u["cols"]
                    src = stream[u["offset"]:u["offset"] + P * n].rearrange("(p n) -> p n", p=P)
                    sp.dma_start(raw[:, u["slot"], 0:n], src).then_inc(landed[u["slot"]], 16)

            def row(dst, name, s, base=None):
                sp.dma_start(dst, rows[name].partition_broadcast(P)).then_inc(S[s], 16)

            def gain_row(n):
                if n >= 2:
                    sp.wait_ge(S["xs_ready"] if n - 2 != 2 else S["h_ready"],
                               xsval(n - 2, 1) if n - 2 != 2 else hval(3, 1))
                row(gain[:, n % 2, :], GAIN_ROWS[n], "in_gain")

            def lora_row(layer):
                if layer:
                    sp.wait_ge(S["cn_done"], 4 * layer)
                row(lora_gain[:], f"lora{layer}", "in_lora")

            sp.dma_start(vec, vectors).then_inc(S["in_vec"], 16)
            sp.dma_start(h[:], x.rearrange("(b p) d -> p b d", p=P)).then_inc(S["in_x"], 16)
            weights(UNITS[0:2])
            row(one["rowB"], "b_mod1", "in_rows")
            row(one["rowA"], "b_mod0", "in_rows")
            gain_row(0)
            sp.dma_start(craw, consts[:, 0:C_HOT]).then_inc(S["in_consts"], 16)
            sp.dma_start(hot, consts[0:BUCKETS + 1, C_HOT:C_HOT + HOT]).then_inc(S["in_rel"], 16)
            sp.dma_start(rb, rel).then_inc(S["in_rel"], 16)
            first = units_of("pw1", 0)[0]["index"]
            weights(UNITS[2:first])
            sp.wait_ge(S["toep_done"], 1)
            sp.dma_start(skew.rearrange("h (p d) -> p h d", p=P), toep).then_inc(S["out_skew"], 16)
            sp.wait_ge(S["out_skew"], 16)
            for slot, head in enumerate(ORDER5):
                src = skew[head, P - 1:P - 1 + P * (3 * P - 1)].rearrange("(p d) -> p d", p=P)[:, 0:2 * P]
                sp.dma_start(bias[:, slot, :], src).then_inc(S["in_skew"], 16)
            at = units_of(("mod", 2), 0)[0]["index"]
            weights(UNITS[first:at])
            gain_row(1)
            row(one["g1"], "b_mod2", "in_rows")
            row(one["g2"], "b_mod5", "in_rows")
            row(one["bpw2"], "b_pw2", "in_rows")
            sp.wait_ge(S["xs_ready"], xsval(0, 1))
            row(one["rowB"], "b_mod4", "in_rows")
            row(one["rowA"], "b_mod3", "in_rows")
            end = units_of("w1", 1)[0]["index"]
            weights(UNITS[at:end])
            gain_row(2)
            at, end = end, units_of(("idx", 0))[0]["index"]
            weights(UNITS[at:end])
            for layer in range(LAYERS):
                n = 3 + 3 * layer
                gain_row(n)
                lora_row(layer)
                at, end = end, units_of(("wo", layer))[0]["index"]
                weights(UNITS[at:end])
                gain_row(n + 1)
                at, end = end, units_of(("gu", layer), 2)[0]["index"]
                weights(UNITS[at:end])
                gain_row(n + 2)
                sp.wait_ge(S["mix_d"], 2 * layer + 2)
                sp.dma_start(pT, p_t[layer].rearrange("(t p) q -> p t q", p=P)).then_inc(S["in_p"], 16)
                at = end
                end = units_of(("idx", layer + 1))[0]["index"] if layer + 1 < LAYERS else len(UNITS)
                weights(UNITS[at:end])
            gain_row(LAST)
            for b in range(NB):
                sp.wait_ge(S["xs_ready"], xsval(LAST, b))
                sp.dma_start(out[b * P:(b + 1) * P, :], xs[:, b, :]).then_inc(S["outs"], 16)
            sp.wait_ge(S["outs"], 32)

        @block.scalar
        def _(act):
            fed = [0]

            def feed(unit, ahead=LOOKAHEAD):
                while fed[0] < min(unit["s"] + 1 + ahead, len(SPLIT)):
                    u = SPLIT[fed[0]]
                    act.wait_ge(landed[u["slot"]], u["landed"])
                    if u["s"] >= SPLIT_SLOTS:
                        act.wait_ge(S["used"], SPLIT[u["s"] - SPLIT_SLOTS]["index"] + 1)
                    n = u["kts"] * u["cols"]
                    nc.scalar.activation(hi[:, u["s"] % SPLIT_SLOTS, 0:n], raw[:, u["slot"], 0:n],
                                         ACT.Copy).then_inc(S["hi_done"], 1)
                    fed[0] += 1

            def squares(n):
                for b in range(NB):
                    if n:
                        act.wait_ge(S["h_ready"], hval(n, b))
                    else:
                        act.wait_ge(S["in_x"], 16)
                        act.wait_ge(S["init_p"], 3)
                    k = 2 * (n % 2) + b
                    nc.scalar.activation(xs[:, b, :], h[:, b, :], ACT.Square,
                                         accum_out=ss[:, k:k + 1]).then_inc(S["sumsq"], 1)

            def high_T(t):
                if before_T(t):
                    act.wait_ge(S["used"], before_T(t)["index"] + 1)
                for b in range(NB):
                    bank = 4 + 2 * b
                    act.wait_ge(S["xT_ps"], tval(t, b))
                    nc.scalar.activation(xh[:, :, b * P:(b + 1) * P],
                                         ps[:, bank:bank + 2, :].rearrange("p a (k m) -> p (a k) m", k=4),
                                         ACT.Copy).then_inc(S["xh_ready"], 1)

            act.wait_ge(S["in_vec"], 16)
            nc.scalar.activation(vec[:, V_C:V_C + KT], vec[:, V_C:V_C + KT], ACT.Silu).then_inc(S["silu_c"], 1)
            squares(0)
            act.wait_ge(S["relb_ps"], 1)
            nc.scalar.activation(toep, ps[:, 3:8, 0:3 * P], ACT.Copy).then_inc(S["toep_done"], 1)
            feed(units_of("pw1", 0)[0])
            high_T(0)
            for f in range(KT):
                feed(units_of("pw1", f)[0], min(LOOKAHEAD, KT - 1 - f))
                product(act, "pw1", f)
                if f >= 2:
                    act.wait_ge(S["glu_done"], f - 1)
                nc.scalar.activation(sig[:, f % 2, :], ps[:, 4 + f % 2, SEQ:2 * SEQ], ACT.Sigmoid,
                                     bias=vec[:, V_BPW1 + KT + f:V_BPW1 + KT + f + 1]).then_inc(S["sig_done"], 1)
            feed(units_of("pw2")[0])
            act.wait_ge(S["mean_ps"], 1)
            nc.scalar.activation(one["mu"], ps[:, 6, 0:SEQ], ACT.Copy, scale=1.0 / D).then_inc(S["mean_done"], 1)
            act.wait_ge(S["cent_done"], 1)
            nc.scalar.activation(sq, cv, ACT.Square).then_inc(S["sq_done"], 1)
            act.wait_ge(S["var_ps"], 1)
            nc.scalar.activation(one["vr"], ps[:, 7, 0:SEQ], ACT.Copy, scale=1.0 / D).then_inc(S["lnvar"], 1)
            act.wait_ge(S["ln_done"], 1)
            for f in range(KT):
                nc.scalar.activation(sq[:, f, :], cv[:, f, :], ACT.Silu, scale=vec[:, V_LNG + f:V_LNG + f + 1],
                                     bias=vec[:, V_LNB + f:V_LNB + f + 1]).then_inc(S["silu_done"], 1)
            act.wait_ge(S["used"], last_of("pw1", KT - 1)["index"] + 1)
            act.wait_ge(S["silu_done"], KT)
            nc.scalar.activation(xh[:], sq, ACT.Copy).then_inc(S["yh_done"], 1)
            feed(last_of("pw2"))
            squares(1)
            feed(units_of("w1", 0)[0])
            high_T(1)
            for j in range(MLP_CHUNKS):
                feed(last_of("w1", j))
                for b in range(NB):
                    block_product(act, "w1_ps", j + 1, b, "w1", j)
                    if j:
                        act.wait_ge(S["hidT_ps"], 2 * (j - 1) + b + 1)
                    nc.scalar.activation(hid1[:, b, :], ps[:, 4 + b, :], ACT.Relu).then_inc(S["relu_done"], 1)
                    act.wait_ge(S["relu_done"], 2 * j + b + 1)
                    nc.scalar.activation(hid1[:, b, :], hid1[:, b, :], ACT.Square).then_inc(S["hid_done"], 1)
                if j:
                    feed(last_of("w2", j - 1))
                    act.wait_ge(S["used"], last_of("w2", j - 1)["index"] + 1)
                for b in range(NB):
                    act.wait_ge(S["hidT_ps"], 2 * j + b + 1)
                    nc.scalar.activation(gh[:, 0:4, b * P:(b + 1) * P], ps[:, 6 + b, :].rearrange("p (k m) -> p k m", k=4),
                                         ACT.Copy).then_inc(S["gh_done"], 1)
            feed(last_of("w2", MLP_CHUNKS - 1))
            squares(2)

            ghv = 2 * MLP_CHUNKS
            for layer in range(LAYERS):
                n, t = 3 + 3 * layer, 2 + 4 * layer
                squares(n)
                feed(units_of(("idx", layer))[0])
                high_T(t)
                feed(last_of(("idx", layer)))
                product(act, ("idx", layer))
                nc.scalar.activation(iqT, ps[:, 4:6, :].rearrange("p a (t q) -> p (a t) q", t=2),
                                     ACT.Copy).then_inc(S["iqT_done"], 1)
                feed(last_of(("mla", layer)))
                product(act, ("mla", layer))
                for b in range(NB):
                    nc.scalar.activation(cn[:, b, 0:QL], ps[:, 2 * b, 0:QL], ACT.Square,
                                         accum_out=lss[:, b, 0:1]).then_inc(S["lora_sq"], 1)
                    nc.scalar.activation(cn[:, b, QL:QL + KVL], ps[:, 2 * b + 1, 0:KVL], ACT.Square,
                                         accum_out=lss[:, b, 1:2]).then_inc(S["lora_sq"], 1)
                for b in range(NB):
                    nc.scalar.activation(q7[:, b, HM, NOPE:QK], ps[:, 2 * b + 1, KVL:KVL + ROPE],
                                         ACT.Copy).then_inc(S["kr_done"], 1)
                act.wait_ge(S["ikT_ps"], layer + 1)
                nc.scalar.activation(ikT, ps[:, 6, 0:SEQ], ACT.Copy).then_inc(S["ikT_done"], 1)
                act.wait_ge(S["isc_ps"], 2 * layer + 1)
                nc.scalar.activation(relu1, ps[:, 4:8, :].rearrange("p a (t q) -> p (a t) q", t=2), ACT.Relu,
                                     scale=DH ** -0.5).then_inc(S["relu_i"], 1)
                act.wait_ge(S["cnT_ps"], layer + 1)
                last_g = last_of("w2", MLP_CHUNKS - 1) if layer == 0 else last_of(("proj", layer - 1))
                act.wait_ge(S["used"], last_g["index"] + 1)
                nc.scalar.activation(gh[:].rearrange("p k m -> p (k m)"), ps[:, 0:3, :].rearrange("p a c -> p (a c)")[:, 0:5 * SEQ],
                                     ACT.Copy).then_inc(S["gh_done"], 1)
                ghv += 1
                act.wait_ge(S["isc_ps"], 2 * layer + 2)
                nc.scalar.activation(relu0, ps[:, 4:6, :].rearrange("p a (t q) -> p (a t) q", t=4), ACT.Relu,
                                     scale=DH ** -0.5).then_inc(S["relu_i"], 1)
                feed(last_of(("dsa", layer)))
                product(act, ("dsa", layer))
                nc.scalar.activation(dT[:, 0:2, :], ps[:, 6, :].rearrange("p (t q) -> p t q", t=2),
                                     ACT.Copy).then_inc(S["dsa_evac"], 1)
                nc.scalar.activation(dT[0:DH, 2, :], ps[0:DH, 7, 0:SEQ], ACT.Copy).then_inc(S["dsa_evac"], 1)
                nc.scalar.activation(dkT[DH:P, :], ps[DH:P, 7, 0:SEQ], ACT.Copy).then_inc(S["dsa_evac"], 1)
                nc.scalar.activation(dkT[0:DH, :], ps[DH:P, 7, 0:SEQ], ACT.Copy).then_inc(S["dsa_evac"], 1)
                nc.scalar.activation(dv, ps[:, 7, SEQ:SEQ + 2 * DH].rearrange("p (b d) -> p b d", b=NB),
                                     ACT.Copy).then_inc(S["dsa_evac"], 1)
                feed(last_of(("uq", layer)))
                product(act, ("uq", layer))
                for b in range(NB):
                    nc.scalar.activation(q7[:, b, 0:HM, :].rearrange("p h d -> p (h d)").rearrange("p (a c) -> p a c", a=2),
                                         ps[:, 2 * b:2 * b + 2, 0:UQ_COLS // 2], ACT.Copy).then_inc(S["q7_done"], 1)
                feed(last_of(("sb", layer)))
                act.wait_ge(S["rope_done"], 2 * layer + 2)
                act.wait_ge(S["kv_done"], 4 * layer + 4)
                for b in range(NB):
                    nc.scalar.activation(kfull[:, b, :, NOPE:QK], q7[:, b, HM:HM + 1, NOPE:QK].broadcast_to([P, HM, ROPE]),
                                         ACT.Copy).then_inc(S["kf_done"], 1)
                product(act, ("sb", layer))
                nc.scalar.activation(sT[:, 0:2, :], ps[:, 0, :].rearrange("p (t q) -> p t q", t=2), ACT.Copy,
                                     scale=DH ** -0.5).then_inc(S["sb_evac"], 1)
                nc.scalar.activation(sT[:, 2:4, :], ps[:, 1, :].rearrange("p (t q) -> p t q", t=2),
                                     ACT.Copy).then_inc(S["sb_evac"], 1)
                nc.scalar.activation(sT[0:DH, 4, :], ps[0:DH, 2, 0:SEQ], ACT.Copy, scale=DH ** -0.5).then_inc(S["sb_evac"], 1)
                nc.scalar.activation(sT[0:DH, 5, :], ps[DH:P, 2, 0:SEQ], ACT.Copy).then_inc(S["sb_evac"], 1)
                feed(last_of(("sv", layer)))
                act.wait_ge(S["qkT_ps"], 2 * layer + 1)
                nc.scalar.activation(qT[0:QK].rearrange("p h q -> p (h q)"), ps[0:QK, 5:8, :].rearrange("p a c -> p (a c)"),
                                     ACT.Copy).then_inc(S["qT_done"], 1)
                for i, b in enumerate((1, 0)):
                    act.wait_ge(S["m_nm"], 2 * layer + i + 1)
                    for hh in range(HM):
                        src = (ps[:, 5:8, :].rearrange("p a (t k) -> p (a t) k", t=2)[:, hh, :] if b else
                               ps[:, 3:5, :].rearrange("p a (t k) -> p (a t) k", t=4)[:, hh, :])
                        k = HM * b + hh
                        nc.scalar.activation(pm[b][:, hh, :], src, ACT.Exp, scale=QK ** -0.5, bias=neg_max[:, k:k + 1],
                                             accum_out=row_sum[:, k:k + 1]).then_inc(S["m_exp"], 1)
                act.wait_ge(S["m_pT_ps"], 2 * layer + 1)
                nc.scalar.activation(pmT[1], ps[:, 5:8, :].rearrange("p a c -> p (a c)"), ACT.Copy).then_inc(S["m_pT"], 1)
                act.wait_ge(S["s_z"], layer + 1)
                zps = ps[:, 0:5, 0:3 * P]
                act.wait_ge(S["qkT_ps"], 2 * layer + 2)
                nc.scalar.activation(sbt, zps, ACT.Abs).then_inc(S["s_abs"], 1)
                act.wait_ge(S["s_abs"], layer + 1)
                nc.scalar.activation(sbt, sbt, ACT.Exp, scale=-1.0).then_inc(S["s_e"], 1)
                act.wait_ge(S["s_e"], layer + 1)
                nc.scalar.activation(sbt, sbt, ACT.Ln, bias=1.0).then_inc(S["s_ln"], 1)
                act.wait_ge(S["s_zs"], layer + 1)
                nc.scalar.activation(sbt, zps, ACT.Exp).then_inc(S["s_w"], 1)
                feed(last_of(("wo", layer)), ahead=-1)
                for i, b in enumerate((1, 0)):
                    act.wait_ge(S["d_nm"], 2 * layer + i + 1)
                    for k in range(HD):
                        c, head = HD * b + k, HD * b + ORDER5[k]
                        nc.scalar.activation(pd[b][:, k, :], pd[b][:, k, :], ACT.Exp, bias=neg_max[:, c:c + 1],
                                             accum_out=row_sum[:, head:head + 1]).then_inc(S["d_exp"], 1)
                act.wait_ge(S["d_pT_ps"], 2 * layer + 1)
                nc.scalar.activation(pdT[1], ps[:, 0:3, :].rearrange("p a c -> p (a c)")[:, 0:2 * HD * P],
                                     ACT.Copy).then_inc(S["d_pT"], 1)
                high_T(t + 1)
                feed(last_of(("wo", layer)))
                squares(n + 1)
                high_T(t + 2)
                for j in range(FF_CHUNKS):
                    feed(last_of(("gu", layer), j))
                    for b in range(NB):
                        k = FF_CHUNKS * layer + j
                        block_product(act, "gu_ps", k + 1, b, ("gu", layer), j)
                        if k:
                            act.wait_ge(S["hid_g"], 2 * (k - 1) + b + 1)
                        nc.scalar.activation(silu2[:, b, :], ps[:, 4 + b, 0:FF_CHUNK], ACT.Silu).then_inc(S["silu_g"], 1)
                    if j:
                        feed(last_of(("dn", layer), j - 1))
                        act.wait_ge(S["used"], last_of(("dn", layer), j - 1)["index"] + 1)
                    else:
                        act.wait_ge(S["used"], last_of(("ukv", layer))["index"] + 1)
                    for b in range(NB):
                        act.wait_ge(S["hidT_ps"], 2 * (MLP_CHUNKS + FF_CHUNKS * layer + j) + b + 1)
                        nc.scalar.activation(gh[:, 0:2, b * P:(b + 1) * P],
                                             ps[:, 6 + b, 0:2 * P].rearrange("p (k m) -> p k m", k=2),
                                             ACT.Copy).then_inc(S["gh_done"], 1)
                feed(last_of(("dn", layer), FF_CHUNKS - 1))
                act.wait_ge(S["in_p"], 16 * (layer + 1))
                act.wait_ge(S["used"], last_of(("dn", layer), FF_CHUNKS - 1)["index"] + 1)
                nc.scalar.activation(gh[:, 0:2, :], pT, ACT.Copy).then_inc(S["ph_done"], 1)
                squares(n + 2)
                product(act, ("proj", layer))
                for b in range(NB):
                    nc.scalar.activation(pp[:, b, :], ps[:, 2 * b:2 * b + 2, :].rearrange("p a c -> p (a c)"),
                                         ACT.Copy).then_inc(S["proj_evac"], 1)
                high_T(t + 3)
                feed(last_of(("gate", layer)))
                for b in range(NB):
                    block_product(act, "gate_ps", layer + 1, b, ("gate", layer))
                    nc.scalar.activation(sg[:, b, :], ps[:, 2 * b:2 * b + 2, :].rearrange("p a c -> p (a c)"),
                                         ACT.Sigmoid).then_inc(S["sig_g"], 1)
            squares(LAST)

        @block.gpsimd
        def _(pool):
            nc.gpsimd.memset(pow_half[:], -0.5).then_inc(S["init_p"], 1)
            nc.gpsimd.memset(neg_ones[:], -1.0).then_inc(S["init_p"], 1)
            nc.gpsimd.memset(cmask[:, 0, :], 0.0).then_inc(S["init_p"], 1)
            nc.gpsimd.memset(one["ones"], 1.0).then_inc(S["init_p"], 1)
            nc.gpsimd.memset(one["pw"], -0.5).then_inc(S["init_p"], 1)
            pool.wait_ge(S["init_p"], 5)

            def rstds(n):
                for b in range(NB):
                    k = 2 * (n % 2) + b
                    pool.wait_ge(S["sumsq"], nval(n, b))
                    nc.gpsimd.tensor_scalar(var[:, k:k + 1], ss[:, k:k + 1], 1.0 / D, EPS, ALU.mult,
                                            ALU.add).then_inc(S["var_done"], 1)
                    pool.wait_ge(S["var_done"], nval(n, b))
                    nc.gpsimd.tensor_tensor(rstd[:, k:k + 1], var[:, k:k + 1], pow_half[:, 0:1],
                                            ALU.pow).then_inc(S["rstd_done"], 1)

            rstds(0)
            pool.wait_ge(S["relb_ps"], 1)
            nc.gpsimd.memset(upad, 0.0).then_inc(S["init_p"], 1)
            pool.wait_ge(S["lnvar"], 1)
            nc.gpsimd.tensor_scalar(one["vr"], one["vr"], 1.0, EPS, ALU.mult, ALU.add).then_inc(S["lnvar2"], 1)
            pool.wait_ge(S["lnvar2"], 1)
            nc.gpsimd.tensor_tensor(one["rs"], one["vr"], one["pw"], ALU.pow).then_inc(S["lnrs"], 1)
            rstds(1)
            rstds(2)
            for layer in range(LAYERS):
                n = 3 + 3 * layer
                rstds(n)
                pool.wait_ge(S["lora_sq"], 4 * layer + 4)
                nc.gpsimd.tensor_scalar(lvar[:, :, 0], lss[:, :, 0], 1.0 / QL, EPS, ALU.mult, ALU.add).then_inc(S["lora_var"], 1)
                nc.gpsimd.tensor_scalar(lvar[:, :, 1], lss[:, :, 1], 1.0 / KVL, EPS, ALU.mult, ALU.add).then_inc(S["lora_var"], 1)
                pool.wait_ge(S["lora_var"], 2 * layer + 2)
                nc.gpsimd.tensor_tensor(lrstd[:].rearrange("p b c -> p (b c)"), lvar[:].rearrange("p b c -> p (b c)"),
                                        pow_half[:], ALU.pow).then_inc(S["lora_rstd"], 1)
                rstds(n + 1)
                rstds(n + 2)
            rstds(LAST)

        @block.vector
        def _(dve):
            fed = [0]

            def feed(unit, ahead=LOOKAHEAD):
                while fed[0] < min(unit["s"] + 1 + ahead, len(SPLIT)):
                    u = SPLIT[fed[0]]
                    n = u["kts"] * u["cols"]
                    slot = u["s"] % SPLIT_SLOTS
                    dve.wait_ge(S["hi_done"], u["s"] + 1)
                    nc.vector.tensor_tensor(lo[:, slot, 0:n], raw[:, u["slot"], 0:n], hi[:, slot, 0:n].bitcast(F32),
                                            ALU.subtract).then_inc(S["lo_done"], 1)
                    fed[0] += 1

            def normalise(n):
                for b in range(NB):
                    k = 2 * (n % 2) + b
                    if b == 0:
                        dve.wait_ge(S["in_gain"], 16 * (n + 1))
                    dve.wait_ge(S["rstd_done"], nval(n, b))
                    last = n in (0, 1)
                    dst = h if n == 2 else xs
                    i = nc.vector.scalar_tensor_tensor(out=dst[:, b, :], in0=h[:, b, :], scalar=rstd[:, k:k + 1],
                                                       in1=gain[:, n % 2, :], op0=ALU.mult, op1=ALU.mult)
                    if last:
                        i.then_inc(S["xs_mid"], 1)
                        dve.wait_ge(S["xs_mid"], nval(n, b))
                        i = nc.vector.tensor_tensor(xs[:, b, :], xs[:, b, :], one["rowA"], ALU.add)
                    i.then_inc(S["h_ready"] if n == 2 else S["xs_ready"], 1)

            def low_T(t):
                for b in range(NB):
                    bank = 4 + 2 * b
                    dve.wait_ge(S["xh_ready"], tval(t, b))
                    sl = slice(b * P, (b + 1) * P)
                    nc.vector.tensor_tensor(xl[:, :, sl], ps[:, bank:bank + 2, :].rearrange("p a (k m) -> p (a k) m", k=4),
                                            xh[:, :, sl].bitcast(F32), ALU.subtract).then_inc(S["xl_ready"], 1)

            def mod_row(v):
                bank = 2 * (v % 2)
                src = ps[:, bank:bank + 2, :].rearrange("p a c -> p (a c)")
                dst = [one["rowB"], one["rowA"], one["g1"], one["rowA"], one["rowB"], one["g2"]][v]
                dve.wait_ge(S["in_rows"], 32 if v < 2 else 16 * 7)
                product(dve, ("mod", v), 3)
                nc.vector.tensor_tensor(dst, src, dst, ALU.add).then_inc(S["mod_evac"], 1)
                if v in (0, 4):
                    n = 0 if v == 0 else 1
                    dve.wait_ge(S["mod_evac"], v + 1)
                    dve.wait_ge(S["in_gain"], 16 * (n + 1))
                    nc.vector.scalar_tensor_tensor(out=gain[:, n, :], in0=dst, scalar=1.0, in1=gain[:, n, :], op0=ALU.add,
                                                   op1=ALU.mult).then_inc(S["mod_mid"], 1)
                    dve.wait_ge(S["mod_mid"], n + 1)

            dve.wait_ge(S["silu_c"], 1)
            nc.vector.tensor_copy(csb, vec[:, V_C:V_C + KT].rearrange("p (k a) -> p k a", a=1).broadcast_to([P, KT, P]))\
                .then_inc(S["csb_done"], 1)
            dve.wait_ge(S["in_consts"], 16)
            craw2 = craw
            for dst, c in ((ident[:], C_ID), (tri[:], C_TRI), (cmask[:, 1, :], C_CAUSAL), (strict[:], C_STRICT),
                           (ident16[:], C_ID), (masks16[:, 0, :], C_CAUSAL), (masks16[:, 1, :], C_STRICT)):
                nc.vector.tensor_copy(dst, craw2[:, c:c + P]).then_inc(S["init_v"], 1)
            nc.vector.tensor_copy(cosines[:].rearrange("p b d -> p (b d)"), craw2[:, C_COS:C_COS + 32]).then_inc(S["init_v"], 1)
            nc.vector.tensor_copy(sines[:].rearrange("p b d -> p (b d)"), craw2[:, C_SIN:C_SIN + 32]).then_inc(S["init_v"], 1)
            dve.wait_ge(S["in_rel"], 32)
            nc.vector.tensor_copy(rbb, rb.rearrange("p (h a) -> p h a", a=1).broadcast_to([BUCKETS + 1, HD, P]))\
                .then_inc(S["relb_done"], 1)
            mod_row(0)
            mod_row(1)
            dve.wait_ge(S["mod_evac"], 2)
            normalise(0)
            feed(units_of("pw1", 0)[0], 1)
            low_T(0)

            def gate_values(f):
                feed(units_of("pw1", f)[0], min(LOOKAHEAD, KT - 1 - f))
                dve.wait_ge(S["sig_done"], f + 1)
                dve.wait_ge(S["init_p"], 6)
                nc.vector.scalar_tensor_tensor(out=upad[:, f, :, HALO:HALO + SEG],
                                               in0=ps[:, 4 + f % 2, 0:SEQ].rearrange("p (s t) -> p s t", s=SEGS),
                                               scalar=vec[:, V_BPW1 + f:V_BPW1 + f + 1],
                                               in1=sig[:, f % 2, :].rearrange("p (s t) -> p s t", s=SEGS),
                                               op0=ALU.add, op1=ALU.mult).then_inc(S["glu_done"], 1)

            def convolve(f):
                dve.wait_ge(S["glu_done"], f + 1)
                if f == 0:
                    dve.wait_ge(S["in_skew"], 16 * HD)
                    dve.wait_ge(S["init_v"], 9)
                acc = cv[:, f, :].rearrange("p (s t) -> p s t", s=SEGS)
                for k in range(TAPS):
                    src = upad[:, f, :, k:k + SEG]
                    if k == 0:
                        i = nc.vector.tensor_scalar(acc, src, dw[:, f, 0:1], vec[:, V_BDW + f:V_BDW + f + 1],
                                                    ALU.mult, ALU.add)
                    else:
                        dve.wait_ge(S["conv_step"], f * TAPS + k)
                        i = nc.vector.scalar_tensor_tensor(out=acc, in0=src, scalar=dw[:, f, k:k + 1], in1=acc,
                                                           op0=ALU.mult, op1=ALU.add)
                    i.then_inc(S["conv_step"], 1)

            gated = 0
            for f in range(KT):
                while gated < min(2 * f + 1, KT):
                    gate_values(gated)
                    gated += 1
                convolve(f)
                if f >= 4:
                    mod_row(f - 2)
            dve.wait_ge(S["mod_evac"], 6)
            nc.vector.tensor_tensor(one["bpw2"], one["bpw2"], one["g1"], ALU.mult).then_inc(S["xprep"], 1)
            dve.wait_ge(S["xprep"], 1)
            for b in range(NB):
                nc.vector.tensor_tensor(h[:, b, :], h[:, b, :], one["bpw2"], ALU.add).then_inc(S["xprep"], 1)
            dve.wait_ge(S["mean_done"], 1)
            nc.vector.tensor_tensor(cv, cv, one["mu"].rearrange("p (a t) -> p a t", a=1).broadcast_to([P, KT, SEQ]),
                                    ALU.subtract).then_inc(S["cent_done"], 1)
            feed(last_of("pw2"), -2)
            dve.wait_ge(S["lnrs"], 1)
            dve.wait_ge(S["cent_done"], 1)
            nc.vector.tensor_tensor(cv, cv, one["rs"].rearrange("p (a t) -> p a t", a=1).broadcast_to([P, KT, SEQ]),
                                    ALU.mult).then_inc(S["ln_done"], 1)
            dve.wait_ge(S["yh_done"], 1)
            nc.vector.tensor_tensor(xl[:], sq, xh[:].bitcast(F32), ALU.subtract).then_inc(S["yl_done"], 1)
            feed(last_of("pw2"))

            rstep = [0]

            def residual(done, value, stage, index, scale_row):
                for b in range(NB):
                    block_product(dve, done, value, b, stage, index)
                    src = ps[:, 2 * b:2 * b + 2, :].rearrange("p a c -> p (a c)")
                    if scale_row is None:
                        nc.vector.tensor_tensor(h[:, b, :], src, h[:, b, :], ALU.add).then_inc(S["h_ready"], 1)
                    else:
                        nc.vector.tensor_tensor(xs[:, b, :], src, scale_row, ALU.mult).then_inc(S["res_step"], 1)
                        rstep[0] += 1
                        dve.wait_ge(S["res_step"], rstep[0])
                        nc.vector.tensor_tensor(h[:, b, :], xs[:, b, :], h[:, b, :], ALU.add).then_inc(S["h_ready"], 1)

            dve.wait_ge(S["xprep"], 3)
            residual("pw2_ps", 1, "pw2", 0, one["g1"])
            normalise(1)
            feed(last_of("w1", 0), 0)
            low_T(1)
            for j in range(MLP_CHUNKS):
                feed(last_of("w1", j))
                if j:
                    feed(last_of("w2", j - 1))
                for b in range(NB):
                    sl = slice(b * P, (b + 1) * P)
                    dve.wait_ge(S["gh_done"], 2 * j + b + 1)
                    nc.vector.tensor_tensor(gl[:, 0:4, sl], ps[:, 6 + b, :].rearrange("p (k m) -> p k m", k=4),
                                            gh[:, 0:4, sl].bitcast(F32), ALU.subtract).then_inc(S["gl_done"], 1)
            feed(last_of("w2", MLP_CHUNKS - 1))
            residual("mlp_ps", 1, "w2", MLP_CHUNKS - 1, one["g2"])
            normalise(2)

            for layer in range(LAYERS):
                n, t = 3 + 3 * layer, 2 + 4 * layer
                ghv = 2 * MLP_CHUNKS + (1 + 2 * FF_CHUNKS) * layer
                normalise(n)
                feed(last_of(("idx", layer)), -2)
                low_T(t)
                feed(last_of(("idx", layer)))
                product(dve, ("idx", layer))
                for c in range(2):
                    nc.vector.tensor_copy(ikd[:, :, c * DH:(c + 1) * DH], ps[:, 6:8, 0:DH]).then_inc(S["ikd_done"], 1)
                nc.vector.tensor_scalar(iw[:], ps[:, 6:8, DH:DH + HI], HI ** -0.5, None, ALU.mult).then_inc(S["iw_done"], 1)
                feed(last_of(("mla", layer)))
                dve.wait_ge(S["lora_rstd"], layer + 1)
                dve.wait_ge(S["in_lora"], 16 * (layer + 1))
                dve.wait_ge(S["kr_done"], 2 * layer + 2)
                for b in range(NB):
                    for c, (a, z) in enumerate(((0, QL), (QL, QL + KVL))):
                        nc.vector.scalar_tensor_tensor(out=cn[:, b, a:z], in0=ps[:, 2 * b + c, 0:z - a],
                                                       scalar=lrstd[:, b, c:c + 1], in1=lora_gain[:, a:z],
                                                       op0=ALU.mult, op1=ALU.mult).then_inc(S["cn_done"], 1)

                istep = [16 * layer]
                tstep = [2 * layer * (2 * TOPK // 8)]

                def index_scores(b):
                    r, order = ((relu1, ORDER8) if b else (relu0, ORDER8_B0))
                    dve.wait_ge(S["relu_i"], 2 * layer + (1 if b else 2))
                    if b:
                        dve.wait_ge(S["iw_done"], layer + 1)
                    for k in range(HI):
                        if k:
                            dve.wait_ge(S["isc_step"], istep[0])
                        head = order[k]
                        in1 = work[b] if k else (cmask[:].rearrange("p a k -> p (a k)") if b else cmask[:, 1, :])
                        nc.vector.scalar_tensor_tensor(out=work[b], in0=r[:, k, :], scalar=iw[:, b, head:head + 1],
                                                       in1=in1, op0=ALU.mult, op1=ALU.add).then_inc(S["isc_step"], 1)
                        istep[0] += 1
                    dve.wait_ge(S["isc_step"], istep[0])

                def top_keys(b):
                    for r in range(TOPK // 8):
                        nc.vector.max(top8[:], work[b]).then_inc(S["topk_step"], 1)
                        tstep[0] += 1
                        dve.wait_ge(S["topk_step"], tstep[0])
                        nc.vector.match_replace(work[b], top8[:], work[b], TAKEN).then_inc(S["topk_step"], 1)
                        tstep[0] += 1
                        dve.wait_ge(S["topk_step"], tstep[0])
                    nc.vector.tensor_scalar(work[b], work[b], 0.5 * TAKEN, NEG, ALU.is_gt, ALU.mult).then_inc(S["sel_done"], 1)

                index_scores(1)
                feed(last_of(("dsa", layer)))
                dve.wait_ge(S["gh_done"], ghv + 1)
                nc.vector.tensor_tensor(gl[:].rearrange("p k m -> p (k m)"),
                                        ps[:, 0:3, :].rearrange("p a c -> p (a c)")[:, 0:5 * SEQ],
                                        gh[:].rearrange("p k m -> p (k m)").bitcast(F32), ALU.subtract).then_inc(S["gl_done"], 1)
                index_scores(0)
                feed(last_of(("uq", layer)))
                top_keys(1)
                feed(last_of(("ukv", layer)))
                product(dve, ("ukv", layer))
                for b in range(NB):
                    src = ps[:, 4 + 2 * b:6 + 2 * b, 0:UKV_COLS // 2].rearrange("p a (h d) -> p a h d", h=3)
                    nc.vector.tensor_copy(mv[:, b, :, :].rearrange("p (a h) d -> p a h d", a=2),
                                          src[:, :, :, NOPE:NOPE + VD]).then_inc(S["kv_done"], 1)
                    nc.vector.tensor_copy(kfull[:, b, :, 0:NOPE].rearrange("p (a h) d -> p a h d", a=2),
                                          src[:, :, :, 0:NOPE]).then_inc(S["kv_done"], 1)
                feed(last_of(("sb", layer)))
                dve.wait_ge(S["q7_done"], 2 * layer + 2)
                dve.wait_ge(S["kr_done"], 2 * layer + 2)
                x1 = q7[:, :, :, NOPE:NOPE + HALF]
                x2 = q7[:, :, :, NOPE + HALF:QK]
                co = cosines[:].rearrange("p b (a d) -> p b a d", a=1).broadcast_to([P, NB, 7, HALF])
                si = sines[:].rearrange("p b (a d) -> p b a d", a=1).broadcast_to([P, NB, 7, HALF])
                for i, (xx, cs) in enumerate(((x1, co), (x2, si), (x1, si), (x2, co))):
                    nc.vector.tensor_tensor(rt[:, i], xx, cs, ALU.mult).then_inc(S["rope_t"], 1)
                dve.wait_ge(S["rope_t"], 4 * layer + 4)
                nc.vector.tensor_tensor(x1, rt[:, 0], rt[:, 1], ALU.subtract).then_inc(S["rope_done"], 1)
                nc.vector.tensor_tensor(x2, rt[:, 2], rt[:, 3], ALU.add).then_inc(S["rope_done"], 1)
                top_keys(0)
                feed(last_of(("sv", layer)))
                product(dve, ("sv", layer))
                for b in range(NB):
                    nc.vector.tensor_copy(sv[:, b, :], ps[:, 3 + b, 0:SV_COLS]).then_inc(S["sv_evac"], 1)
                dve.wait_ge(S["qkT_ps"], 2 * layer + 2)
                nc.vector.tensor_copy(kT[0:QK].rearrange("p h q -> p (h q)"),
                                      ps[0:QK, 0:3, :].rearrange("p a c -> p (a c)")).then_inc(S["kT_done"], 1)
                for i, b in enumerate((1, 0)):
                    dve.wait_ge(S["m_sc"], 2 * layer + i + 1)
                    src = (ps[:, 5:8, :].rearrange("p a (t k) -> p (a t) k", t=2) if b else
                           ps[:, 3:5, :].rearrange("p a (t k) -> p (a t) k", t=4)[:, 0:HM, :])
                    nc.vector.tensor_reduce(row_max[:, HM * b:HM * (b + 1)], src, AX.X, ALU.max).then_inc(S["m_max"], 1)
                    dve.wait_ge(S["m_max"], 2 * layer + i + 1)
                    nc.vector.tensor_scalar(neg_max[:, HM * b:HM * (b + 1)], row_max[:, HM * b:HM * (b + 1)],
                                            -QK ** -0.5, None, ALU.mult).then_inc(S["m_nm"], 1)
                dve.wait_ge(S["m_exp"], 2 * HM * (layer + 1))
                nc.vector.reciprocal(row_inv[:], row_sum[:]).then_inc(S["m_inv"], 1)
                dve.wait_ge(S["m_pT_ps"], 2 * layer + 2)
                nc.vector.tensor_copy(pmT[0], ps[:, 3:5, :].rearrange("p a c -> p (a c)")[:, 0:HM * P]).then_inc(S["m_pT"], 1)
                dve.wait_ge(S["m_inv"], layer + 1)

                def mix_out(name, o, banks, at, heads, inv):
                    for i, b in enumerate((1, 0)):
                        dve.wait_ge(S[o], 2 * layer + i + 1)
                        dst = xs[:, b, at:at + heads * DH].rearrange("p (h d) -> p h d", h=heads)
                        src = ps[:, banks[b], 0:heads * DH].rearrange("p (h d) -> p h d", h=heads)
                        if inv is None:
                            nc.vector.tensor_copy(dst, src).then_inc(S[name], 1)
                        else:
                            r = row_inv[:, heads * b:heads * (b + 1)].rearrange("p (h a) -> p h a", a=1)
                            nc.vector.tensor_tensor(dst, src, r.broadcast_to([P, heads, DH]), ALU.mult).then_inc(S[name], 1)

                mix_out("mix_m", "m_o", [3, 4], 0, HM, True)
                dve.wait_ge(S["s_ln"], layer + 1)
                nc.vector.scalar_tensor_tensor(out=sbt, in0=ps[:, 0:5, 0:3 * P], scalar=0.0, in1=sbt, op0=ALU.max,
                                               op1=ALU.add).then_inc(S["s_sp"], 1)
                mix_out("mix_s", "s_o", [5, 6], (HM + HD) * DH, HS, None)
                for i, b in enumerate((1, 0)):
                    nk = P * (b + 1)
                    dve.wait_ge(S["d_sc"], 2 * layer + i + 1)
                    bank = 0 if b else 3
                    src = ps[:, bank:bank + 3, :].rearrange("p a (t k) -> p (a t) k", t=2)[:, 0:HD, 0:nk]
                    bs = bias[:, :, 0:2 * P] if b else bias[:, :, P:2 * P]
                    nc.vector.scalar_tensor_tensor(out=pd[b], in0=src, scalar=DH ** -0.5, in1=bs, op0=ALU.mult,
                                                   op1=ALU.add).then_inc(S["d_b"], 1)
                    dve.wait_ge(S["d_b"], 2 * layer + i + 1)
                    dve.wait_ge(S["sel_done"], 2 * layer + 2)
                    chosen = work[b].rearrange("p (a k) -> p a k", a=1).broadcast_to([P, HD, nk])
                    nc.vector.tensor_tensor(pd[b], pd[b], chosen, ALU.add).then_inc(S["d_s"], 1)
                    dve.wait_ge(S["d_s"], 2 * layer + i + 1)
                    nc.vector.tensor_reduce(neg_max[:, HD * b:HD * (b + 1)], pd[b], AX.X, ALU.max,
                                            negate=True).then_inc(S["d_nm"], 1)
                dve.wait_ge(S["d_exp"], 2 * HD * (layer + 1))
                nc.vector.reciprocal(row_inv[:, 0:2 * HD], row_sum[:, 0:2 * HD]).then_inc(S["d_inv"], 1)
                dve.wait_ge(S["d_pT_ps"], 2 * layer + 2)
                nc.vector.tensor_copy(pdT[0], ps[:, 3:5, :].rearrange("p a c -> p (a c)")[:, 0:HD * P]).then_inc(S["d_pT"], 1)
                dve.wait_ge(S["d_inv"], layer + 1)
                mix_out("mix_d", "d_o", [5, 6], HM * DH, HD, True)
                feed(last_of(("wo", layer)), -2)
                low_T(t + 1)
                feed(last_of(("wo", layer)))
                residual("wo_ps", layer + 1, ("wo", layer), 0, None)
                normalise(n + 1)
                low_T(t + 2)
                for j in range(FF_CHUNKS):
                    feed(last_of(("gu", layer), j))
                    for b in range(NB):
                        k = FF_CHUNKS * layer + j
                        dve.wait_ge(S["silu_g"], 2 * k + b + 1)
                        if j:
                            dve.wait_ge(S["hidT_ps"], 2 * (MLP_CHUNKS + k - 1) + b + 1)
                        nc.vector.tensor_tensor(hid2[:, b, :], ps[:, 4 + b, FF_CHUNK:2 * FF_CHUNK], silu2[:, b, :],
                                                ALU.mult).then_inc(S["hid_g"], 1)
                    if j:
                        feed(last_of(("dn", layer), j - 1))
                    for b in range(NB):
                        sl = slice(b * P, (b + 1) * P)
                        dve.wait_ge(S["gh_done"], ghv + 1 + 2 * j + b + 1)
                        nc.vector.tensor_tensor(gl[:, 0:2, sl], ps[:, 6 + b, 0:2 * P].rearrange("p (k m) -> p k m", k=2),
                                                gh[:, 0:2, sl].bitcast(F32), ALU.subtract).then_inc(S["gl_done"], 1)
                feed(last_of(("dn", layer), FF_CHUNKS - 1))
                dve.wait_ge(S["ph_done"], layer + 1)
                nc.vector.tensor_tensor(gl[:, 0:2, :], pT, gh[:, 0:2, :].bitcast(F32), ALU.subtract).then_inc(S["pl_done"], 1)
                residual("dn_ps", layer + 1, ("dn", layer), FF_CHUNKS - 1, None)
                feed(last_of(("proj", layer)), 1)
                normalise(n + 2)
                low_T(t + 3)
                feed(last_of(("gate", layer)))
                for b in range(NB):
                    dve.wait_ge(S["sig_g"], 2 * layer + b + 1)
                    dve.wait_ge(S["proj_evac"], 2 * layer + b + 1)
                    nc.vector.tensor_tensor(sg[:, b, :], sg[:, b, :], pp[:, b, :], ALU.mult).then_inc(S["gmul"], 1)
                    dve.wait_ge(S["gmul"], 2 * layer + b + 1)
                    nc.vector.tensor_tensor(h[:, b, :], h[:, b, :], sg[:, b, :], ALU.add).then_inc(S["h_ready"], 1)
            normalise(LAST)

        @block.tensor
        def _(pe):
            def used(ins, u):
                ins.then_inc(S["used"], 1)

            def parts(u):
                n = u["kts"] * u["cols"]
                s = u["s"] % SPLIT_SLOTS
                pe.wait_ge(S["lo_done"], u["s"] + 1)
                return (hi[:, s, 0:n].rearrange("p (k c) -> p k c", k=u["kts"]),
                        lo[:, s, 0:n].rearrange("p (k c) -> p k c", k=u["kts"]))

            def three(out, ah, al, wh, wl, start, stop, skip=False, activation_first=True):
                ins = None
                passes = ((ah, wh), (al, wh), (ah, wl))
                for i, (a, w) in enumerate(passes):
                    l, r = (a, w) if activation_first else (w, a)
                    ins = nc.tensor.matmul(out, l, r, start=start and i == 0, stop=stop and i == 2,
                                           skip_group_check=skip)
                return ins

            def token_major(units, ah, al, columns, place, done=None, k_total=None, first=False, waits=None):
                k_total = k_total or sum(u["kts"] for u in units)
                for u in units:
                    wh, wl = parts(u)
                    for b in range(NB):
                        if waits:
                            waits(u, b)
                        sl = slice(b * P, (b + 1) * P)
                        for k in range(u["kts"]):
                            kk = u["k0"] + k
                            for i, c in enumerate(columns):
                                ins = three(place(b, i), ah[:, kk, sl], al[:, kk, sl], wh[:, k, c], wl[:, k, c],
                                            start=kk == 0, stop=kk == k_total - 1)
                        if u is units[-1] and done and b == 0:
                            done(ins)
                    used(ins, u)


            def transposes_T(t):
                norm = norm_of(t) if t >= 2 and (t - 2) % 4 != 1 or t < 2 else None
                for b in range(NB):
                    bank = 4 + 2 * b
                    if norm is not None:
                        pe.wait_ge(S["xs_ready"], xsval(norm, b))
                    for k in range(KT):
                        ins = nc.tensor.transpose(ps[:, bank + k // 4, (k % 4) * P:(k % 4 + 1) * P],
                                                  xs[:, b, k * P:(k + 1) * P], ident[:])
                    ins.then_inc(S["xT_ps"], 1)

            def xT(t):
                def waits(u, b):
                    if u["part"] == 0:
                        pe.wait_ge(S["xl_ready"], tval(t, b))
                return waits

            def mod_vector(v):
                bank = 2 * (v % 2)
                if v >= 2:
                    pe.wait_ge(S["mod_evac"], v - 1)
                for q in range(4):
                    u = units_of(("mod", v), q)[0]
                    pe.wait_ge(landed[u["slot"]], u["landed"])
                    w = raw[:, u["slot"], :].rearrange("p (k c) -> p k c", k=KT)
                    for k in range(KT):
                        ins = nc.tensor.matmul(ps[:, bank + q // 2, (q % 2) * 256:(q % 2 + 1) * 256], csb[:, k, :], w[:, k, :],
                                               start=(k == 0), stop=(k == KT - 1))
                    used(ins, u)

            pe.wait_ge(S["csb_done"], 1)
            pe.wait_ge(S["init_v"], 9)
            pe.wait_ge(S["relb_done"], 1)
            for head in range(HD):
                ins = nc.tensor.matmul(ps[:, 3 + head, 0:HOT], rbb[:, head, :], hot, start=True, stop=True)
            ins.then_inc(S["relb_ps"], 1)
            pe.wait_ge(S["toep_done"], 1)
            mod_vector(0)
            mod_vector(1)
            transposes_T(0)
            for f in range(KT):
                u = units_of("pw1", f)[0]
                wh, wl = parts(u)
                if f == 0:
                    pe.wait_ge(S["xl_ready"], tval(0, 1))
                if f >= 2:
                    pe.wait_ge(S["glu_done"], f - 1)
                for k in range(KT):
                    for c in range(2):
                        cs = slice(c * P, (c + 1) * P)
                        out_ = ps[:, 4 + f % 2, c * SEQ:(c + 1) * SEQ]
                        for i, (a, w) in enumerate(((xh, wh), (xl, wh), (xh, wl))):
                            ins = nc.tensor.matmul(out_, w[:, k, cs], a[:, k, :], start=(k == 0 and c == 0 and i == 0),
                                                   stop=(k == KT - 1 and i == 2), skip_group_check=True)
                used(ins, u)
            for v in range(2, 6):
                mod_vector(v)
            pe.wait_ge(S["conv_step"], KT * TAPS)
            pe.wait_ge(S["init_p"], 5)
            for f in range(KT):
                ins = nc.tensor.matmul(ps[:, 6, 0:SEQ], one["ones"], cv[:, f, :], start=(f == 0), stop=(f == KT - 1))
            ins.then_inc(S["mean_ps"], 1)
            pe.wait_ge(S["sq_done"], 1)
            for f in range(KT):
                ins = nc.tensor.matmul(ps[:, 7, 0:SEQ], one["ones"], sq[:, f, :], start=(f == 0), stop=(f == KT - 1))
            ins.then_inc(S["var_ps"], 1)
            pe.wait_ge(S["yl_done"], 1)
            halves = [slice(0, 512), slice(512, 1024)]
            pe.wait_ge(S["mod_evac"], 6)
            token_major(units_of("pw2"), xh, xl, halves, lambda b, i: ps[:, 2 * b + i, :],
                        done=lambda ins: ins.then_inc(S["pw2_ps"], 1))
            transposes_T(1)
            def w2_product(j):
                pe.wait_ge(S["gl_done"], 2 * j + 2)
                units = units_of("w2", j)
                for u in units:
                    wh, wl = parts(u)
                    for b in range(NB):
                        sl = slice(b * P, (b + 1) * P)
                        for k in range(u["kts"]):
                            kk = u["k0"] + k
                            for i, c in enumerate(halves):
                                ins = three(ps[:, 2 * b + i, :], gh[:, kk, sl], gl[:, kk, sl], wh[:, k, c], wl[:, k, c],
                                            start=(j == 0 and kk == 0), stop=(j == MLP_CHUNKS - 1 and kk == 3))
                        if j == MLP_CHUNKS - 1 and u is units[-1] and b == 0:
                            ins.then_inc(S["mlp_ps"], 1)
                    used(ins, u)

            for j in range(MLP_CHUNKS):
                xw = xT(1)

                def waits(u, b, j=j):
                    if j == 0:
                        xw(u, b)
                    if j and u["part"] == 0:
                        pe.wait_ge(S["relu_done"], 2 * (j - 1) + b + 1)

                token_major(units_of("w1", j), xh, xl, [slice(0, MLP_CHUNK)], lambda b, i: ps[:, 4 + b, :],
                            done=lambda ins: ins.then_inc(S["w1_ps"], 1), waits=waits)
                if j:
                    w2_product(j - 1)
                for b in range(NB):
                    pe.wait_ge(S["hid_done"], 2 * j + b + 1)
                    if j:
                        pe.wait_ge(S["gl_done"], 2 * (j - 1) + b + 1)
                    for k in range(4):
                        ins = nc.tensor.transpose(ps[:, 6 + b, k * P:(k + 1) * P], hid1[:, b, k * P:(k + 1) * P], ident[:])
                    ins.then_inc(S["hidT_ps"], 1)
            w2_product(MLP_CHUNKS - 1)

            for layer in range(LAYERS):
                t = 2 + 4 * layer
                glv = 2 * MLP_CHUNKS + (1 + 2 * FF_CHUNKS) * layer
                transposes_T(t)
                for u in units_of(("idx", layer)):
                    wh, wl = parts(u)
                    if u["part"] == 0:
                        pe.wait_ge(S["xl_ready"], tval(t, 1))
                    for k in range(u["kts"]):
                        kk = u["k0"] + k
                        for c in range(4):
                            cs = slice(c * P, (c + 1) * P)
                            for i, (a, w) in enumerate(((xh, wh), (xl, wh), (xh, wl))):
                                nc.tensor.matmul(ps[:, 4 + c // 2, (c % 2) * SEQ:(c % 2 + 1) * SEQ], w[:, k, cs], a[:, kk, :],
                                                 start=(kk == 0 and c % 2 == 0 and i == 0), stop=(kk == KT - 1 and i == 2),
                                                 skip_group_check=True)
                        for b in range(NB):
                            sl = slice(b * P, (b + 1) * P)
                            ins = three(ps[:, 6 + b, 0:DH + HI], xh[:, kk, sl], xl[:, kk, sl], wh[:, k, 512:IDX_COLS],
                                        wl[:, k, 512:IDX_COLS], start=kk == 0, stop=kk == KT - 1)
                    used(ins, u)
                units = units_of(("mla", layer))
                for u in units:
                    wh, wl = parts(u)
                    for b in range(NB):
                        sl = slice(b * P, (b + 1) * P)
                        for k in range(u["kts"]):
                            kk = u["k0"] + k
                            for i, c in enumerate((slice(0, QL), slice(QL, MLA_COLS))):
                                ins = three(ps[:, 2 * b + i, 0:c.stop - c.start], xh[:, kk, sl], xl[:, kk, sl],
                                            wh[:, k, c], wl[:, k, c], start=kk == 0, stop=kk == KT - 1)
                    used(ins, u)
                pe.wait_ge(S["ikd_done"], 2 * layer + 2)
                pe.wait_ge(S["iw_done"], layer + 1)
                for b in range(NB):
                    ins = nc.tensor.transpose(ps[:, 6, b * P:(b + 1) * P], ikd[:, b, :], ident[:])
                ins.then_inc(S["ikT_ps"], 1)
                pe.wait_ge(S["iqT_done"], layer + 1)
                pe.wait_ge(S["ikT_done"], layer + 1)
                for slot, head in enumerate(ORDER8):
                    r = slice(DH * (head % 2), DH * (head % 2) + DH)
                    ins = nc.tensor.matmul(ps[:, 4 + slot // 2, (slot % 2) * SEQ:(slot % 2 + 1) * SEQ], iqT[r, head // 2, P:2 * P],
                                           ikT[r, :], start=True, stop=True)
                ins.then_inc(S["isc_ps"], 1)
                pe.wait_ge(S["cn_done"], 4 * layer + 4)
                pe.wait_ge(S["kr_done"], 2 * layer + 2)
                for k in range(5):
                    for b in range(NB):
                        at = k * SEQ + b * P
                        ins = nc.tensor.transpose(ps[:, at // 512, at % 512:at % 512 + P], cn[:, b, k * P:(k + 1) * P], ident[:])
                ins.then_inc(S["cnT_ps"], 1)
                pe.wait_ge(S["relu_i"], 2 * layer + 1)
                for slot, head in enumerate(ORDER8_B0):
                    r = slice(DH * (head % 2), DH * (head % 2) + DH)
                    ins = nc.tensor.matmul(ps[:, 4 + slot // 4, (slot % 4) * P:(slot % 4 + 1) * P], iqT[r, head // 2, 0:P],
                                           ikT[r, 0:P], start=True, stop=True)
                ins.then_inc(S["isc_ps"], 1)
                units = units_of(("dsa", layer))
                for u in units:
                    wh, wl = parts(u)
                    for k in range(u["kts"]):
                        kk = u["k0"] + k
                        for c in range(3):
                            cs = slice(c * P, (c + 1) * P)
                            for i, (a, w) in enumerate(((xh, wh), (xl, wh), (xh, wl))):
                                nc.tensor.matmul(ps[:, 6 + c // 2, (c % 2) * SEQ:(c % 2 + 1) * SEQ], w[:, k, cs], a[:, kk, :],
                                                 start=(kk == 0 and c % 2 == 0 and i == 0), stop=(kk == KT - 1 and i == 2),
                                                 skip_group_check=True)
                        for b in range(NB):
                            sl = slice(b * P, (b + 1) * P)
                            for i, (a, w) in enumerate(((xh, wh), (xl, wh), (xh, wl))):
                                ins = nc.tensor.matmul(ps[:, 7, SEQ + b * DH:SEQ + (b + 1) * DH], a[:, kk, sl],
                                                       w[:, k, 3 * P:DSA_COLS], start=False,
                                                       stop=(kk == KT - 1 and i == 2), skip_group_check=True)
                    used(ins, u)
                for stage, cols, k0, bank0 in (("uq", UQ_COLS, 0, 0), ("ukv", UKV_COLS, 3, 4)):
                    u = units_of((stage, layer))[0]
                    wh, wl = parts(u)
                    if stage == "uq":
                        pe.wait_ge(S["gl_done"], glv + 1)
                    else:
                        pe.wait_ge(S["relu_i"], 2 * layer + 2)
                        pe.wait_ge(S["dsa_evac"], 5 * (layer + 1))
                    for b in range(NB):
                        sl = slice(b * P, (b + 1) * P)
                        for k in range(u["kts"]):
                            for i in range(2):
                                c = slice(i * cols // 2, (i + 1) * cols // 2)
                                ins = three(ps[:, bank0 + 2 * b + i, 0:cols // 2], gh[:, k0 + k, sl], gl[:, k0 + k, sl],
                                            wh[:, k, c], wl[:, k, c], start=k == 0, stop=k == u["kts"] - 1)
                    used(ins, u)
                pe.wait_ge(S["q7_done"], 2 * layer + 2)
                units = units_of(("sb", layer))
                for u in units:
                    wh, wl = parts(u)
                    for k in range(u["kts"]):
                        kk = u["k0"] + k
                        for c in range(5):
                            cs = slice(c * P, (c + 1) * P)
                            for i, (a, w) in enumerate(((xh, wh), (xl, wh), (xh, wl))):
                                ins = nc.tensor.matmul(ps[:, c // 2, (c % 2) * SEQ:(c % 2 + 1) * SEQ], w[:, k, cs], a[:, kk, :],
                                                       start=(kk == 0 and c % 2 == 0 and i == 0),
                                                       stop=(kk == KT - 1 and i == 2), skip_group_check=True)
                    used(ins, u)
                units = units_of(("sv", layer))
                for u in units:
                    wh, wl = parts(u)
                    for b in range(NB):
                        sl = slice(b * P, (b + 1) * P)
                        for k in range(u["kts"]):
                            kk = u["k0"] + k
                            ins = three(ps[:, 3 + b, 0:SV_COLS], xh[:, kk, sl], xl[:, kk, sl], wh[:, k, :], wl[:, k, :],
                                        start=kk == 0, stop=kk == KT - 1)
                    used(ins, u)
                pe.wait_ge(S["rope_done"], 2 * layer + 2)
                for hh in range(HM):
                    for b in range(NB):
                        at = hh * SEQ + b * P
                        ins = nc.tensor.transpose(ps[0:QK, 5 + at // 512, at % 512:at % 512 + P], q7[:, b, hh, :], ident[:])
                ins.then_inc(S["qkT_ps"], 1)
                pe.wait_ge(S["kf_done"], 2 * layer + 2)
                pe.wait_ge(S["sb_evac"], 4 * (layer + 1))
                for hh in range(HM):
                    for b in range(NB):
                        at = hh * SEQ + b * P
                        ins = nc.tensor.transpose(ps[0:QK, at // 512, at % 512:at % 512 + P], kfull[:, b, hh, :], ident[:])
                ins.then_inc(S["qkT_ps"], 1)
                pe.wait_ge(S["qT_done"], layer + 1)
                pe.wait_ge(S["kT_done"], layer + 1)
                pe.wait_ge(S["sv_evac"], 2 * layer + 2)
                for b in (1, 0):
                    nk = P * (b + 1)
                    for hh in range(HM):
                        at = hh * nk
                        bank = (5 if b else 3) + at // 512
                        nc.tensor.matmul(ps[:, bank, at % 512:at % 512 + nk], qT[0:QK, hh, b * P:(b + 1) * P], kT[0:QK, hh, 0:nk],
                                         start=True, stop=False, skip_group_check=True)
                        at += nk - P
                        ins = nc.tensor.matmul(ps[:, bank, at % 512:at % 512 + P], ident16[:], masks16[:, 0, :],
                                               start=False, stop=True, skip_group_check=True)
                    ins.then_inc(S["m_sc"], 1)
                pe.wait_ge(S["m_exp"], 2 * HM * layer + HM)
                for hh in range(HM):
                    for k in range(2):
                        at = (2 * hh + k) * P
                        ins = nc.tensor.transpose(ps[:, 5 + at // 512, at % 512:at % 512 + P], pm[1][:, hh, k * P:(k + 1) * P], ident[:])
                ins.then_inc(S["m_pT_ps"], 1)
                pe.wait_ge(S["m_exp"], 2 * HM * (layer + 1))
                for hh in range(HM):
                    at = hh * P
                    ins = nc.tensor.transpose(ps[:, 3 + at // 512, at % 512:at % 512 + P], pm[0][:, hh, :], ident[:])
                ins.then_inc(S["m_pT_ps"], 1)

                pe.wait_ge(S["m_pT"], 2 * layer + 2)
                v = pmT[1].rearrange("p (h k q) -> p h k q", h=HM, k=2)
                for b in (1, 0):
                    for hh in range(HM):
                        if b:
                            for k in range(2):
                                ins = nc.tensor.matmul(ps[:, 4, hh * VD:(hh + 1) * VD], v[:, hh, k, :], mv[:, k, hh, :],
                                                       start=k == 0, stop=k == 1)
                        else:
                            ins = nc.tensor.matmul(ps[:, 3, hh * VD:(hh + 1) * VD],
                                                   pmT[0][:, hh * P:(hh + 1) * P], mv[:, 0, hh, :], start=True, stop=True)
                    ins.then_inc(S["m_o"], 1)
                pe.wait_ge(S["mix_m"], 2 * layer + 2)
                rows_of = [(slice(0, DH), 0, 2), (slice(DH, P), 0, 2), (slice(0, DH), 1, 3), (slice(DH, P), 1, 3),
                           (slice(0, DH), 4, 5)]
                for hh in range(HS):
                    r, tq, tk = rows_of[hh]
                    nc.tensor.matmul(ps[:, hh, 0:2 * P], sT[r, tk, 0:P], sT[r, tq, :], start=True, stop=False,
                                     skip_group_check=True)
                    nc.tensor.matmul(ps[:, hh, 2 * P:3 * P], sT[r, tk, P:2 * P], sT[r, tq, P:2 * P], start=False,
                                     stop=False, skip_group_check=True)
                for hh in range(HS):
                    for c in (0, 2):
                        ins = nc.tensor.matmul(ps[:, hh, c * P:(c + 1) * P], ident16[:], masks16[:, 1, :], start=False,
                                               stop=True, skip_group_check=True)
                ins.then_inc(S["s_z"], 1)
                pe.wait_ge(S["s_sp"], layer + 1)
                for hh in range(HS):
                    for dst, w, src in ((slice(0, P), tri, slice(0, P)), (slice(P, 2 * P), tri, slice(P, 2 * P)),
                                        (slice(P, 2 * P), neg_ones, slice(2 * P, 3 * P)), (slice(2 * P, 3 * P), tri, slice(2 * P, 3 * P))):
                        ins = nc.tensor.matmul(ps[:, hh, dst], w[:], sbt[:, hh, src], start=False, stop=True,
                                               skip_group_check=True)
                ins.then_inc(S["s_zs"], 1)
                pe.wait_ge(S["s_w"], layer + 1)
                for b in (1, 0):
                    for hh in range(HS):
                        o = ps[:, 5 + b, hh * DH:(hh + 1) * DH]
                        if b:
                            nc.tensor.matmul(o, sbt[:, hh, P:2 * P], sv[:, 0, hh * DH:(hh + 1) * DH], start=True, stop=False)
                            ins = nc.tensor.matmul(o, sbt[:, hh, 2 * P:3 * P], sv[:, 1, hh * DH:(hh + 1) * DH], start=False, stop=True)
                        else:
                            ins = nc.tensor.matmul(o, sbt[:, hh, 0:P], sv[:, 0, hh * DH:(hh + 1) * DH], start=True, stop=True)
                    ins.then_inc(S["s_o"], 1)
                pe.wait_ge(S["mix_s"], 2 * layer + 2)
                for b in (1, 0):
                    nk = P * (b + 1)
                    for slot, head in enumerate(ORDER5):
                        r = slice(DH * (head % 2), DH * (head % 2) + DH)
                        ins = nc.tensor.matmul(ps[:, (0 if b else 3) + slot // 2, (slot % 2) * SEQ:(slot % 2) * SEQ + nk],
                                               dT[r, head // 2, b * P:(b + 1) * P], dkT[r, 0:nk], start=True, stop=True)
                    ins.then_inc(S["d_sc"], 1)
                pe.wait_ge(S["d_exp"], 2 * HD * layer + HD)
                pe.wait_ge(S["d_b"], 2 * layer + 2)
                for slot in range(HD):
                    for k in range(2):
                        at = (2 * slot + k) * P
                        ins = nc.tensor.transpose(ps[:, at // 512, at % 512:at % 512 + P], pd[1][:, slot, k * P:(k + 1) * P], ident[:])
                ins.then_inc(S["d_pT_ps"], 1)
                pe.wait_ge(S["d_exp"], 2 * HD * (layer + 1))
                for slot in range(HD):
                    at = slot * P
                    ins = nc.tensor.transpose(ps[:, 3 + at // 512, at % 512:at % 512 + P], pd[0][:, slot, :], ident[:])
                ins.then_inc(S["d_pT_ps"], 1)
                pe.wait_ge(S["d_pT"], 2 * layer + 2)
                for b in (1, 0):
                    for slot, head in enumerate(ORDER5):
                        o = ps[:, 5 + b, head * DH:(head + 1) * DH]
                        nkt = b + 1
                        for k in range(nkt):
                            at = (nkt * slot + k) * P
                            ins = nc.tensor.matmul(o, pdT[b][:, at:at + P], dv[:, k, :], start=k == 0, stop=k == nkt - 1)
                    ins.then_inc(S["d_o"], 1)
                pe.wait_ge(S["mix_d"], 2 * layer + 2)
                transposes_T(t + 1)
                token_major(units_of(("wo", layer)), xh, xl, halves, lambda b, i: ps[:, 2 * b + i, :],
                            done=lambda ins: ins.then_inc(S["wo_ps"], 1), waits=xT(t + 1))
                transposes_T(t + 2)

                def dn_product(j):
                    pe.wait_ge(S["gl_done"], glv + 1 + 2 * (j + 1))
                    u = units_of(("dn", layer), j)[0]
                    wh, wl = parts(u)
                    last = j == FF_CHUNKS - 1
                    for b in range(NB):
                        sl = slice(b * P, (b + 1) * P)
                        for k in range(u["kts"]):
                            for i, c in enumerate(halves):
                                ins = three(ps[:, 2 * b + i, :], gh[:, k, sl], gl[:, k, sl], wh[:, k, c], wl[:, k, c],
                                            start=(j == 0 and k == 0), stop=last and k == 1)
                        if last and b == 0:
                            ins.then_inc(S["dn_ps"], 1)
                    used(ins, u)

                for j in range(FF_CHUNKS):
                    xw = xT(t + 2)
                    k_ = FF_CHUNKS * layer + j

                    def waits(u, b, j=j, k_=k_):
                        if j == 0:
                            xw(u, b)
                        elif u["part"] == 0:
                            pe.wait_ge(S["hid_g"], 2 * (k_ - 1) + b + 1)

                    token_major(units_of(("gu", layer), j), xh, xl, [slice(0, 512)], lambda b, i: ps[:, 4 + b, :],
                                done=lambda ins: ins.then_inc(S["gu_ps"], 1), waits=waits)
                    if j == 1:
                        pe.wait_ge(S["h_ready"], hval(4 + 3 * layer, 1))
                    if j:
                        dn_product(j - 1)
                    for b in range(NB):
                        pe.wait_ge(S["hid_g"], 2 * k_ + b + 1)
                        if j:
                            pe.wait_ge(S["gl_done"], glv + 1 + 2 * (j - 1) + b + 1)
                        for k in range(2):
                            ins = nc.tensor.transpose(ps[:, 6 + b, k * P:(k + 1) * P], hid2[:, b, k * P:(k + 1) * P], ident[:])
                        ins.then_inc(S["hidT_ps"], 1)
                dn_product(FF_CHUNKS - 1)
                pe.wait_ge(S["pl_done"], layer + 1)
                pe.wait_ge(S["h_ready"], hval(5 + 3 * layer, 1))
                u = units_of(("proj", layer))[0]
                wh, wl = parts(u)
                for b in range(NB):
                    sl = slice(b * P, (b + 1) * P)
                    for k in range(2):
                        for i, c in enumerate(halves):
                            ins = three(ps[:, 2 * b + i, :], gh[:, k, sl], gl[:, k, sl], wh[:, k, c], wl[:, k, c],
                                        start=k == 0, stop=k == 1)
                used(ins, u)
                transposes_T(t + 3)
                xw3 = xT(t + 3)

                def waits3(u, b):
                    xw3(u, b)
                    if u["part"] == 0:
                        pe.wait_ge(S["proj_evac"], 2 * layer + b + 1)

                token_major(units_of(("gate", layer)), xh, xl, halves, lambda b, i: ps[:, 2 * b + i, :],
                            done=lambda ins: ins.then_inc(S["gate_ps"], 1), waits=waits3)


def bucket_table():
    d = (2 * P - 1 - np.arange(HOT)).astype(np.int64)
    exact = BUCKETS // 2
    dd = np.maximum(d, 1).astype(np.float32)
    large = exact + (np.log(dd / np.float32(exact)) / np.float32(np.log(MAX_DIST / exact)) * (BUCKETS - exact)).astype(np.int32)
    bucket = np.where(d < exact, d, np.minimum(large, BUCKETS - 1))
    table = np.zeros((P, HOT), np.float32)
    for i in range(HOT):
        if d[i] >= 0:
            table[bucket[i], i] = 1.0
        else:
            table[BUCKETS, i] = NEG
    return table


def constants():
    c = np.zeros((P, C_END), np.float32)
    a, b = np.arange(P)[:, None], np.arange(P)[None, :]
    c[:, C_ID:C_ID + P] = a == b
    c[:, C_TRI:C_TRI + P] = -1.0 * (a >= b)
    c[:, C_CAUSAL:C_CAUSAL + P] = np.where(b > a, NEG, 0.0)
    c[:, C_STRICT:C_STRICT + P] = np.where(a >= b, NEG, 0.0)
    inv = np.float32(10000.0) ** (-np.arange(HALF, dtype=np.float32) / np.float32(HALF))
    ang = np.arange(SEQ, dtype=np.float32)[:, None] * inv[None, :]
    for tab, at in ((np.cos(ang), C_COS), (np.sin(ang), C_SIN)):
        c[:, at:at + NB * HALF] = tab.astype(np.float32).reshape(NB, P, HALF).transpose(1, 0, 2).reshape(P, NB * HALF)
    c[:, C_HOT:] = bucket_table()
    return c


def lay_out(inputs):
    g = lambda n: np.ascontiguousarray(inputs[n])
    flat = np.empty(STREAM, np.float32)

    def put(stage, n, w):
        for u in units_of(stage, n):
            part = w[u["k0"] * P:(u["k0"] + u["kts"]) * P]
            assert part.shape[1] == u["cols"]
            flat[u["offset"]:u["offset"] + part.size] = part.reshape(u["kts"], P, u["cols"]).transpose(1, 0, 2).reshape(-1)

    wm = g("w_mod")[0]
    order = [1, 0, 2, 3, 4, 5]
    for v, src in enumerate(order):
        for q in range(4):
            put(("mod", v), q, wm[:, src * D + q * 256:src * D + (q + 1) * 256])
    pw1 = g("conv_w_pw1")[0]
    for f in range(KT):
        put("pw1", f, np.concatenate([pw1[:, f * P:(f + 1) * P], pw1[:, D + f * P:D + (f + 1) * P]], 1))
    put("pw2", 0, g("conv_w_pw2")[0])
    w1, w2 = g("mlp_w1")[0], g("mlp_w2")[0]
    for j in range(MLP_CHUNKS):
        put("w1", j, w1[:, j * MLP_CHUNK:(j + 1) * MLP_CHUNK])
        put("w2", j, w2[j * MLP_CHUNK:(j + 1) * MLP_CHUNK])
    for layer in range(LAYERS):
        w = g("w_in_2")[layer]
        at = np.cumsum([0, QL, KVL, ROPE, HD * DH, DH, DH, HI * DH, DH, HI, HS * DH, HS * DH, HS * DH])
        put(("idx", layer), 0, w[:, at[6]:at[9]])
        put(("mla", layer), 0, w[:, at[0]:at[3]])
        put(("dsa", layer), 0, w[:, at[3]:at[6]])
        q, k = at[9], at[10]
        put(("sb", layer), 0, np.concatenate([w[:, q:q + 128], w[:, q + 128:q + 256], w[:, k:k + 128], w[:, k + 128:k + 256],
                                              w[:, q + 256:q + 320], w[:, k + 256:k + 320]], 1))
        put(("sv", layer), 0, w[:, at[11]:at[12]])
        put(("uq", layer), 0, g("mla_w_uq_2")[layer])
        put(("ukv", layer), 0, g("mla_w_ukv_2")[layer])
        put(("wo", layer), 0, g("w_o_2")[layer])
        wg, wu, wd = g("w_gate_2")[layer], g("w_up_2")[layer], g("w_down_2")[layer]
        for j in range(FF_CHUNKS):
            c = slice(j * FF_CHUNK, (j + 1) * FF_CHUNK)
            put(("gu", layer), j, np.concatenate([wg[:, c], wu[:, c]], 1))
            put(("dn", layer), j, wd[c])
        put(("proj", layer), 0, g("w_ple_proj_2")[layer])
        put(("gate", layer), 0, g("w_ple_gate_2")[layer])

    cols = lambda v: v.reshape(-1, P).T
    vectors = np.concatenate([cols(g("c")[0]), cols(g("conv_b_pw1")[0]), cols(g("conv_b_dw")[0]), cols(g("conv_ln_g")[0]),
                              cols(g("conv_ln_b")[0]),
                              g("conv_w_dw")[0].reshape(TAPS, KT, P).transpose(2, 1, 0).reshape(P, KT * TAPS)], 1)
    bm = g("b_mod")[0]
    rows = {f"b_mod{i}": bm[i * D:(i + 1) * D] for i in range(6)}
    rows.update(b_pw2=g("conv_b_pw2")[0], norm1_g=g("norm1_g")[0], norm2_g=g("norm2_g")[0], final_g=g("final_g"),
                final=g("final_norm_2"))
    for l in range(LAYERS):
        rows[f"attn{l}"] = g("attn_norm_2")[l]
        rows[f"ffn{l}"] = g("ffn_norm_2")[l]
        rows[f"ple{l}"] = g("ple_norm_2")[l]
        rows[f"lora{l}"] = np.concatenate([g("mla_q_norm_2")[l], g("mla_kv_norm_2")[l]])
    rel = np.concatenate([g("rel_bias_2"), np.ones((1, HD), np.float32)], 0)
    arrays = dict(stream=flat, x=g("x")[0], p_t=np.ascontiguousarray(g("p_2")[:, 0].transpose(0, 2, 1)),
                  vectors=np.ascontiguousarray(vectors), rel=rel, consts=constants())
    for k, v in rows.items():
        arrays["row_" + k] = np.ascontiguousarray(v)
    return arrays


def kernel(**inputs):
    import concourse.bacc as bacc
    from concourse.bass_utils import run_bass_kernel_spmd as run

    nc = bacc.Bacc("TRN2", target_bir_lowering=False, num_devices=1)
    arrays = lay_out(inputs)
    aps = {n: nc.dram_tensor(n, a.shape, mybir.dt.from_np(a.dtype), kind="ExternalInput").ap() for n, a in arrays.items()}
    rows = {n[4:]: ap for n, ap in aps.items() if n.startswith("row_")}
    out = nc.dram_tensor("out", (SEQ, D), F32, kind="ExternalOutput").ap()
    build(nc, aps["stream"], aps["x"], aps["p_t"], aps["vectors"], rows, aps["rel"], aps["consts"], out)
    r = run(nc, [arrays], core_ids=[0])
    return r.results[0]["out"].reshape(1, SEQ, D)
```

```python
from contextlib import ExitStack

import numpy as np

import concourse.bass as bass
from concourse import mybir

F32 = mybir.dt.float32
F32R = mybir.dt.float32r
BF16 = mybir.dt.bfloat16
ALU = mybir.AluOpType
ACT = mybir.ActivationFunctionType
AX = mybir.AxisListType

P = 128
D = 1024
KT = D // P
SEQ = 256
NB = SEQ // P
EPS = 1e-6
LAYERS = 2

SEG = 64
SEGS = SEQ // SEG
TAPS = 31
HALO = TAPS // 2
PADDED = SEG + 2 * HALO
FFN1 = 4 * D
MLP_CHUNK = 512
MLP_CHUNKS = FFN1 // MLP_CHUNK

HM, NOPE, ROPE, VD = 6, 64, 32, 64
HALF = ROPE // 2
QK = NOPE + ROPE
QL, KVL = 384, 256
HD = 5
HI = 8
HS = 5
DH = 64
TOPK = 64
BUCKETS, MAX_DIST = 32, 128
DFF = 2816
FF_CHUNK = 256
FF_CHUNKS = DFF // FF_CHUNK
PLE = 256

SLOT = 2048
RAW_SLOTS = 4
SPLIT_SLOTS = 3
LOOKAHEAD = SPLIT_SLOTS - 1
NEG = -1.0e30
TAKEN = -3.0e38

IDX_COLS = HI * DH + DH + HI
MLA_COLS = QL + KVL + ROPE
DSA_COLS = (HD + 2) * DH
SB_COLS = 2 * HS * DH
SV_COLS = HS * DH
UQ_COLS = HM * QK
UKV_COLS = HM * (NOPE + VD)

ORDER5 = [0, 2, 1, 3, 4]
ORDER8 = [0, 2, 1, 3, 4, 6, 5, 7]
ORDER8_B0 = [0, 2, 4, 6, 1, 3, 5, 7]


def plan_units():
    units = []

    def add(stage, n, kts, cols, split=True):
        k0 = 0
        for i, k in enumerate(kts):
            units.append(dict(stage=stage, n=n, part=i, k0=k0, kts=k, cols=cols, split=split))
            k0 += k

    for v in range(2):
        for q in range(4):
            add(("mod", v), q, [KT], 256, split=False)
    for f in range(KT):
        add("pw1", f, [KT], 256)
    for v in range(2, 6):
        for q in range(4):
            add(("mod", v), q, [KT], 256, split=False)
    add("pw2", 0, [2] * 4, D)
    for j in range(MLP_CHUNKS + 1):
        if j < MLP_CHUNKS:
            add("w1", j, [4, 4], MLP_CHUNK)
        if j:
            add("w2", j - 1, [2, 2], D)
    for layer in range(LAYERS):
        add(("idx", layer), 0, [3, 3, 2], IDX_COLS)
        add(("mla", layer), 0, [3, 3, 2], MLA_COLS)
        add(("dsa", layer), 0, [4, 4], DSA_COLS)
        add(("uq", layer), 0, [QL // P], UQ_COLS)
        add(("ukv", layer), 0, [KVL // P], UKV_COLS)
        add(("sb", layer), 0, [3, 3, 2], SB_COLS)
        add(("sv", layer), 0, [4, 4], SV_COLS)
        add(("wo", layer), 0, [2] * 4, D)
        for j in range(FF_CHUNKS + 1):
            if j < FF_CHUNKS:
                add(("gu", layer), j, [4, 4], 2 * FF_CHUNK)
            if j:
                add(("dn", layer), j - 1, [2], D)
        add(("proj", layer), 0, [PLE // P], D)
        add(("gate", layer), 0, [2] * 4, D)
    at, split, landed = 0, 0, [0] * RAW_SLOTS
    for i, u in enumerate(units):
        u["index"] = i
        u["offset"] = at
        at += P * u["kts"] * u["cols"]
        u["slot"] = i % RAW_SLOTS
        landed[u["slot"]] += 16
        u["landed"] = landed[u["slot"]]
        if u["split"]:
            u["s"] = split
            split += 1
    return units, at


UNITS, STREAM = plan_units()
SPLIT = [u for u in UNITS if u["split"]]


def units_of(stage, n=0):
    return [u for u in UNITS if u["stage"] == stage and u["n"] == n]


def last_of(stage, n=0):
    return units_of(stage, n)[-1]


C_ID, C_TRI, C_OPEN, C_CAUSAL, C_STRICT = (i * P for i in range(5))
C_COS = C_STRICT + P
C_SIN = C_COS + NB * HALF
C_HOT = C_SIN + NB * HALF
HOT = 3 * P
C_END = C_HOT + HOT

POOL_PAIRS = ((0, 1), (4, 5))
DVE_PAIRS = ((2, 3), (6, 7))
PRODUCTS = 4
GATES = 4

V_C, V_BPW1, V_BDW, V_LNG, V_LNB, V_DW = 0, 8, 24, 32, 40, 48
V_END = V_DW + KT * TAPS


def build(nc, stream, x, p_t, vectors, rows, rel, consts, out):
    ctx = ExitStack()
    with ctx:
        def sb(name, shape, dt=F32):
            return ctx.enter_context(nc.sbuf_tensor(name, shape, dt))

        def sem(name):
            return ctx.enter_context(nc.semaphore(name))

        raw = sb("raw", [P, RAW_SLOTS, SLOT])
        hi = sb("hi", [P, SPLIT_SLOTS, SLOT], F32R)
        lo = sb("lo", [P, SPLIT_SLOTS, SLOT], F32R)
        xh = sb("xh", [P, KT, SEQ], F32R)
        xl = sb("xl", [P, KT, SEQ], F32R)
        gh = sb("gh", [P, 5, SEQ], F32R)
        gl = sb("gl", [P, 5, SEQ], F32R)
        h = sb("h", [P, NB, D])
        xs = sb("xs", [P, NB, D])
        gain = sb("gain", [P, 2, D])
        lora_gain = sb("lora_gain", [P, QL + KVL])
        table = sb("table", [P, C_HOT])
        neg_ones = sb("neg_ones", [P, P])
        ident16 = sb("ident16", [P, P], BF16)
        masks16 = sb("masks16", [P, 2, P], BF16)
        bias = sb("bias", [P, HD, 2 * P])
        ss = sb("ss", [P, 4])
        var = sb("var", [P, 4])
        rstd = sb("rstd", [P, 4])
        pow_half = sb("pow_half", [P, 4])
        lss = sb("lss", [P, NB, 2])
        lvar = sb("lvar", [P, NB, 2])
        lrstd = sb("lrstd", [P, NB, 2])
        top8 = sb("top8", [P, 8])
        neg_max = sb("neg_max", [P, 12])
        row_max = sb("row_max", [P, 12])
        row_sum = sb("row_sum", [P, 12])
        row_inv = sb("row_inv", [P, 12])
        iw = sb("iw", [P, NB, HI])
        epsilon = sb("epsilon", [P, 1])
        scratch = sb("scratch", [P, 16512])
        ident = table[:, C_ID:C_ID + P]
        tri = table[:, C_TRI:C_TRI + P]
        cmask = table[:, C_OPEN:C_OPEN + 2 * P]
        cosines = table[:, C_COS:C_COS + NB * HALF].rearrange("p (b d) -> p b d", b=NB)
        sines = table[:, C_SIN:C_SIN + NB * HALF].rearrange("p (b d) -> p b d", b=NB)

        ps = ctx.enter_context(nc.psum_tensor("ps", [P, 8, 512], F32))

        def carve(table, start=0):
            views, at = {}, start
            for name, size in table:
                views[name] = scratch[:, at:at + size]
                at += size
            assert at <= 16512, at
            return views

        one = carve([("upad", KT * SEGS * PADDED), ("sig", GATES * SEQ), ("cv", KT * SEQ), ("rs", SEQ), ("sq", KT * SEQ), ("csb", KT * P), ("rowA", D), ("rowB", D),
                     ("g1", D), ("g2", D), ("bpw2", D), ("vec", V_END), ("ones", P), ("rbb", HD * P)])
        upad = one["upad"].rearrange("p (f s t) -> p f s t", f=KT, s=SEGS)
        sig = one["sig"].rearrange("p (b t) -> p b t", b=GATES)
        cv = one["cv"].rearrange("p (f t) -> p f t", f=KT)
        sq = one["sq"].rearrange("p (f t) -> p f t", f=KT)
        csb = one["csb"].rearrange("p (k m) -> p k m", k=KT)
        vec = one["vec"]
        dw = vec[:, V_DW:V_END].rearrange("p (f k) -> p f k", f=KT)
        hid1 = one["sq"][:, 0:NB * MLP_CHUNK].rearrange("p (b c) -> p b c", b=NB)
        taps = one["sq"].rearrange("p (i f t) -> p i f t", i=PRODUCTS, f=2)
        rbb = one["rbb"][0:BUCKETS + 1, :].rearrange("p (h m) -> p h m", h=HD)
        rb = one["cv"][0:BUCKETS + 1, 0:HD]
        hot = one["cv"][0:BUCKETS + 1, 512:512 + HOT]
        toep = one["sq"][:, 0:HD * 3 * P].rearrange("p (h d) -> p h d", h=HD)

        two = carve([("Z", 3072), ("X", 2304), ("Y", 2304), ("iqT", 4 * SEQ), ("ikT", SEQ), ("work", 3 * P),
                     ("dT", 3 * SEQ), ("dkT", SEQ), ("dv", NB * DH), ("sT", 6 * SEQ), ("sv", NB * SV_COLS),
                     ("mv", NB * HM * VD), ("qT", HM * SEQ), ("kT", HM * SEQ)])
        relu1 = two["Z"][:, 0:2048].rearrange("p (h k) -> p h k", h=HI)
        relu0 = two["Z"][:, 2048:3072].rearrange("p (h k) -> p h k", h=HI)
        kfull = two["Z"][:, 0:NB * HM * QK].rearrange("p (b h d) -> p b h d", b=NB, h=HM)
        sbt = two["Z"][:, 1152:1152 + HS * 384].rearrange("p (h k) -> p h k", h=HS)
        cn = two["X"][:, 0:NB * (QL + KVL)].rearrange("p (b c) -> p b c", b=NB)
        q7 = two["Y"][:, 0:NB * 7 * QK].rearrange("p (b h d) -> p b h d", b=NB, h=7)
        rt = two["Y"][:, 1344:1344 + 4 * 224].rearrange("p (i b h d) -> p i b h d", i=4, b=NB, h=7)
        ikd = two["Y"][:, 2048:2304].rearrange("p (b d) -> p b d", b=NB)
        pm = [two["X"][:, 1536:2304].rearrange("p (h k) -> p h k", h=HM),
              two["X"][:, 0:1536].rearrange("p (h k) -> p h k", h=HM)]
        pmT = [two["Y"][:, 1536:2304], two["Y"][:, 0:1536]]
        pd = [two["X"][:, 1280:1920].rearrange("p (h k) -> p h k", h=HD),
              two["X"][:, 0:1280].rearrange("p (h k) -> p h k", h=HD)]
        pdT = [two["Y"][:, 1280:1920], two["Y"][:, 0:1280]]
        iqT = two["iqT"].rearrange("p (t q) -> p t q", t=4)
        ikT = two["ikT"]
        work = [two["work"][:, 0:P], two["work"][:, P:3 * P]]
        dT = two["dT"].rearrange("p (t q) -> p t q", t=3)
        dkT = two["dkT"]
        dv = two["dv"].rearrange("p (b d) -> p b d", b=NB)
        sT = two["sT"].rearrange("p (t q) -> p t q", t=6)
        sv = two["sv"].rearrange("p (b c) -> p b c", b=NB)
        mv = two["mv"].rearrange("p (b h d) -> p b h d", b=NB, h=HM)
        qT = two["qT"].rearrange("p (h q) -> p h q", h=HM)
        kT = two["kT"].rearrange("p (h q) -> p h q", h=HM)

        three = carve([("pp", NB * D), ("sg", NB * D), ("hid", NB * FF_CHUNK), ("silu", NB * FF_CHUNK), ("pT", 2 * SEQ)])
        pp = three["pp"].rearrange("p (b c) -> p b c", b=NB)
        sg = three["sg"].rearrange("p (b c) -> p b c", b=NB)
        hid2 = three["hid"].rearrange("p (b c) -> p b c", b=NB)
        silu2 = three["silu"].rearrange("p (b c) -> p b c", b=NB)
        pT = three["pT"].rearrange("p (t q) -> p t q", t=2)

        skew = nc.dram_tensor("skew", (HD, P * 3 * P), F32, kind="Internal").ap()

        landed = [sem(f"landed{i}") for i in range(RAW_SLOTS)]
        names = """used hi_done lo_done in_consts in_vec in_x in_rows in_rel in_gain in_lora in_p in_skew out_skew
        masks_done init_p silu_c csb_done relb_ps toep_done relb_done
        mod_evac mod_mid shift_done
        sumsq var_done rstd_done h_ready xs_mid xs_ready xT_ps xh_ready xl_ready
        sig_done glu_done tap_ready tap_added conv_first conv_step mean_ps cent_done sq_done var_ps deviation ln_scale ln_done
        silu_done yh_done yl_done
        pw2_ps res_step xprep
        w1_ps relu_done hid_done hidT_ps gh_done gl_done mlp_ps
        iqT_done ikd_done iw_done ikT_ps ikT_done isc_ps relu_i isc_step topk_step sel_done
        lora_sq lora_var lora_rstd cn_done kr_done cnT_ps
        dsa_evac q7_done kv_done sb_evac sv_evac
        rope_t rope_done kf_done qkT_ps qT_done kT_done
        m_sc m_max m_nm m_exp m_inv m_pT_ps m_pT m_o mix_m
        s_z s_abs s_e s_ln s_sp s_zs s_w s_o mix_s
        d_sc d_b d_s d_nm d_exp d_inv d_pT_ps d_pT d_o mix_d
        wo_ps gu_ps silu_g hid_g dn_ps ph_done pl_done proj_evac gate_ps sig_g gmul outs""".split()
        S = {n: sem(n) for n in names}

        block = ctx.enter_context(nc.Block())

        def product(eng, stage, n=0):
            eng.wait_ge(S["used"], last_of(stage, n)["index"] + 1)

        def block_product(eng, first, value, b, stage, n=0):
            if b == 0:
                eng.wait_ge(S[first], value)
            else:
                product(eng, stage, n)

        MOD_BANK = [0, 2, 0, 2, 0, 4]

        NORMS = 3 + 3 * LAYERS + 1
        LAST = NORMS - 1

        def nval(n, b):
            return 2 * n + b + 1

        def hval(n, b):
            return 2 * (n - 1) + b + 1

        def xsval(n, b):
            return 2 * (n if n < 2 else n - 1) + b + 1

        def tval(t, b):
            return 2 * t + b + 1

        def norm_of(t):
            return t if t < 2 else 3 + 3 * ((t - 2) // 4) + (0, None, 1, 2)[(t - 2) % 4]

        def before_T(t):
            if t == 0:
                return None
            if t == 1:
                return last_of("pw2")
            layer, k = (t - 2) // 4, (t - 2) % 4
            if k == 0:
                return last_of("w1", MLP_CHUNKS - 1) if layer == 0 else last_of(("gate", layer - 1))
            return (None, last_of(("sv", layer)), last_of(("wo", layer)), last_of(("gu", layer), FF_CHUNKS - 1))[k]

        GAIN_ROWS = ["norm1_g", "norm2_g", "final_g"] + [f"{k}{l}" for l in range(LAYERS) for k in ("attn", "ffn", "ple")] + ["final"]

        @block.sync
        def _(sp):
            def weights(units):
                for u in units:
                    if u["index"] >= RAW_SLOTS:
                        old = UNITS[u["index"] - RAW_SLOTS]
                        if old["split"]:
                            sp.wait_ge(S["lo_done"], old["s"] + 1)
                        else:
                            sp.wait_ge(S["used"], old["index"] + 1)
                    n = u["kts"] * u["cols"]
                    src = stream[u["offset"]:u["offset"] + P * n].rearrange("(p n) -> p n", p=P)
                    sp.dma_start(raw[:, u["slot"], 0:n], src).then_inc(landed[u["slot"]], 16)

            def row(dst, name, s, base=None):
                sp.dma_start(dst, rows[name].partition_broadcast(P)).then_inc(S[s], 16)

            def gain_row(n):
                if n >= 2:
                    sp.wait_ge(S["xs_ready"] if n - 2 != 2 else S["h_ready"],
                               xsval(n - 2, 1) if n - 2 != 2 else hval(3, 1))
                row(gain[:, n % 2, :], GAIN_ROWS[n], "in_gain")

            def lora_row(layer):
                if layer:
                    sp.wait_ge(S["cn_done"], 4 * layer)
                row(lora_gain[:], f"lora{layer}", "in_lora")

            sp.dma_start(vec, vectors).then_inc(S["in_vec"], 16)
            weights(UNITS[0:1])
            sp.dma_start(h[:], x.rearrange("(b p) d -> p b d", p=P)).then_inc(S["in_x"], 16)
            weights(UNITS[1:3])
            row(one["rowB"], "b_mod1", "in_rows")
            gain_row(0)
            weights(UNITS[3:5])
            row(one["rowA"], "b_mod0", "in_rows")
            sp.dma_start(table[:], consts[:, 0:C_HOT]).then_inc(S["in_consts"], 16)
            sp.dma_start(hot, consts[0:BUCKETS + 1, C_HOT:C_HOT + HOT]).then_inc(S["in_rel"], 16)
            sp.dma_start(rb, rel).then_inc(S["in_rel"], 16)
            first = units_of("pw1", 0)[0]["index"]
            weights(UNITS[5:first + 4])
            sp.wait_ge(S["toep_done"], 1)
            sp.dma_start(skew.rearrange("h (p d) -> p h d", p=P), toep).then_inc(S["out_skew"], 16)
            weights(UNITS[first + 4:first + 6])
            sp.wait_ge(S["out_skew"], 16)
            for slot, head in enumerate(ORDER5):
                src = skew[head, P - 1:P - 1 + P * (3 * P - 1)].rearrange("(p d) -> p d", p=P)[:, 0:2 * P]
                sp.dma_start(bias[:, slot, :], src).then_inc(S["in_skew"], 16)
            first += 6
            at = units_of(("mod", 2), 0)[0]["index"]
            weights(UNITS[first:at])
            gain_row(1)
            row(one["g1"], "b_mod2", "in_rows")
            row(one["g2"], "b_mod5", "in_rows")
            row(one["bpw2"], "b_pw2", "in_rows")
            sp.wait_ge(S["xs_ready"], xsval(0, 1))
            row(one["rowB"], "b_mod4", "in_rows")
            row(one["rowA"], "b_mod3", "in_rows")
            end = units_of("w1", 1)[0]["index"]
            weights(UNITS[at:end])
            gain_row(2)
            at, end = end, units_of(("idx", 0))[0]["index"]
            weights(UNITS[at:end])
            for layer in range(LAYERS):
                n = 3 + 3 * layer
                gain_row(n)
                lora_row(layer)
                at, end = end, units_of(("wo", layer))[0]["index"]
                weights(UNITS[at:end])
                gain_row(n + 1)
                at, end = end, units_of(("gu", layer), 2)[0]["index"]
                weights(UNITS[at:end])
                gain_row(n + 2)
                sp.wait_ge(S["mix_d"], 2 * layer + 2)
                sp.dma_start(pT, p_t[layer].rearrange("(t p) q -> p t q", p=P)).then_inc(S["in_p"], 16)
                at = end
                end = units_of(("idx", layer + 1))[0]["index"] if layer + 1 < LAYERS else len(UNITS)
                weights(UNITS[at:end])
            gain_row(LAST)
            for b in range(NB):
                sp.wait_ge(S["xs_ready"], xsval(LAST, b))
                sp.dma_start(out[b * P:(b + 1) * P, :], xs[:, b, :]).then_inc(S["outs"], 16)
            sp.wait_ge(S["outs"], 32)

        @block.scalar
        def _(act):
            fed = [0]

            def feed(unit, ahead=LOOKAHEAD):
                while fed[0] < min(unit["s"] + 1 + ahead, len(SPLIT)):
                    u = SPLIT[fed[0]]
                    act.wait_ge(landed[u["slot"]], u["landed"])
                    if u["s"] >= SPLIT_SLOTS:
                        act.wait_ge(S["used"], SPLIT[u["s"] - SPLIT_SLOTS]["index"] + 1)
                    n = u["kts"] * u["cols"]
                    nc.scalar.activation(hi[:, u["s"] % SPLIT_SLOTS, 0:n], raw[:, u["slot"], 0:n],
                                         ACT.Copy).then_inc(S["hi_done"], 1)
                    fed[0] += 1

            def squares(n):
                for b in range(NB):
                    if n:
                        act.wait_ge(S["h_ready"], hval(n, b))
                    else:
                        act.wait_ge(S["in_x"], 16)
                        act.wait_ge(S["init_p"], 2)
                    k = 2 * (n % 2) + b
                    nc.scalar.activation(xs[:, b, :], h[:, b, :], ACT.Square,
                                         accum_out=ss[:, k:k + 1]).then_inc(S["sumsq"], 1)

            def high_T(t):
                if before_T(t):
                    act.wait_ge(S["used"], before_T(t)["index"] + 1)
                for b in range(NB):
                    bank = 4 + 2 * b
                    act.wait_ge(S["xT_ps"], tval(t, b))
                    nc.scalar.activation(xh[:, :, b * P:(b + 1) * P],
                                         ps[:, bank:bank + 2, :].rearrange("p a (k m) -> p (a k) m", k=4),
                                         ACT.Copy).then_inc(S["xh_ready"], 1)

            act.wait_ge(S["in_vec"], 16)
            nc.scalar.activation(vec[:, V_C:V_C + KT], vec[:, V_C:V_C + KT], ACT.Silu).then_inc(S["silu_c"], 1)
            squares(0)
            feed(units_of("pw1", 0)[0], 1)
            high_T(0)
            act.wait_ge(S["relb_ps"], 1)
            nc.scalar.activation(toep.rearrange("p h d -> p (h d)"),
                                 ps[:, 0:4, :].rearrange("p a c -> p (a c)")[:, 0:HD * HOT], ACT.Copy).then_inc(S["toep_done"], 1)

            def tap_products(p, k0, k1):
                pair = POOL_PAIRS[p]
                act.wait_ge(S["glu_done"], pair[1] + 1)
                if p == 0:
                    act.wait_ge(S["out_skew"], 16)
                for k in range(k0, k1):
                    made = (TAPS - 1) * p + k - 1
                    if k and made >= PRODUCTS:
                        act.wait_ge(S["tap_added"], made - PRODUCTS + 1)
                    for i, f in enumerate(pair):
                        src = upad[:, f, :, k:k + SEG]
                        dst = taps[:, made % PRODUCTS, i, :] if k else cv[:, f, :]
                        bias_ = vec[:, V_BDW + f:V_BDW + f + 1] if k == 0 else 0.0
                        ins = nc.scalar.activation(dst.rearrange("p (s t) -> p s t", s=SEGS), src, ACT.Identity,
                                                   scale=dw[:, f, k:k + 1], bias=bias_)
                        ins.then_inc(S["tap_ready"] if k else S["conv_first"], 1)

            done = 0
            for f in range(KT):
                feed(units_of("pw1", f)[0], min(LOOKAHEAD, KT - 1 - f))
                product(act, "pw1", f)
                if f >= GATES:
                    act.wait_ge(S["glu_done"], f - GATES + 1)
                nc.scalar.activation(sig[:, f % GATES, :], ps[:, 4 + f % 4, SEQ:2 * SEQ], ACT.Sigmoid,
                                     bias=vec[:, V_BPW1 + KT + f:V_BPW1 + KT + f + 1]).then_inc(S["sig_done"], 1)
                if f > POOL_PAIRS[0][1]:
                    tap_products(0, done, done + 3)
                    done += 3
            tap_products(0, done, TAPS)
            tap_products(1, 0, TAPS)
            for i in range(2):
                act.wait_ge(S["cent_done"], i + 1)
                half = slice(i * KT // 2, (i + 1) * KT // 2)
                nc.scalar.activation(sq[:, half, :], cv[:, half, :], ACT.Square).then_inc(S["sq_done"], 1)
            feed(units_of("pw2")[0], 0)
            act.wait_ge(S["var_ps"], 1)
            nc.scalar.activation(one["rs"], ps[:, 7, 0:SEQ], ACT.Sqrt, bias=epsilon[:]).then_inc(S["deviation"], 1)
            feed(units_of("pw2")[0], 1)
            act.wait_ge(S["used"], last_of("pw1", KT - 1)["index"] + 1)
            for i in range(KT // 2):
                act.wait_ge(S["ln_done"], i + 1)
                for f in (2 * i, 2 * i + 1):
                    nc.scalar.activation(sq[:, f, :], cv[:, f, :], ACT.Silu, scale=vec[:, V_LNG + f:V_LNG + f + 1],
                                         bias=vec[:, V_LNB + f:V_LNB + f + 1]).then_inc(S["silu_done"], 1)
                act.wait_ge(S["silu_done"], 2 * (i + 1))
                pair = slice(2 * i, 2 * i + 2)
                nc.scalar.activation(xh[:, pair, :], sq[:, pair, :], ACT.Copy).then_inc(S["yh_done"], 1)
            feed(last_of("pw2"))
            squares(1)
            feed(units_of("w1", 0)[0])
            high_T(1)
            for j in range(MLP_CHUNKS):
                feed(last_of("w1", j))
                for b in range(NB):
                    block_product(act, "w1_ps", j + 1, b, "w1", j)
                    if j:
                        act.wait_ge(S["hidT_ps"], 2 * (j - 1) + b + 1)
                    nc.scalar.activation(hid1[:, b, :], ps[:, 4 + b, :], ACT.Relu).then_inc(S["relu_done"], 1)
                    act.wait_ge(S["relu_done"], 2 * j + b + 1)
                    nc.scalar.activation(hid1[:, b, :], hid1[:, b, :], ACT.Square).then_inc(S["hid_done"], 1)
                if j:
                    feed(last_of("w2", j - 1))
                    act.wait_ge(S["used"], last_of("w2", j - 1)["index"] + 1)
                for b in range(NB):
                    act.wait_ge(S["hidT_ps"], 2 * j + b + 1)
                    nc.scalar.activation(gh[:, 0:4, b * P:(b + 1) * P], ps[:, 6 + b, :].rearrange("p (k m) -> p k m", k=4),
                                         ACT.Copy).then_inc(S["gh_done"], 1)
            feed(last_of("w2", MLP_CHUNKS - 1))
            squares(2)

            ghv = 2 * MLP_CHUNKS
            for layer in range(LAYERS):
                n, t = 3 + 3 * layer, 2 + 4 * layer
                squares(n)
                feed(units_of(("idx", layer))[0])
                high_T(t)
                feed(last_of(("idx", layer)))
                product(act, ("idx", layer))
                nc.scalar.activation(iqT, ps[:, 4:6, :].rearrange("p a (t q) -> p (a t) q", t=2),
                                     ACT.Copy).then_inc(S["iqT_done"], 1)
                feed(last_of(("mla", layer)))
                product(act, ("mla", layer))
                for b in range(NB):
                    nc.scalar.activation(cn[:, b, 0:QL], ps[:, 2 * b, 0:QL], ACT.Square,
                                         accum_out=lss[:, b, 0:1]).then_inc(S["lora_sq"], 1)
                    nc.scalar.activation(cn[:, b, QL:QL + KVL], ps[:, 2 * b + 1, 0:KVL], ACT.Square,
                                         accum_out=lss[:, b, 1:2]).then_inc(S["lora_sq"], 1)
                for b in range(NB):
                    nc.scalar.activation(q7[:, b, HM, NOPE:QK], ps[:, 2 * b + 1, KVL:KVL + ROPE],
                                         ACT.Copy).then_inc(S["kr_done"], 1)
                act.wait_ge(S["ikT_ps"], layer + 1)
                nc.scalar.activation(ikT, ps[:, 6, 0:SEQ], ACT.Copy).then_inc(S["ikT_done"], 1)
                act.wait_ge(S["isc_ps"], 2 * layer + 1)
                nc.scalar.activation(relu1, ps[:, 4:8, :].rearrange("p a (t q) -> p (a t) q", t=2), ACT.Relu,
                                     scale=DH ** -0.5).then_inc(S["relu_i"], 1)
                act.wait_ge(S["cnT_ps"], layer + 1)
                last_g = last_of("w2", MLP_CHUNKS - 1) if layer == 0 else last_of(("proj", layer - 1))
                act.wait_ge(S["used"], last_g["index"] + 1)
                nc.scalar.activation(gh[:].rearrange("p k m -> p (k m)"), ps[:, 0:3, :].rearrange("p a c -> p (a c)")[:, 0:5 * SEQ],
                                     ACT.Copy).then_inc(S["gh_done"], 1)
                ghv += 1
                act.wait_ge(S["isc_ps"], 2 * layer + 2)
                nc.scalar.activation(relu0, ps[:, 4:6, :].rearrange("p a (t q) -> p (a t) q", t=4), ACT.Relu,
                                     scale=DH ** -0.5).then_inc(S["relu_i"], 1)
                feed(last_of(("dsa", layer)))
                product(act, ("dsa", layer))
                nc.scalar.activation(dT[:, 0:2, :], ps[:, 6, :].rearrange("p (t q) -> p t q", t=2),
                                     ACT.Copy).then_inc(S["dsa_evac"], 1)
                nc.scalar.activation(dT[0:DH, 2, :], ps[0:DH, 7, 0:SEQ], ACT.Copy).then_inc(S["dsa_evac"], 1)
                nc.scalar.activation(dkT[DH:P, :], ps[DH:P, 7, 0:SEQ], ACT.Copy).then_inc(S["dsa_evac"], 1)
                nc.scalar.activation(dkT[0:DH, :], ps[DH:P, 7, 0:SEQ], ACT.Copy).then_inc(S["dsa_evac"], 1)
                nc.scalar.activation(dv, ps[:, 7, SEQ:SEQ + 2 * DH].rearrange("p (b d) -> p b d", b=NB),
                                     ACT.Copy).then_inc(S["dsa_evac"], 1)
                feed(last_of(("uq", layer)))
                product(act, ("uq", layer))
                for b in range(NB):
                    nc.scalar.activation(q7[:, b, 0:HM, :].rearrange("p h d -> p (h d)").rearrange("p (a c) -> p a c", a=2),
                                         ps[:, 2 * b:2 * b + 2, 0:UQ_COLS // 2], ACT.Copy).then_inc(S["q7_done"], 1)
                feed(last_of(("sb", layer)))
                act.wait_ge(S["rope_done"], 2 * layer + 2)
                act.wait_ge(S["kv_done"], 4 * layer + 4)
                for b in range(NB):
                    nc.scalar.activation(kfull[:, b, :, NOPE:QK], q7[:, b, HM:HM + 1, NOPE:QK].broadcast_to([P, HM, ROPE]),
                                         ACT.Copy).then_inc(S["kf_done"], 1)
                product(act, ("sb", layer))
                nc.scalar.activation(sT[:, 0:2, :], ps[:, 0, :].rearrange("p (t q) -> p t q", t=2), ACT.Copy,
                                     scale=DH ** -0.5).then_inc(S["sb_evac"], 1)
                nc.scalar.activation(sT[:, 2:4, :], ps[:, 1, :].rearrange("p (t q) -> p t q", t=2),
                                     ACT.Copy).then_inc(S["sb_evac"], 1)
                nc.scalar.activation(sT[0:DH, 4, :], ps[0:DH, 2, 0:SEQ], ACT.Copy, scale=DH ** -0.5).then_inc(S["sb_evac"], 1)
                nc.scalar.activation(sT[0:DH, 5, :], ps[DH:P, 2, 0:SEQ], ACT.Copy).then_inc(S["sb_evac"], 1)
                feed(last_of(("sv", layer)))
                act.wait_ge(S["qkT_ps"], 2 * layer + 1)
                nc.scalar.activation(qT[0:QK].rearrange("p h q -> p (h q)"), ps[0:QK, 5:8, :].rearrange("p a c -> p (a c)"),
                                     ACT.Copy).then_inc(S["qT_done"], 1)
                for i, b in enumerate((1, 0)):
                    act.wait_ge(S["m_nm"], 2 * layer + i + 1)
                    for hh in range(HM):
                        src = (ps[:, 5:8, :].rearrange("p a (t k) -> p (a t) k", t=2)[:, hh, :] if b else
                               ps[:, 3:5, :].rearrange("p a (t k) -> p (a t) k", t=4)[:, hh, :])
                        k = HM * b + hh
                        nc.scalar.activation(pm[b][:, hh, :], src, ACT.Exp, scale=QK ** -0.5, bias=neg_max[:, k:k + 1],
                                             accum_out=row_sum[:, k:k + 1]).then_inc(S["m_exp"], 1)
                act.wait_ge(S["m_pT_ps"], 2 * layer + 1)
                nc.scalar.activation(pmT[1], ps[:, 5:8, :].rearrange("p a c -> p (a c)"), ACT.Copy).then_inc(S["m_pT"], 1)
                act.wait_ge(S["s_z"], layer + 1)
                zps = ps[:, 0:5, 0:3 * P]
                act.wait_ge(S["qkT_ps"], 2 * layer + 2)
                nc.scalar.activation(sbt, zps, ACT.Abs).then_inc(S["s_abs"], 1)
                act.wait_ge(S["s_abs"], layer + 1)
                nc.scalar.activation(sbt, sbt, ACT.Exp, scale=-1.0).then_inc(S["s_e"], 1)
                act.wait_ge(S["s_e"], layer + 1)
                nc.scalar.activation(sbt, sbt, ACT.Ln, bias=1.0).then_inc(S["s_ln"], 1)
                act.wait_ge(S["s_zs"], layer + 1)
                nc.scalar.activation(sbt, zps, ACT.Exp).then_inc(S["s_w"], 1)
                feed(last_of(("wo", layer)), ahead=-1)
                for i, b in enumerate((1, 0)):
                    act.wait_ge(S["d_nm"], 2 * layer + i + 1)
                    for k in range(HD):
                        c, head = HD * b + k, HD * b + ORDER5[k]
                        nc.scalar.activation(pd[b][:, k, :], pd[b][:, k, :], ACT.Exp, bias=neg_max[:, c:c + 1],
                                             accum_out=row_sum[:, head:head + 1]).then_inc(S["d_exp"], 1)
                act.wait_ge(S["d_pT_ps"], 2 * layer + 1)
                nc.scalar.activation(pdT[1], ps[:, 0:3, :].rearrange("p a c -> p (a c)")[:, 0:2 * HD * P],
                                     ACT.Copy).then_inc(S["d_pT"], 1)
                high_T(t + 1)
                feed(last_of(("wo", layer)))
                squares(n + 1)
                high_T(t + 2)
                for j in range(FF_CHUNKS):
                    feed(last_of(("gu", layer), j))
                    for b in range(NB):
                        k = FF_CHUNKS * layer + j
                        block_product(act, "gu_ps", k + 1, b, ("gu", layer), j)
                        if k:
                            act.wait_ge(S["hid_g"], 2 * (k - 1) + b + 1)
                        nc.scalar.activation(silu2[:, b, :], ps[:, 4 + b, 0:FF_CHUNK], ACT.Silu).then_inc(S["silu_g"], 1)
                    if j:
                        feed(last_of(("dn", layer), j - 1))
                        act.wait_ge(S["used"], last_of(("dn", layer), j - 1)["index"] + 1)
                    else:
                        act.wait_ge(S["used"], last_of(("ukv", layer))["index"] + 1)
                    for b in range(NB):
                        act.wait_ge(S["hidT_ps"], 2 * (MLP_CHUNKS + FF_CHUNKS * layer + j) + b + 1)
                        nc.scalar.activation(gh[:, 0:2, b * P:(b + 1) * P],
                                             ps[:, 6 + b, 0:2 * P].rearrange("p (k m) -> p k m", k=2),
                                             ACT.Copy).then_inc(S["gh_done"], 1)
                feed(last_of(("dn", layer), FF_CHUNKS - 1))
                act.wait_ge(S["in_p"], 16 * (layer + 1))
                act.wait_ge(S["used"], last_of(("dn", layer), FF_CHUNKS - 1)["index"] + 1)
                nc.scalar.activation(gh[:, 0:2, :], pT, ACT.Copy).then_inc(S["ph_done"], 1)
                squares(n + 2)
                product(act, ("proj", layer))
                for b in range(NB):
                    nc.scalar.activation(pp[:, b, :], ps[:, 2 * b:2 * b + 2, :].rearrange("p a c -> p (a c)"),
                                         ACT.Copy).then_inc(S["proj_evac"], 1)
                high_T(t + 3)
                feed(last_of(("gate", layer)))
                for b in range(NB):
                    block_product(act, "gate_ps", layer + 1, b, ("gate", layer))
                    nc.scalar.activation(sg[:, b, :], ps[:, 2 * b:2 * b + 2, :].rearrange("p a c -> p (a c)"),
                                         ACT.Sigmoid).then_inc(S["sig_g"], 1)
            squares(LAST)

        @block.gpsimd
        def _(pool):
            nc.gpsimd.memset(pow_half[:], -0.5).then_inc(S["init_p"], 1)
            nc.gpsimd.memset(neg_ones[:], -1.0).then_inc(S["init_p"], 1)
            nc.gpsimd.memset(one["ones"], 1.0 / D).then_inc(S["init_p"], 1)
            nc.gpsimd.memset(epsilon[:], EPS).then_inc(S["init_p"], 1)
            nc.gpsimd.memset(upad, 0.0).then_inc(S["init_p"], 1)
            pool.wait_ge(S["init_p"], 5)

            def rstds(n):
                for b in range(NB):
                    k = 2 * (n % 2) + b
                    pool.wait_ge(S["sumsq"], nval(n, b))
                    nc.gpsimd.tensor_scalar(var[:, k:k + 1], ss[:, k:k + 1], 1.0 / D, EPS, ALU.mult,
                                            ALU.add).then_inc(S["var_done"], 1)
                    pool.wait_ge(S["var_done"], nval(n, b))
                    nc.gpsimd.tensor_tensor(rstd[:, k:k + 1], var[:, k:k + 1], pow_half[:, 0:1],
                                            ALU.pow).then_inc(S["rstd_done"], 1)

            rstds(0)
            for p, (f, _) in enumerate(POOL_PAIRS):
                pool.wait_ge(S["conv_first"], 2 * (p + 1))
                for k in range(1, TAPS):
                    made = (TAPS - 1) * p + k - 1
                    pool.wait_ge(S["tap_ready"], 2 * (made + 1))
                    if k > 1:
                        pool.wait_ge(S["tap_added"], made)
                    nc.gpsimd.tensor_tensor(cv[:, f:f + 2, :], cv[:, f:f + 2, :], taps[:, made % PRODUCTS],
                                            ALU.add).then_inc(S["tap_added"], 1)
            rstds(1)
            rstds(2)
            for layer in range(LAYERS):
                n = 3 + 3 * layer
                rstds(n)
                pool.wait_ge(S["lora_sq"], 4 * layer + 4)
                nc.gpsimd.tensor_scalar(lvar[:, :, 0], lss[:, :, 0], 1.0 / QL, EPS, ALU.mult, ALU.add).then_inc(S["lora_var"], 1)
                nc.gpsimd.tensor_scalar(lvar[:, :, 1], lss[:, :, 1], 1.0 / KVL, EPS, ALU.mult, ALU.add).then_inc(S["lora_var"], 1)
                pool.wait_ge(S["lora_var"], 2 * layer + 2)
                nc.gpsimd.tensor_tensor(lrstd[:].rearrange("p b c -> p (b c)"), lvar[:].rearrange("p b c -> p (b c)"),
                                        pow_half[:], ALU.pow).then_inc(S["lora_rstd"], 1)
                rstds(n + 1)
                rstds(n + 2)
            rstds(LAST)

        @block.vector
        def _(dve):
            fed = [0]

            def feed(unit, ahead=LOOKAHEAD):
                while fed[0] < min(unit["s"] + 1 + ahead, len(SPLIT)):
                    u = SPLIT[fed[0]]
                    n = u["kts"] * u["cols"]
                    slot = u["s"] % SPLIT_SLOTS
                    dve.wait_ge(S["hi_done"], u["s"] + 1)
                    nc.vector.tensor_tensor(lo[:, slot, 0:n], raw[:, u["slot"], 0:n], hi[:, slot, 0:n].bitcast(F32),
                                            ALU.subtract).then_inc(S["lo_done"], 1)
                    fed[0] += 1

            def normalise(n):
                for b in range(NB):
                    k = 2 * (n % 2) + b
                    if b == 0:
                        dve.wait_ge(S["in_gain"], 16 * (n + 1))
                    dve.wait_ge(S["rstd_done"], nval(n, b))
                    dst = h if n == 2 else xs
                    i = nc.vector.scalar_tensor_tensor(out=dst[:, b, :], in0=h[:, b, :], scalar=rstd[:, k:k + 1],
                                                       in1=gain[:, n % 2, :], op0=ALU.mult, op1=ALU.mult)
                    if n == 1:
                        i.then_inc(S["xs_mid"], 1)
                        dve.wait_ge(S["xs_mid"], b + 1)
                        i = nc.vector.tensor_tensor(xs[:, b, :], xs[:, b, :], one["rowA"], ALU.add)
                    i.then_inc(S["h_ready"] if n == 2 else S["xs_ready"], 1)

            def low_T(t):
                for b in range(NB):
                    bank = 4 + 2 * b
                    dve.wait_ge(S["xh_ready"], tval(t, b))
                    sl = slice(b * P, (b + 1) * P)
                    nc.vector.tensor_tensor(xl[:, :, sl], ps[:, bank:bank + 2, :].rearrange("p a (k m) -> p (a k) m", k=4),
                                            xh[:, :, sl].bitcast(F32), ALU.subtract).then_inc(S["xl_ready"], 1)

            def mod_row(v):
                bank = MOD_BANK[v]
                src = ps[:, bank:bank + 2, :].rearrange("p a c -> p (a c)")
                dst = [one["rowB"], None, one["g1"], one["rowA"], one["rowB"], one["g2"]][v]
                dve.wait_ge(S["in_rows"], 16 if v == 0 else 16 * 7)
                product(dve, ("mod", v), 3)
                nc.vector.tensor_tensor(dst, src, dst, ALU.add).then_inc(S["mod_evac"], 1)
                if v in (0, 4):
                    n = 0 if v == 0 else 1
                    dve.wait_ge(S["mod_evac"], 1 if v == 0 else 4)
                    dve.wait_ge(S["in_gain"], 16 * (n + 1))
                    nc.vector.scalar_tensor_tensor(out=gain[:, n, :], in0=dst, scalar=1.0, in1=gain[:, n, :], op0=ALU.add,
                                                   op1=ALU.mult).then_inc(S["mod_mid"], 1)
                    dve.wait_ge(S["mod_mid"], n + 1)

            dve.wait_ge(S["silu_c"], 1)
            nc.vector.tensor_copy(csb, vec[:, V_C:V_C + KT].rearrange("p (k a) -> p k a", a=1).broadcast_to([P, KT, P]))\
                .then_inc(S["csb_done"], 1)
            dve.wait_ge(S["in_consts"], 16)
            for dst, c in ((ident16[:], C_ID), (masks16[:, 0, :], C_CAUSAL), (masks16[:, 1, :], C_STRICT)):
                nc.vector.tensor_copy(dst, table[:, c:c + P]).then_inc(S["masks_done"], 1)
            dve.wait_ge(S["in_rel"], 32)
            nc.vector.tensor_copy(rbb, rb.rearrange("p (h a) -> p h a", a=1).broadcast_to([BUCKETS + 1, HD, P]))\
                .then_inc(S["relb_done"], 1)
            mod_row(0)
            for b in range(NB):
                dve.wait_ge(S["rstd_done"], nval(0, b))
                nc.vector.scalar_tensor_tensor(out=xs[:, b, :], in0=h[:, b, :], scalar=rstd[:, b:b + 1],
                                               in1=gain[:, 0, :], op0=ALU.mult, op1=ALU.mult).then_inc(S["shift_done"], 1)
            dve.wait_ge(S["in_rows"], 32)
            for b in range(NB):
                dve.wait_ge(S["shift_done"], b + 1)
                nc.vector.tensor_tensor(xs[:, b, :], xs[:, b, :], one["rowA"], ALU.add).then_inc(S["shift_done"], 1)
            feed(units_of("pw1", 0)[0], 1)
            product(dve, ("mod", 1), 3)
            for b in range(NB):
                dve.wait_ge(S["shift_done"], NB + b + 1)
                src = ps[:, MOD_BANK[1]:MOD_BANK[1] + 2, :].rearrange("p a c -> p (a c)")
                nc.vector.tensor_tensor(xs[:, b, :], xs[:, b, :], src, ALU.add).then_inc(S["xs_ready"], 1)
            low_T(0)

            def gate_values(f):
                feed(units_of("pw1", f)[0], min(LOOKAHEAD, KT - 1 - f))
                dve.wait_ge(S["sig_done"], f + 1)
                nc.vector.scalar_tensor_tensor(out=upad[:, f, :, HALO:HALO + SEG],
                                               in0=ps[:, 4 + f % 4, 0:SEQ].rearrange("p (s t) -> p s t", s=SEGS),
                                               scalar=vec[:, V_BPW1 + f:V_BPW1 + f + 1],
                                               in1=sig[:, f % GATES, :].rearrange("p (s t) -> p s t", s=SEGS),
                                               op0=ALU.add, op1=ALU.mult).then_inc(S["glu_done"], 1)

            steps = [0]

            def convolve(p, k0, k1):
                for k in range(k0, k1):
                    for f in DVE_PAIRS[p]:
                        acc = cv[:, f, :].rearrange("p (s t) -> p s t", s=SEGS)
                        src = upad[:, f, :, k:k + SEG]
                        if k == 0:
                            dve.wait_ge(S["glu_done"], f + 1)
                            ins = nc.vector.tensor_scalar(acc, src, dw[:, f, 0:1], vec[:, V_BDW + f:V_BDW + f + 1],
                                                          ALU.mult, ALU.add)
                        else:
                            dve.wait_ge(S["conv_step"], steps[0] - 1)
                            ins = nc.vector.scalar_tensor_tensor(out=acc, in0=src, scalar=dw[:, f, k:k + 1], in1=acc,
                                                                 op0=ALU.mult, op1=ALU.add)
                        ins.then_inc(S["conv_step"], 1)
                        steps[0] += 1

            for f in range(DVE_PAIRS[0][1]):
                gate_values(f)
            done = 0
            for f in range(DVE_PAIRS[0][1], KT):
                gate_values(f)
                if f < KT - 1:
                    convolve(0, done, done + 3)
                    done += 3
            convolve(0, done, TAPS)
            mod_row(2)
            dve.wait_ge(S["mod_evac"], 2)
            nc.vector.tensor_tensor(one["bpw2"], one["bpw2"], one["g1"], ALU.mult).then_inc(S["xprep"], 1)
            dve.wait_ge(S["xprep"], 1)
            for b in range(NB):
                nc.vector.tensor_tensor(h[:, b, :], h[:, b, :], one["bpw2"], ALU.add).then_inc(S["xprep"], 1)
            convolve(1, 0, TAPS // 2)
            mod_row(3)
            convolve(1, TAPS // 2, TAPS)
            mod_row(4)
            dve.wait_ge(S["mean_ps"], 1)
            for i in range(2):
                half = cv[:, i * KT // 2:(i + 1) * KT // 2, :]
                mean = ps[:, 6, 0:SEQ].rearrange("p (a t) -> p a t", a=1).broadcast_to([P, KT // 2, SEQ])
                nc.vector.tensor_tensor(half, half, mean, ALU.subtract).then_inc(S["cent_done"], 1)
            feed(units_of("pw2")[0], 0)
            dve.wait_ge(S["deviation"], 1)
            nc.vector.reciprocal(one["rs"], one["rs"]).then_inc(S["ln_scale"], 1)
            dve.wait_ge(S["ln_scale"], 1)

            def low_silu(i):
                pair = slice(2 * i, 2 * i + 2)
                dve.wait_ge(S["yh_done"], i + 1)
                nc.vector.tensor_tensor(xl[:, pair, :], sq[:, pair, :], xh[:, pair, :].bitcast(F32),
                                        ALU.subtract).then_inc(S["yl_done"], 1)

            for i in range(KT // 2):
                pair = cv[:, 2 * i:2 * i + 2, :]
                nc.vector.tensor_tensor(pair, pair, one["rs"].rearrange("p (a t) -> p a t", a=1).broadcast_to([P, 2, SEQ]),
                                        ALU.mult).then_inc(S["ln_done"], 1)
                if i:
                    low_silu(i - 1)
            low_silu(KT // 2 - 1)
            mod_row(5)
            feed(last_of("pw2"))

            rstep = [0]

            def residual(done, value, stage, index, scale_row):
                for b in range(NB):
                    block_product(dve, done, value, b, stage, index)
                    src = ps[:, 2 * b:2 * b + 2, :].rearrange("p a c -> p (a c)")
                    if scale_row is None:
                        nc.vector.tensor_tensor(h[:, b, :], src, h[:, b, :], ALU.add).then_inc(S["h_ready"], 1)
                    else:
                        nc.vector.tensor_tensor(xs[:, b, :], src, scale_row, ALU.mult).then_inc(S["res_step"], 1)
                        rstep[0] += 1
                        dve.wait_ge(S["res_step"], rstep[0])
                        nc.vector.tensor_tensor(h[:, b, :], xs[:, b, :], h[:, b, :], ALU.add).then_inc(S["h_ready"], 1)

            dve.wait_ge(S["xprep"], 3)
            residual("pw2_ps", 1, "pw2", 0, one["g1"])
            normalise(1)
            feed(last_of("w1", 0), 0)
            low_T(1)
            for j in range(MLP_CHUNKS):
                feed(last_of("w1", j))
                if j:
                    feed(last_of("w2", j - 1))
                for b in range(NB):
                    sl = slice(b * P, (b + 1) * P)
                    dve.wait_ge(S["gh_done"], 2 * j + b + 1)
                    nc.vector.tensor_tensor(gl[:, 0:4, sl], ps[:, 6 + b, :].rearrange("p (k m) -> p k m", k=4),
                                            gh[:, 0:4, sl].bitcast(F32), ALU.subtract).then_inc(S["gl_done"], 1)
            feed(last_of("w2", MLP_CHUNKS - 1))
            residual("mlp_ps", 1, "w2", MLP_CHUNKS - 1, one["g2"])
            normalise(2)

            for layer in range(LAYERS):
                n, t = 3 + 3 * layer, 2 + 4 * layer
                ghv = 2 * MLP_CHUNKS + (1 + 2 * FF_CHUNKS) * layer
                normalise(n)
                feed(last_of(("idx", layer)), -2)
                low_T(t)
                feed(last_of(("idx", layer)))
                product(dve, ("idx", layer))
                for c in range(2):
                    nc.vector.tensor_copy(ikd[:, :, c * DH:(c + 1) * DH], ps[:, 6:8, 0:DH]).then_inc(S["ikd_done"], 1)
                nc.vector.tensor_scalar(iw[:], ps[:, 6:8, DH:DH + HI], HI ** -0.5, None, ALU.mult).then_inc(S["iw_done"], 1)
                feed(last_of(("mla", layer)))
                dve.wait_ge(S["lora_rstd"], layer + 1)
                dve.wait_ge(S["in_lora"], 16 * (layer + 1))
                dve.wait_ge(S["kr_done"], 2 * layer + 2)
                for b in range(NB):
                    for c, (a, z) in enumerate(((0, QL), (QL, QL + KVL))):
                        nc.vector.scalar_tensor_tensor(out=cn[:, b, a:z], in0=ps[:, 2 * b + c, 0:z - a],
                                                       scalar=lrstd[:, b, c:c + 1], in1=lora_gain[:, a:z],
                                                       op0=ALU.mult, op1=ALU.mult).then_inc(S["cn_done"], 1)

                istep = [16 * layer]
                tstep = [2 * layer * (2 * TOPK // 8)]

                def index_scores(b):
                    r, order = ((relu1, ORDER8) if b else (relu0, ORDER8_B0))
                    dve.wait_ge(S["relu_i"], 2 * layer + (1 if b else 2))
                    if b:
                        dve.wait_ge(S["iw_done"], layer + 1)
                    for k in range(HI):
                        if k:
                            dve.wait_ge(S["isc_step"], istep[0])
                        head = order[k]
                        in1 = work[b] if k else (cmask if b else cmask[:, P:])
                        nc.vector.scalar_tensor_tensor(out=work[b], in0=r[:, k, :], scalar=iw[:, b, head:head + 1],
                                                       in1=in1, op0=ALU.mult, op1=ALU.add).then_inc(S["isc_step"], 1)
                        istep[0] += 1
                    dve.wait_ge(S["isc_step"], istep[0])

                def top_keys(b):
                    for r in range(TOPK // 8):
                        nc.vector.max(top8[:], work[b]).then_inc(S["topk_step"], 1)
                        tstep[0] += 1
                        dve.wait_ge(S["topk_step"], tstep[0])
                        nc.vector.match_replace(work[b], top8[:], work[b], TAKEN).then_inc(S["topk_step"], 1)
                        tstep[0] += 1
                        dve.wait_ge(S["topk_step"], tstep[0])
                    nc.vector.tensor_scalar(work[b], work[b], 0.5 * TAKEN, NEG, ALU.is_gt, ALU.mult).then_inc(S["sel_done"], 1)

                index_scores(1)
                feed(last_of(("dsa", layer)))
                dve.wait_ge(S["gh_done"], ghv + 1)
                nc.vector.tensor_tensor(gl[:].rearrange("p k m -> p (k m)"),
                                        ps[:, 0:3, :].rearrange("p a c -> p (a c)")[:, 0:5 * SEQ],
                                        gh[:].rearrange("p k m -> p (k m)").bitcast(F32), ALU.subtract).then_inc(S["gl_done"], 1)
                index_scores(0)
                feed(last_of(("uq", layer)))
                top_keys(1)
                feed(last_of(("ukv", layer)))
                product(dve, ("ukv", layer))
                for b in range(NB):
                    src = ps[:, 4 + 2 * b:6 + 2 * b, 0:UKV_COLS // 2].rearrange("p a (h d) -> p a h d", h=3)
                    nc.vector.tensor_copy(mv[:, b, :, :].rearrange("p (a h) d -> p a h d", a=2),
                                          src[:, :, :, NOPE:NOPE + VD]).then_inc(S["kv_done"], 1)
                    nc.vector.tensor_copy(kfull[:, b, :, 0:NOPE].rearrange("p (a h) d -> p a h d", a=2),
                                          src[:, :, :, 0:NOPE]).then_inc(S["kv_done"], 1)
                feed(last_of(("sb", layer)))
                dve.wait_ge(S["q7_done"], 2 * layer + 2)
                dve.wait_ge(S["kr_done"], 2 * layer + 2)
                x1 = q7[:, :, :, NOPE:NOPE + HALF]
                x2 = q7[:, :, :, NOPE + HALF:QK]
                co = cosines.rearrange("p b (a d) -> p b a d", a=1).broadcast_to([P, NB, 7, HALF])
                si = sines.rearrange("p b (a d) -> p b a d", a=1).broadcast_to([P, NB, 7, HALF])
                for i, (xx, cs) in enumerate(((x1, co), (x2, si), (x1, si), (x2, co))):
                    nc.vector.tensor_tensor(rt[:, i], xx, cs, ALU.mult).then_inc(S["rope_t"], 1)
                dve.wait_ge(S["rope_t"], 4 * layer + 4)
                nc.vector.tensor_tensor(x1, rt[:, 0], rt[:, 1], ALU.subtract).then_inc(S["rope_done"], 1)
                nc.vector.tensor_tensor(x2, rt[:, 2], rt[:, 3], ALU.add).then_inc(S["rope_done"], 1)
                top_keys(0)
                feed(last_of(("sv", layer)))
                product(dve, ("sv", layer))
                for b in range(NB):
                    nc.vector.tensor_copy(sv[:, b, :], ps[:, 3 + b, 0:SV_COLS]).then_inc(S["sv_evac"], 1)
                dve.wait_ge(S["qkT_ps"], 2 * layer + 2)
                nc.vector.tensor_copy(kT[0:QK].rearrange("p h q -> p (h q)"),
                                      ps[0:QK, 0:3, :].rearrange("p a c -> p (a c)")).then_inc(S["kT_done"], 1)
                for i, b in enumerate((1, 0)):
                    dve.wait_ge(S["m_sc"], 2 * layer + i + 1)
                    src = (ps[:, 5:8, :].rearrange("p a (t k) -> p (a t) k", t=2) if b else
                           ps[:, 3:5, :].rearrange("p a (t k) -> p (a t) k", t=4)[:, 0:HM, :])
                    nc.vector.tensor_reduce(row_max[:, HM * b:HM * (b + 1)], src, AX.X, ALU.max).then_inc(S["m_max"], 1)
                    dve.wait_ge(S["m_max"], 2 * layer + i + 1)
                    nc.vector.tensor_scalar(neg_max[:, HM * b:HM * (b + 1)], row_max[:, HM * b:HM * (b + 1)],
                                            -QK ** -0.5, None, ALU.mult).then_inc(S["m_nm"], 1)
                dve.wait_ge(S["m_exp"], 2 * HM * (layer + 1))
                nc.vector.reciprocal(row_inv[:], row_sum[:]).then_inc(S["m_inv"], 1)
                dve.wait_ge(S["m_pT_ps"], 2 * layer + 2)
                nc.vector.tensor_copy(pmT[0], ps[:, 3:5, :].rearrange("p a c -> p (a c)")[:, 0:HM * P]).then_inc(S["m_pT"], 1)
                dve.wait_ge(S["m_inv"], layer + 1)

                def mix_out(name, o, banks, at, heads, inv):
                    for i, b in enumerate((1, 0)):
                        dve.wait_ge(S[o], 2 * layer + i + 1)
                        dst = xs[:, b, at:at + heads * DH].rearrange("p (h d) -> p h d", h=heads)
                        src = ps[:, banks[b], 0:heads * DH].rearrange("p (h d) -> p h d", h=heads)
                        if inv is None:
                            nc.vector.tensor_copy(dst, src).then_inc(S[name], 1)
                        else:
                            r = row_inv[:, heads * b:heads * (b + 1)].rearrange("p (h a) -> p h a", a=1)
                            nc.vector.tensor_tensor(dst, src, r.broadcast_to([P, heads, DH]), ALU.mult).then_inc(S[name], 1)

                mix_out("mix_m", "m_o", [3, 4], 0, HM, True)
                dve.wait_ge(S["s_ln"], layer + 1)
                nc.vector.scalar_tensor_tensor(out=sbt, in0=ps[:, 0:5, 0:3 * P], scalar=0.0, in1=sbt, op0=ALU.max,
                                               op1=ALU.add).then_inc(S["s_sp"], 1)
                mix_out("mix_s", "s_o", [5, 6], (HM + HD) * DH, HS, None)
                for i, b in enumerate((1, 0)):
                    nk = P * (b + 1)
                    dve.wait_ge(S["d_sc"], 2 * layer + i + 1)
                    bank = 0 if b else 3
                    src = ps[:, bank:bank + 3, :].rearrange("p a (t k) -> p (a t) k", t=2)[:, 0:HD, 0:nk]
                    bs = bias[:, :, 0:2 * P] if b else bias[:, :, P:2 * P]
                    nc.vector.scalar_tensor_tensor(out=pd[b], in0=src, scalar=DH ** -0.5, in1=bs, op0=ALU.mult,
                                                   op1=ALU.add).then_inc(S["d_b"], 1)
                    dve.wait_ge(S["d_b"], 2 * layer + i + 1)
                    dve.wait_ge(S["sel_done"], 2 * layer + 2)
                    chosen = work[b].rearrange("p (a k) -> p a k", a=1).broadcast_to([P, HD, nk])
                    nc.vector.tensor_tensor(pd[b], pd[b], chosen, ALU.add).then_inc(S["d_s"], 1)
                    dve.wait_ge(S["d_s"], 2 * layer + i + 1)
                    nc.vector.tensor_reduce(neg_max[:, HD * b:HD * (b + 1)], pd[b], AX.X, ALU.max,
                                            negate=True).then_inc(S["d_nm"], 1)
                dve.wait_ge(S["d_exp"], 2 * HD * (layer + 1))
                nc.vector.reciprocal(row_inv[:, 0:2 * HD], row_sum[:, 0:2 * HD]).then_inc(S["d_inv"], 1)
                dve.wait_ge(S["d_pT_ps"], 2 * layer + 2)
                nc.vector.tensor_copy(pdT[0], ps[:, 3:5, :].rearrange("p a c -> p (a c)")[:, 0:HD * P]).then_inc(S["d_pT"], 1)
                dve.wait_ge(S["d_inv"], layer + 1)
                mix_out("mix_d", "d_o", [5, 6], HM * DH, HD, True)
                feed(last_of(("wo", layer)), -2)
                low_T(t + 1)
                feed(last_of(("wo", layer)))
                residual("wo_ps", layer + 1, ("wo", layer), 0, None)
                normalise(n + 1)
                low_T(t + 2)
                for j in range(FF_CHUNKS):
                    feed(last_of(("gu", layer), j))
                    for b in range(NB):
                        k = FF_CHUNKS * layer + j
                        dve.wait_ge(S["silu_g"], 2 * k + b + 1)
                        if j:
                            dve.wait_ge(S["hidT_ps"], 2 * (MLP_CHUNKS + k - 1) + b + 1)
                        nc.vector.tensor_tensor(hid2[:, b, :], ps[:, 4 + b, FF_CHUNK:2 * FF_CHUNK], silu2[:, b, :],
                                                ALU.mult).then_inc(S["hid_g"], 1)
                    if j:
                        feed(last_of(("dn", layer), j - 1))
                    for b in range(NB):
                        sl = slice(b * P, (b + 1) * P)
                        dve.wait_ge(S["gh_done"], ghv + 1 + 2 * j + b + 1)
                        nc.vector.tensor_tensor(gl[:, 0:2, sl], ps[:, 6 + b, 0:2 * P].rearrange("p (k m) -> p k m", k=2),
                                                gh[:, 0:2, sl].bitcast(F32), ALU.subtract).then_inc(S["gl_done"], 1)
                feed(last_of(("dn", layer), FF_CHUNKS - 1))
                dve.wait_ge(S["ph_done"], layer + 1)
                nc.vector.tensor_tensor(gl[:, 0:2, :], pT, gh[:, 0:2, :].bitcast(F32), ALU.subtract).then_inc(S["pl_done"], 1)
                residual("dn_ps", layer + 1, ("dn", layer), FF_CHUNKS - 1, None)
                feed(last_of(("proj", layer)), 1)
                normalise(n + 2)
                low_T(t + 3)
                feed(last_of(("gate", layer)))
                for b in range(NB):
                    dve.wait_ge(S["sig_g"], 2 * layer + b + 1)
                    dve.wait_ge(S["proj_evac"], 2 * layer + b + 1)
                    nc.vector.tensor_tensor(sg[:, b, :], sg[:, b, :], pp[:, b, :], ALU.mult).then_inc(S["gmul"], 1)
                    dve.wait_ge(S["gmul"], 2 * layer + b + 1)
                    nc.vector.tensor_tensor(h[:, b, :], h[:, b, :], sg[:, b, :], ALU.add).then_inc(S["h_ready"], 1)
            normalise(LAST)

        @block.tensor
        def _(pe):
            def used(ins, u):
                ins.then_inc(S["used"], 1)

            def parts(u):
                n = u["kts"] * u["cols"]
                s = u["s"] % SPLIT_SLOTS
                pe.wait_ge(S["lo_done"], u["s"] + 1)
                return (hi[:, s, 0:n].rearrange("p (k c) -> p k c", k=u["kts"]),
                        lo[:, s, 0:n].rearrange("p (k c) -> p k c", k=u["kts"]))

            def three(out, ah, al, wh, wl, start, stop, skip=False, activation_first=True):
                ins = None
                passes = ((ah, wh), (al, wh), (ah, wl))
                for i, (a, w) in enumerate(passes):
                    l, r = (a, w) if activation_first else (w, a)
                    ins = nc.tensor.matmul(out, l, r, start=start and i == 0, stop=stop and i == 2,
                                           skip_group_check=skip)
                return ins

            def token_major(units, ah, al, columns, place, done=None, k_total=None, first=False, waits=None):
                k_total = k_total or sum(u["kts"] for u in units)
                for u in units:
                    wh, wl = parts(u)
                    for b in range(NB):
                        if waits:
                            waits(u, b)
                        sl = slice(b * P, (b + 1) * P)
                        for k in range(u["kts"]):
                            kk = u["k0"] + k
                            for i, c in enumerate(columns):
                                ins = three(place(b, i), ah[:, kk, sl], al[:, kk, sl], wh[:, k, c], wl[:, k, c],
                                            start=kk == 0, stop=kk == k_total - 1)
                        if u is units[-1] and done and b == 0:
                            done(ins)
                    used(ins, u)


            def transposes_T(t):
                norm = norm_of(t) if t >= 2 and (t - 2) % 4 != 1 or t < 2 else None
                for b in range(NB):
                    bank = 4 + 2 * b
                    if norm is not None:
                        pe.wait_ge(S["xs_ready"], xsval(norm, b))
                    for k in range(KT):
                        ins = nc.tensor.transpose(ps[:, bank + k // 4, (k % 4) * P:(k % 4 + 1) * P],
                                                  xs[:, b, k * P:(k + 1) * P], ident)
                    ins.then_inc(S["xT_ps"], 1)

            def xT(t):
                def waits(u, b):
                    if u["part"] == 0:
                        pe.wait_ge(S["xl_ready"], tval(t, b))
                return waits

            def mod_vector(v, q0=0, q1=4):
                bank = MOD_BANK[v]
                for q in range(q0, q1):
                    u = units_of(("mod", v), q)[0]
                    pe.wait_ge(landed[u["slot"]], u["landed"])
                    w = raw[:, u["slot"], :].rearrange("p (k c) -> p k c", k=KT)
                    for k in range(KT):
                        ins = nc.tensor.matmul(ps[:, bank + q // 2, (q % 2) * 256:(q % 2 + 1) * 256], csb[:, k, :], w[:, k, :],
                                               start=(k == 0), stop=(k == KT - 1))
                    used(ins, u)

            pe.wait_ge(S["csb_done"], 1)
            mod_vector(0)
            mod_vector(1)
            pe.wait_ge(S["in_consts"], 16)
            transposes_T(0)
            pe.wait_ge(S["relb_done"], 1)
            for head in range(HD):
                at = 0
                while at < HOT:
                    bank, c = (head * HOT + at) // 512, (head * HOT + at) % 512
                    n = min(HOT - at, 512 - c)
                    ins = nc.tensor.matmul(ps[:, bank, c:c + n], rbb[:, head, :], hot[:, at:at + n], start=True, stop=True)
                    at += n
            ins.then_inc(S["relb_ps"], 1)
            for f in range(KT):
                u = units_of("pw1", f)[0]
                wh, wl = parts(u)
                if f == 0:
                    pe.wait_ge(S["xl_ready"], tval(0, 1))
                if f >= 4:
                    pe.wait_ge(S["glu_done"], f - 3)
                for k in range(KT):
                    for c in range(2):
                        cs = slice(c * P, (c + 1) * P)
                        out_ = ps[:, 4 + f % 4, c * SEQ:(c + 1) * SEQ]
                        for i, (a, w) in enumerate(((xh, wh), (xl, wh), (xh, wl))):
                            ins = nc.tensor.matmul(out_, w[:, k, cs], a[:, k, :], start=(k == 0 and c == 0 and i == 0),
                                                   stop=(k == KT - 1 and i == 2), skip_group_check=True)
                used(ins, u)
            pe.wait_ge(S["toep_done"], 1)
            mod_vector(2)
            mod_vector(3)
            pe.wait_ge(S["mod_evac"], 2)
            mod_vector(4)
            pe.wait_ge(S["glu_done"], KT)
            mod_vector(5, 0, 2)
            order = POOL_PAIRS[0] + DVE_PAIRS[0] + POOL_PAIRS[1] + DVE_PAIRS[1]
            pe.wait_ge(S["init_p"], 5)
            for i, f in enumerate(order):
                p, vector = i // 4, i // 2 % 2
                if vector:
                    pe.wait_ge(S["conv_step"], 2 * TAPS * (p + 1))
                else:
                    pe.wait_ge(S["tap_added"], (TAPS - 1) * (p + 1))
                ins = nc.tensor.matmul(ps[:, 6, 0:SEQ], one["ones"], cv[:, f, :], start=(i == 0), stop=(i == KT - 1))
            ins.then_inc(S["mean_ps"], 1)
            mod_vector(5, 2, 3)
            for f in range(KT):
                pe.wait_ge(S["sq_done"], 1 + f // (KT // 2))
                ins = nc.tensor.matmul(ps[:, 7, 0:SEQ], one["ones"], sq[:, f, :], start=(f == 0), stop=(f == KT - 1))
            ins.then_inc(S["var_ps"], 1)
            mod_vector(5, 3, 4)
            halves = [slice(0, 512), slice(512, 1024)]
            pe.wait_ge(S["mod_evac"], 4)
            token_major(units_of("pw2"), xh, xl, halves, lambda b, i: ps[:, 2 * b + i, :],
                        done=lambda ins: ins.then_inc(S["pw2_ps"], 1),
                        waits=lambda u, b: pe.wait_ge(S["yl_done"], u["part"] + 1))
            pe.wait_ge(S["mod_evac"], 5)
            transposes_T(1)
            def w2_product(j):
                pe.wait_ge(S["gl_done"], 2 * j + 2)
                units = units_of("w2", j)
                for u in units:
                    wh, wl = parts(u)
                    for b in range(NB):
                        sl = slice(b * P, (b + 1) * P)
                        for k in range(u["kts"]):
                            kk = u["k0"] + k
                            for i, c in enumerate(halves):
                                ins = three(ps[:, 2 * b + i, :], gh[:, kk, sl], gl[:, kk, sl], wh[:, k, c], wl[:, k, c],
                                            start=(j == 0 and kk == 0), stop=(j == MLP_CHUNKS - 1 and kk == 3))
                        if j == MLP_CHUNKS - 1 and u is units[-1] and b == 0:
                            ins.then_inc(S["mlp_ps"], 1)
                    used(ins, u)

            for j in range(MLP_CHUNKS):
                xw = xT(1)

                def waits(u, b, j=j):
                    if j == 0:
                        xw(u, b)
                    if j and u["part"] == 0:
                        pe.wait_ge(S["relu_done"], 2 * (j - 1) + b + 1)

                token_major(units_of("w1", j), xh, xl, [slice(0, MLP_CHUNK)], lambda b, i: ps[:, 4 + b, :],
                            done=lambda ins: ins.then_inc(S["w1_ps"], 1), waits=waits)
                if j:
                    w2_product(j - 1)
                for b in range(NB):
                    pe.wait_ge(S["hid_done"], 2 * j + b + 1)
                    if j:
                        pe.wait_ge(S["gl_done"], 2 * (j - 1) + b + 1)
                    for k in range(4):
                        ins = nc.tensor.transpose(ps[:, 6 + b, k * P:(k + 1) * P], hid1[:, b, k * P:(k + 1) * P], ident)
                    ins.then_inc(S["hidT_ps"], 1)
            w2_product(MLP_CHUNKS - 1)

            for layer in range(LAYERS):
                t = 2 + 4 * layer
                glv = 2 * MLP_CHUNKS + (1 + 2 * FF_CHUNKS) * layer
                transposes_T(t)
                for u in units_of(("idx", layer)):
                    wh, wl = parts(u)
                    if u["part"] == 0:
                        pe.wait_ge(S["xl_ready"], tval(t, 1))
                    for k in range(u["kts"]):
                        kk = u["k0"] + k
                        for c in range(4):
                            cs = slice(c * P, (c + 1) * P)
                            for i, (a, w) in enumerate(((xh, wh), (xl, wh), (xh, wl))):
                                nc.tensor.matmul(ps[:, 4 + c // 2, (c % 2) * SEQ:(c % 2 + 1) * SEQ], w[:, k, cs], a[:, kk, :],
                                                 start=(kk == 0 and c % 2 == 0 and i == 0), stop=(kk == KT - 1 and i == 2),
                                                 skip_group_check=True)
                        for b in range(NB):
                            sl = slice(b * P, (b + 1) * P)
                            ins = three(ps[:, 6 + b, 0:DH + HI], xh[:, kk, sl], xl[:, kk, sl], wh[:, k, 512:IDX_COLS],
                                        wl[:, k, 512:IDX_COLS], start=kk == 0, stop=kk == KT - 1)
                    used(ins, u)
                units = units_of(("mla", layer))
                for u in units:
                    wh, wl = parts(u)
                    for b in range(NB):
                        sl = slice(b * P, (b + 1) * P)
                        for k in range(u["kts"]):
                            kk = u["k0"] + k
                            for i, c in enumerate((slice(0, QL), slice(QL, MLA_COLS))):
                                ins = three(ps[:, 2 * b + i, 0:c.stop - c.start], xh[:, kk, sl], xl[:, kk, sl],
                                            wh[:, k, c], wl[:, k, c], start=kk == 0, stop=kk == KT - 1)
                    used(ins, u)
                pe.wait_ge(S["ikd_done"], 2 * layer + 2)
                pe.wait_ge(S["iw_done"], layer + 1)
                for b in range(NB):
                    ins = nc.tensor.transpose(ps[:, 6, b * P:(b + 1) * P], ikd[:, b, :], ident)
                ins.then_inc(S["ikT_ps"], 1)
                pe.wait_ge(S["iqT_done"], layer + 1)
                pe.wait_ge(S["ikT_done"], layer + 1)
                for slot, head in enumerate(ORDER8):
                    r = slice(DH * (head % 2), DH * (head % 2) + DH)
                    ins = nc.tensor.matmul(ps[:, 4 + slot // 2, (slot % 2) * SEQ:(slot % 2 + 1) * SEQ], iqT[r, head // 2, P:2 * P],
                                           ikT[r, :], start=True, stop=True)
                ins.then_inc(S["isc_ps"], 1)
                pe.wait_ge(S["cn_done"], 4 * layer + 4)
                pe.wait_ge(S["kr_done"], 2 * layer + 2)
                for k in range(5):
                    for b in range(NB):
                        at = k * SEQ + b * P
                        ins = nc.tensor.transpose(ps[:, at // 512, at % 512:at % 512 + P], cn[:, b, k * P:(k + 1) * P], ident)
                ins.then_inc(S["cnT_ps"], 1)
                pe.wait_ge(S["relu_i"], 2 * layer + 1)
                for slot, head in enumerate(ORDER8_B0):
                    r = slice(DH * (head % 2), DH * (head % 2) + DH)
                    ins = nc.tensor.matmul(ps[:, 4 + slot // 4, (slot % 4) * P:(slot % 4 + 1) * P], iqT[r, head // 2, 0:P],
                                           ikT[r, 0:P], start=True, stop=True)
                ins.then_inc(S["isc_ps"], 1)
                units = units_of(("dsa", layer))
                for u in units:
                    wh, wl = parts(u)
                    for k in range(u["kts"]):
                        kk = u["k0"] + k
                        for c in range(3):
                            cs = slice(c * P, (c + 1) * P)
                            for i, (a, w) in enumerate(((xh, wh), (xl, wh), (xh, wl))):
                                nc.tensor.matmul(ps[:, 6 + c // 2, (c % 2) * SEQ:(c % 2 + 1) * SEQ], w[:, k, cs], a[:, kk, :],
                                                 start=(kk == 0 and c % 2 == 0 and i == 0), stop=(kk == KT - 1 and i == 2),
                                                 skip_group_check=True)
                        for b in range(NB):
                            sl = slice(b * P, (b + 1) * P)
                            for i, (a, w) in enumerate(((xh, wh), (xl, wh), (xh, wl))):
                                ins = nc.tensor.matmul(ps[:, 7, SEQ + b * DH:SEQ + (b + 1) * DH], a[:, kk, sl],
                                                       w[:, k, 3 * P:DSA_COLS], start=False,
                                                       stop=(kk == KT - 1 and i == 2), skip_group_check=True)
                    used(ins, u)
                for stage, cols, k0, bank0 in (("uq", UQ_COLS, 0, 0), ("ukv", UKV_COLS, 3, 4)):
                    u = units_of((stage, layer))[0]
                    wh, wl = parts(u)
                    if stage == "uq":
                        pe.wait_ge(S["gl_done"], glv + 1)
                    else:
                        pe.wait_ge(S["relu_i"], 2 * layer + 2)
                        pe.wait_ge(S["dsa_evac"], 5 * (layer + 1))
                    for b in range(NB):
                        sl = slice(b * P, (b + 1) * P)
                        for k in range(u["kts"]):
                            for i in range(2):
                                c = slice(i * cols // 2, (i + 1) * cols // 2)
                                ins = three(ps[:, bank0 + 2 * b + i, 0:cols // 2], gh[:, k0 + k, sl], gl[:, k0 + k, sl],
                                            wh[:, k, c], wl[:, k, c], start=k == 0, stop=k == u["kts"] - 1)
                    used(ins, u)
                pe.wait_ge(S["q7_done"], 2 * layer + 2)
                units = units_of(("sb", layer))
                for u in units:
                    wh, wl = parts(u)
                    for k in range(u["kts"]):
                        kk = u["k0"] + k
                        for c in range(5):
                            cs = slice(c * P, (c + 1) * P)
                            for i, (a, w) in enumerate(((xh, wh), (xl, wh), (xh, wl))):
                                ins = nc.tensor.matmul(ps[:, c // 2, (c % 2) * SEQ:(c % 2 + 1) * SEQ], w[:, k, cs], a[:, kk, :],
                                                       start=(kk == 0 and c % 2 == 0 and i == 0),
                                                       stop=(kk == KT - 1 and i == 2), skip_group_check=True)
                    used(ins, u)
                units = units_of(("sv", layer))
                for u in units:
                    wh, wl = parts(u)
                    for b in range(NB):
                        sl = slice(b * P, (b + 1) * P)
                        for k in range(u["kts"]):
                            kk = u["k0"] + k
                            ins = three(ps[:, 3 + b, 0:SV_COLS], xh[:, kk, sl], xl[:, kk, sl], wh[:, k, :], wl[:, k, :],
                                        start=kk == 0, stop=kk == KT - 1)
                    used(ins, u)
                pe.wait_ge(S["rope_done"], 2 * layer + 2)
                for hh in range(HM):
                    for b in range(NB):
                        at = hh * SEQ + b * P
                        ins = nc.tensor.transpose(ps[0:QK, 5 + at // 512, at % 512:at % 512 + P], q7[:, b, hh, :], ident)
                ins.then_inc(S["qkT_ps"], 1)
                pe.wait_ge(S["kf_done"], 2 * layer + 2)
                pe.wait_ge(S["sb_evac"], 4 * (layer + 1))
                for hh in range(HM):
                    for b in range(NB):
                        at = hh * SEQ + b * P
                        ins = nc.tensor.transpose(ps[0:QK, at // 512, at % 512:at % 512 + P], kfull[:, b, hh, :], ident)
                ins.then_inc(S["qkT_ps"], 1)
                if layer == 0:
                    pe.wait_ge(S["masks_done"], 3)
                pe.wait_ge(S["qT_done"], layer + 1)
                pe.wait_ge(S["kT_done"], layer + 1)
                pe.wait_ge(S["sv_evac"], 2 * layer + 2)
                for b in (1, 0):
                    nk = P * (b + 1)
                    for hh in range(HM):
                        at = hh * nk
                        bank = (5 if b else 3) + at // 512
                        nc.tensor.matmul(ps[:, bank, at % 512:at % 512 + nk], qT[0:QK, hh, b * P:(b + 1) * P], kT[0:QK, hh, 0:nk],
                                         start=True, stop=False, skip_group_check=True)
                        at += nk - P
                        ins = nc.tensor.matmul(ps[:, bank, at % 512:at % 512 + P], ident16[:], masks16[:, 0, :],
                                               start=False, stop=True, skip_group_check=True)
                    ins.then_inc(S["m_sc"], 1)
                pe.wait_ge(S["m_exp"], 2 * HM * layer + HM)
                for hh in range(HM):
                    for k in range(2):
                        at = (2 * hh + k) * P
                        ins = nc.tensor.transpose(ps[:, 5 + at // 512, at % 512:at % 512 + P], pm[1][:, hh, k * P:(k + 1) * P], ident)
                ins.then_inc(S["m_pT_ps"], 1)
                pe.wait_ge(S["m_exp"], 2 * HM * (layer + 1))
                for hh in range(HM):
                    at = hh * P
                    ins = nc.tensor.transpose(ps[:, 3 + at // 512, at % 512:at % 512 + P], pm[0][:, hh, :], ident)
                ins.then_inc(S["m_pT_ps"], 1)

                pe.wait_ge(S["m_pT"], 2 * layer + 2)
                v = pmT[1].rearrange("p (h k q) -> p h k q", h=HM, k=2)
                for b in (1, 0):
                    for hh in range(HM):
                        if b:
                            for k in range(2):
                                ins = nc.tensor.matmul(ps[:, 4, hh * VD:(hh + 1) * VD], v[:, hh, k, :], mv[:, k, hh, :],
                                                       start=k == 0, stop=k == 1)
                        else:
                            ins = nc.tensor.matmul(ps[:, 3, hh * VD:(hh + 1) * VD],
                                                   pmT[0][:, hh * P:(hh + 1) * P], mv[:, 0, hh, :], start=True, stop=True)
                    ins.then_inc(S["m_o"], 1)
                pe.wait_ge(S["mix_m"], 2 * layer + 2)
                rows_of = [(slice(0, DH), 0, 2), (slice(DH, P), 0, 2), (slice(0, DH), 1, 3), (slice(DH, P), 1, 3),
                           (slice(0, DH), 4, 5)]
                for hh in range(HS):
                    r, tq, tk = rows_of[hh]
                    nc.tensor.matmul(ps[:, hh, 0:2 * P], sT[r, tk, 0:P], sT[r, tq, :], start=True, stop=False,
                                     skip_group_check=True)
                    nc.tensor.matmul(ps[:, hh, 2 * P:3 * P], sT[r, tk, P:2 * P], sT[r, tq, P:2 * P], start=False,
                                     stop=False, skip_group_check=True)
                for hh in range(HS):
                    for c in (0, 2):
                        ins = nc.tensor.matmul(ps[:, hh, c * P:(c + 1) * P], ident16[:], masks16[:, 1, :], start=False,
                                               stop=True, skip_group_check=True)
                ins.then_inc(S["s_z"], 1)
                pe.wait_ge(S["s_sp"], layer + 1)
                for hh in range(HS):
                    for dst, w, src in ((slice(0, P), tri, slice(0, P)), (slice(P, 2 * P), tri, slice(P, 2 * P)),
                                        (slice(P, 2 * P), neg_ones[:], slice(2 * P, 3 * P)), (slice(2 * P, 3 * P), tri, slice(2 * P, 3 * P))):
                        ins = nc.tensor.matmul(ps[:, hh, dst], w, sbt[:, hh, src], start=False, stop=True,
                                               skip_group_check=True)
                ins.then_inc(S["s_zs"], 1)
                pe.wait_ge(S["s_w"], layer + 1)
                for b in (1, 0):
                    for hh in range(HS):
                        o = ps[:, 5 + b, hh * DH:(hh + 1) * DH]
                        if b:
                            nc.tensor.matmul(o, sbt[:, hh, P:2 * P], sv[:, 0, hh * DH:(hh + 1) * DH], start=True, stop=False)
                            ins = nc.tensor.matmul(o, sbt[:, hh, 2 * P:3 * P], sv[:, 1, hh * DH:(hh + 1) * DH], start=False, stop=True)
                        else:
                            ins = nc.tensor.matmul(o, sbt[:, hh, 0:P], sv[:, 0, hh * DH:(hh + 1) * DH], start=True, stop=True)
                    ins.then_inc(S["s_o"], 1)
                pe.wait_ge(S["mix_s"], 2 * layer + 2)
                for b in (1, 0):
                    nk = P * (b + 1)
                    for slot, head in enumerate(ORDER5):
                        r = slice(DH * (head % 2), DH * (head % 2) + DH)
                        ins = nc.tensor.matmul(ps[:, (0 if b else 3) + slot // 2, (slot % 2) * SEQ:(slot % 2) * SEQ + nk],
                                               dT[r, head // 2, b * P:(b + 1) * P], dkT[r, 0:nk], start=True, stop=True)
                    ins.then_inc(S["d_sc"], 1)
                pe.wait_ge(S["d_exp"], 2 * HD * layer + HD)
                pe.wait_ge(S["d_b"], 2 * layer + 2)
                for slot in range(HD):
                    for k in range(2):
                        at = (2 * slot + k) * P
                        ins = nc.tensor.transpose(ps[:, at // 512, at % 512:at % 512 + P], pd[1][:, slot, k * P:(k + 1) * P], ident)
                ins.then_inc(S["d_pT_ps"], 1)
                pe.wait_ge(S["d_exp"], 2 * HD * (layer + 1))
                for slot in range(HD):
                    at = slot * P
                    ins = nc.tensor.transpose(ps[:, 3 + at // 512, at % 512:at % 512 + P], pd[0][:, slot, :], ident)
                ins.then_inc(S["d_pT_ps"], 1)
                pe.wait_ge(S["d_pT"], 2 * layer + 2)
                for b in (1, 0):
                    for slot, head in enumerate(ORDER5):
                        o = ps[:, 5 + b, head * DH:(head + 1) * DH]
                        nkt = b + 1
                        for k in range(nkt):
                            at = (nkt * slot + k) * P
                            ins = nc.tensor.matmul(o, pdT[b][:, at:at + P], dv[:, k, :], start=k == 0, stop=k == nkt - 1)
                    ins.then_inc(S["d_o"], 1)
                pe.wait_ge(S["mix_d"], 2 * layer + 2)
                transposes_T(t + 1)
                token_major(units_of(("wo", layer)), xh, xl, halves, lambda b, i: ps[:, 2 * b + i, :],
                            done=lambda ins: ins.then_inc(S["wo_ps"], 1), waits=xT(t + 1))
                transposes_T(t + 2)

                def dn_product(j):
                    pe.wait_ge(S["gl_done"], glv + 1 + 2 * (j + 1))
                    u = units_of(("dn", layer), j)[0]
                    wh, wl = parts(u)
                    last = j == FF_CHUNKS - 1
                    for b in range(NB):
                        sl = slice(b * P, (b + 1) * P)
                        for k in range(u["kts"]):
                            for i, c in enumerate(halves):
                                ins = three(ps[:, 2 * b + i, :], gh[:, k, sl], gl[:, k, sl], wh[:, k, c], wl[:, k, c],
                                            start=(j == 0 and k == 0), stop=last and k == 1)
                        if last and b == 0:
                            ins.then_inc(S["dn_ps"], 1)
                    used(ins, u)

                for j in range(FF_CHUNKS):
                    xw = xT(t + 2)
                    k_ = FF_CHUNKS * layer + j

                    def waits(u, b, j=j, k_=k_):
                        if j == 0:
                            xw(u, b)
                        elif u["part"] == 0:
                            pe.wait_ge(S["hid_g"], 2 * (k_ - 1) + b + 1)

                    token_major(units_of(("gu", layer), j), xh, xl, [slice(0, 512)], lambda b, i: ps[:, 4 + b, :],
                                done=lambda ins: ins.then_inc(S["gu_ps"], 1), waits=waits)
                    if j == 1:
                        pe.wait_ge(S["h_ready"], hval(4 + 3 * layer, 1))
                    if j:
                        dn_product(j - 1)
                    for b in range(NB):
                        pe.wait_ge(S["hid_g"], 2 * k_ + b + 1)
                        if j:
                            pe.wait_ge(S["gl_done"], glv + 1 + 2 * (j - 1) + b + 1)
                        for k in range(2):
                            ins = nc.tensor.transpose(ps[:, 6 + b, k * P:(k + 1) * P], hid2[:, b, k * P:(k + 1) * P], ident)
                        ins.then_inc(S["hidT_ps"], 1)
                dn_product(FF_CHUNKS - 1)
                pe.wait_ge(S["pl_done"], layer + 1)
                pe.wait_ge(S["h_ready"], hval(5 + 3 * layer, 1))
                u = units_of(("proj", layer))[0]
                wh, wl = parts(u)
                for b in range(NB):
                    sl = slice(b * P, (b + 1) * P)
                    for k in range(2):
                        for i, c in enumerate(halves):
                            ins = three(ps[:, 2 * b + i, :], gh[:, k, sl], gl[:, k, sl], wh[:, k, c], wl[:, k, c],
                                        start=k == 0, stop=k == 1)
                used(ins, u)
                transposes_T(t + 3)
                xw3 = xT(t + 3)

                def waits3(u, b):
                    xw3(u, b)
                    if u["part"] == 0:
                        pe.wait_ge(S["proj_evac"], 2 * layer + b + 1)

                token_major(units_of(("gate", layer)), xh, xl, halves, lambda b, i: ps[:, 2 * b + i, :],
                            done=lambda ins: ins.then_inc(S["gate_ps"], 1), waits=waits3)


def bucket_table():
    d = (2 * P - 1 - np.arange(HOT)).astype(np.int64)
    exact = BUCKETS // 2
    dd = np.maximum(d, 1).astype(np.float32)
    large = exact + (np.log(dd / np.float32(exact)) / np.float32(np.log(MAX_DIST / exact)) * (BUCKETS - exact)).astype(np.int32)
    bucket = np.where(d < exact, d, np.minimum(large, BUCKETS - 1))
    table = np.zeros((P, HOT), np.float32)
    for i in range(HOT):
        if d[i] >= 0:
            table[bucket[i], i] = 1.0
        else:
            table[BUCKETS, i] = NEG
    return table


def constants():
    c = np.zeros((P, C_END), np.float32)
    a, b = np.arange(P)[:, None], np.arange(P)[None, :]
    c[:, C_ID:C_ID + P] = a == b
    c[:, C_TRI:C_TRI + P] = -1.0 * (a >= b)
    c[:, C_CAUSAL:C_CAUSAL + P] = np.where(b > a, NEG, 0.0)
    c[:, C_STRICT:C_STRICT + P] = np.where(a >= b, NEG, 0.0)
    inv = np.float32(10000.0) ** (-np.arange(HALF, dtype=np.float32) / np.float32(HALF))
    ang = np.arange(SEQ, dtype=np.float32)[:, None] * inv[None, :]
    for tab, at in ((np.cos(ang), C_COS), (np.sin(ang), C_SIN)):
        c[:, at:at + NB * HALF] = tab.astype(np.float32).reshape(NB, P, HALF).transpose(1, 0, 2).reshape(P, NB * HALF)
    c[:, C_HOT:] = bucket_table()
    return c


def lay_out(inputs):
    g = lambda n: np.ascontiguousarray(inputs[n])
    flat = np.empty(STREAM, np.float32)

    def put(stage, n, w):
        for u in units_of(stage, n):
            part = w[u["k0"] * P:(u["k0"] + u["kts"]) * P]
            assert part.shape[1] == u["cols"]
            flat[u["offset"]:u["offset"] + part.size] = part.reshape(u["kts"], P, u["cols"]).transpose(1, 0, 2).reshape(-1)

    wm = g("w_mod")[0]
    order = [1, 0, 2, 3, 4, 5]
    for v, src in enumerate(order):
        for q in range(4):
            put(("mod", v), q, wm[:, src * D + q * 256:src * D + (q + 1) * 256])
    pw1 = g("conv_w_pw1")[0]
    for f in range(KT):
        put("pw1", f, np.concatenate([pw1[:, f * P:(f + 1) * P], pw1[:, D + f * P:D + (f + 1) * P]], 1))
    put("pw2", 0, g("conv_w_pw2")[0])
    w1, w2 = g("mlp_w1")[0], g("mlp_w2")[0]
    for j in range(MLP_CHUNKS):
        put("w1", j, w1[:, j * MLP_CHUNK:(j + 1) * MLP_CHUNK])
        put("w2", j, w2[j * MLP_CHUNK:(j + 1) * MLP_CHUNK])
    for layer in range(LAYERS):
        w = g("w_in_2")[layer]
        at = np.cumsum([0, QL, KVL, ROPE, HD * DH, DH, DH, HI * DH, DH, HI, HS * DH, HS * DH, HS * DH])
        put(("idx", layer), 0, w[:, at[6]:at[9]])
        put(("mla", layer), 0, w[:, at[0]:at[3]])
        put(("dsa", layer), 0, w[:, at[3]:at[6]])
        q, k = at[9], at[10]
        put(("sb", layer), 0, np.concatenate([w[:, q:q + 128], w[:, q + 128:q + 256], w[:, k:k + 128], w[:, k + 128:k + 256],
                                              w[:, q + 256:q + 320], w[:, k + 256:k + 320]], 1))
        put(("sv", layer), 0, w[:, at[11]:at[12]])
        put(("uq", layer), 0, g("mla_w_uq_2")[layer])
        put(("ukv", layer), 0, g("mla_w_ukv_2")[layer])
        put(("wo", layer), 0, g("w_o_2")[layer])
        wg, wu, wd = g("w_gate_2")[layer], g("w_up_2")[layer], g("w_down_2")[layer]
        for j in range(FF_CHUNKS):
            c = slice(j * FF_CHUNK, (j + 1) * FF_CHUNK)
            put(("gu", layer), j, np.concatenate([wg[:, c], wu[:, c]], 1))
            put(("dn", layer), j, wd[c])
        put(("proj", layer), 0, g("w_ple_proj_2")[layer])
        put(("gate", layer), 0, g("w_ple_gate_2")[layer])

    cols = lambda v: v.reshape(-1, P).T
    vectors = np.concatenate([cols(g("c")[0]), cols(g("conv_b_pw1")[0]), cols(g("conv_b_dw")[0]), cols(g("conv_ln_g")[0]),
                              cols(g("conv_ln_b")[0]),
                              g("conv_w_dw")[0].reshape(TAPS, KT, P).transpose(2, 1, 0).reshape(P, KT * TAPS)], 1)
    bm = g("b_mod")[0]
    rows = {f"b_mod{i}": bm[i * D:(i + 1) * D] for i in range(6)}
    rows.update(b_pw2=g("conv_b_pw2")[0], norm1_g=g("norm1_g")[0], norm2_g=g("norm2_g")[0], final_g=g("final_g"),
                final=g("final_norm_2"))
    for l in range(LAYERS):
        rows[f"attn{l}"] = g("attn_norm_2")[l]
        rows[f"ffn{l}"] = g("ffn_norm_2")[l]
        rows[f"ple{l}"] = g("ple_norm_2")[l]
        rows[f"lora{l}"] = np.concatenate([g("mla_q_norm_2")[l], g("mla_kv_norm_2")[l]])
    rel = np.concatenate([g("rel_bias_2"), np.ones((1, HD), np.float32)], 0)
    arrays = dict(stream=flat, x=g("x")[0], p_t=np.ascontiguousarray(g("p_2")[:, 0].transpose(0, 2, 1)),
                  vectors=np.ascontiguousarray(vectors), rel=rel, consts=constants())
    for k, v in rows.items():
        arrays["row_" + k] = np.ascontiguousarray(v)
    return arrays


def kernel(**inputs):
    import concourse.bacc as bacc
    from concourse.bass_utils import run_bass_kernel_spmd as run

    nc = bacc.Bacc("TRN2", target_bir_lowering=False, num_devices=1)
    arrays = lay_out(inputs)
    aps = {n: nc.dram_tensor(n, a.shape, mybir.dt.from_np(a.dtype), kind="ExternalInput").ap() for n, a in arrays.items()}
    rows = {n[4:]: ap for n, ap in aps.items() if n.startswith("row_")}
    out = nc.dram_tensor("out", (SEQ, D), F32, kind="ExternalOutput").ap()
    build(nc, aps["stream"], aps["x"], aps["p_t"], aps["vectors"], rows, aps["rel"], aps["consts"], out)
    r = run(nc, [arrays], core_ids=[0])
    return r.results[0]["out"].reshape(1, SEQ, D)
```

```python
from contextlib import ExitStack

import numpy as np

import concourse.bass as bass
from concourse import mybir

F32 = mybir.dt.float32
F32R = mybir.dt.float32r
BF16 = mybir.dt.bfloat16
ALU = mybir.AluOpType
ACT = mybir.ActivationFunctionType
AX = mybir.AxisListType

P = 128
D = 1024
KT = D // P
SEQ = 256
NB = SEQ // P
EPS = 1e-6
LAYERS = 2

SEG = 64
SEGS = SEQ // SEG
TAPS = 31
HALO = TAPS // 2
PADDED = SEG + 2 * HALO
FFN1 = 4 * D
MLP_CHUNK = 512
MLP_CHUNKS = FFN1 // MLP_CHUNK

HM, NOPE, ROPE, VD = 6, 64, 32, 64
HALF = ROPE // 2
QK = NOPE + ROPE
QL, KVL = 384, 256
HD = 5
HI = 8
HS = 5
DH = 64
TOPK = 64
BUCKETS, MAX_DIST = 32, 128
DFF = 2816
FF_CHUNK = 256
FF_CHUNKS = DFF // FF_CHUNK
PLE = 256

SLOT = 2048
RAW_SLOTS = 4
SPLIT_SLOTS = 3
LOOKAHEAD = SPLIT_SLOTS - 1
NEG = -1.0e30
TAKEN = -3.0e38

IDX_COLS = HI * DH + DH + HI
MLA_COLS = QL + KVL + ROPE
DSA_COLS = (HD + 2) * DH
SV = HS * DH
SB_COLS = 2 * (HS - 1) * DH
SV_COLS = SV + 2 * DH
UQ_COLS = HM * QK
UKV_COLS = HM * (NOPE + VD)

ORDER5 = [0, 2, 1, 3, 4]
ORDER8 = [0, 2, 1, 3, 4, 6, 5, 7]
ORDER8_B0 = [0, 2, 4, 6, 1, 3, 5, 7]


def plan_units():
    units = []

    def add(stage, n, kts, cols, split=True):
        k0 = 0
        for i, k in enumerate(kts):
            units.append(dict(stage=stage, n=n, part=i, k0=k0, kts=k, cols=cols, split=split))
            k0 += k

    for v in range(2):
        for q in range(4):
            add(("mod", v), q, [KT], 256, split=False)
    for f in range(KT):
        add("pw1", f, [KT], 256)
    for v in range(2, 6):
        for q in range(4 if v < 5 else 0):
            add(("mod", v), q, [KT], 256, split=False)
    add("pw2", 0, [2] * 4, D)
    for q in range(4):
        add(("mod", 5), q, [KT], 256, split=False)
    for j in range(MLP_CHUNKS + 1):
        if j < MLP_CHUNKS:
            add("w1", j, [4, 4], MLP_CHUNK)
        if j:
            add("w2", j - 1, [2, 2], D)
    for layer in range(LAYERS):
        add(("mla", layer), 0, [3, 3, 2], MLA_COLS)
        add(("idx", layer), 0, [3, 3, 2], IDX_COLS)
        add(("dsa", layer), 0, [4, 4], DSA_COLS)
        add(("uq", layer), 0, [QL // P], UQ_COLS)
        add(("ukv", layer), 0, [KVL // P], UKV_COLS)
        add(("sb", layer), 0, [4, 4], SB_COLS)
        add(("sv", layer), 0, [4, 4], SV_COLS)
        add(("wo", layer), 0, [2] * 4, D)
        for j in range(FF_CHUNKS + 1):
            if j < FF_CHUNKS:
                add(("gu", layer), j, [4, 4], 2 * FF_CHUNK)
            if j:
                add(("dn", layer), j - 1, [2], D)
        add(("proj", layer), 0, [PLE // P], D)
        add(("gate", layer), 0, [2] * 4, D)
    at, split, landed = 0, 0, [0] * RAW_SLOTS
    for i, u in enumerate(units):
        u["index"] = i
        u["offset"] = at
        at += P * u["kts"] * u["cols"]
        u["slot"] = i % RAW_SLOTS
        landed[u["slot"]] += 16
        u["landed"] = landed[u["slot"]]
        if u["split"]:
            u["s"] = split
            split += 1
    return units, at


UNITS, STREAM = plan_units()
SPLIT = [u for u in UNITS if u["split"]]


def units_of(stage, n=0):
    return [u for u in UNITS if u["stage"] == stage and u["n"] == n]


def last_of(stage, n=0):
    return units_of(stage, n)[-1]


C_ID, C_TRI, C_OPEN, C_CAUSAL, C_STRICT = (i * P for i in range(5))
C_COS = C_STRICT + P
C_SIN = C_COS + NB * HALF
C_HOT = C_SIN + NB * HALF
HOT = 3 * P
C_END = C_HOT + HOT

POOL_TILES = (0, 1, 2)
DVE_GROUPS = ((3, 4), (5, 6))
PE_TILE = 7
ROWS = ("b_mod1", "b_mod0", "b_mod2", "b_mod3", "b_mod4", "b_mod5", "norm1_g", "b_pw2")
PRODUCTS = 2
GATES = 4
DIAGONALS = 16
LOW_ROW = 32

V_C, V_BPW1, V_BDW, V_LNG, V_LNB, V_DW = 0, 8, 24, 32, 40, 48
V_END = V_DW + KT * TAPS


def build(nc, stream, x, p_t, vectors, rows, rel, consts, out):
    ctx = ExitStack()
    with ctx:
        def sb(name, shape, dt=F32):
            return ctx.enter_context(nc.sbuf_tensor(name, shape, dt))

        def sem(name):
            return ctx.enter_context(nc.semaphore(name))

        raw = sb("raw", [P, RAW_SLOTS, SLOT])
        hi = sb("hi", [P, SPLIT_SLOTS, SLOT], F32R)
        lo = sb("lo", [P, SPLIT_SLOTS, SLOT], F32R)
        xh = sb("xh", [P, KT, SEQ], F32R)
        xl = sb("xl", [P, KT, SEQ], F32R)
        gh = sb("gh", [P, 5, SEQ], F32R)
        gl = sb("gl", [P, 5, SEQ], F32R)
        h = sb("h", [P, NB, D])
        xs = sb("xs", [P, NB, D])
        gain = sb("gain", [P, 2, D])
        lora_gain = sb("lora_gain", [P, QL + KVL])
        table = sb("table", [P, C_HOT])
        neg_ones = sb("neg_ones", [P, P])
        ident16 = sb("ident16", [P, P], BF16)
        masks16 = sb("masks16", [P, 2, P], BF16)
        bias = sb("bias", [P, HD, 2 * P])
        ss = sb("ss", [P, 4])
        var = sb("var", [P, 4])
        rstd = sb("rstd", [P, 4])
        pow_half = sb("pow_half", [P, 4])
        lss = sb("lss", [P, NB, 2])
        lvar = sb("lvar", [P, NB, 2])
        lrstd = sb("lrstd", [P, NB, 2])
        top8 = sb("top8", [P, NB, 8])
        neg_max = sb("neg_max", [P, 12])
        row_max = sb("row_max", [P, 12])
        row_sum = sb("row_sum", [P, 12])
        row_inv = sb("row_inv", [P, 12])
        iw = sb("iw", [P, NB, HI])
        epsilon = sb("epsilon", [P, 1])
        scratch = sb("scratch", [P, 16512])
        ident = table[:, C_ID:C_ID + P]
        tri = table[:, C_TRI:C_TRI + P]
        cmask = table[:, C_OPEN:C_OPEN + 2 * P]
        cosines = table[:, C_COS:C_COS + NB * HALF].rearrange("p (b d) -> p b d", b=NB)
        sines = table[:, C_SIN:C_SIN + NB * HALF].rearrange("p (b d) -> p b d", b=NB)

        ps = ctx.enter_context(nc.psum_tensor("ps", [P, 8, 512], F32))

        def carve(table, start=0):
            views, at = {}, start
            for name, size in table:
                views[name] = scratch[:, at:at + size]
                at += size
            assert at <= 16512, at
            return views

        one = carve([("upad", KT * SEGS * PADDED), ("sig", GATES * SEQ), ("cv", KT * SEQ), ("rs", SEQ), ("sq", KT * SEQ), ("csb", KT * P), ("shift", D),
                     ("g1", D), ("g2", D), ("vec", V_END), ("ones", P), ("rbb", HD * P)])
        upad = one["upad"].rearrange("p (f s t) -> p f s t", f=KT, s=SEGS)
        sig = one["sig"].rearrange("p (b t) -> p b t", b=GATES)
        cv = one["cv"].rearrange("p (f t) -> p f t", f=KT)
        sq = one["sq"].rearrange("p (f t) -> p f t", f=KT)
        csb = one["csb"].rearrange("p (k m) -> p k m", k=KT)
        vec = one["vec"]
        rows_raw = one["cv"][0:LOW_ROW + len(ROWS), KT * SEQ - D:]
        brows = gh[0:LOW_ROW + len(ROWS)].rearrange("p k m -> p (k m)")[:, 0:D]
        pick = gl[0:LOW_ROW + len(ROWS)].rearrange("p k m -> p (k m)")[:, 0:len(ROWS) * P].rearrange("p (i m) -> p i m", i=len(ROWS))
        dw = vec[:, V_DW:V_END].rearrange("p (f k) -> p f k", f=KT)
        hid1 = one["sq"][:, 0:NB * MLP_CHUNK].rearrange("p (b c) -> p b c", b=NB)
        taps = one["sq"][:, 0:PRODUCTS * len(POOL_TILES) * SEQ].rearrange("p (i f t) -> p i f t", i=PRODUCTS, f=len(POOL_TILES))
        diagonals = xs[:].rearrange("p b (i m) -> p (b i) m", m=P)
        rbb = one["rbb"][0:BUCKETS + 1, :].rearrange("p (h m) -> p h m", h=HD)
        rb = one["cv"][0:BUCKETS + 1, 0:HD]
        hot = one["cv"][0:BUCKETS + 1, 512:512 + HOT]
        toep = one["sq"][:, 0:HD * 3 * P].rearrange("p (h d) -> p h d", h=HD)

        two = carve([("Z", 3072), ("X", 2304), ("Y", 2304), ("iqT", 4 * SEQ), ("ikT", SEQ), ("work", 3 * P),
                     ("dT", 3 * SEQ), ("dkT", SEQ), ("dv", NB * DH), ("sT", 6 * SEQ), ("sv", NB * SV),
                     ("mv", NB * HM * VD), ("qT", HM * SEQ), ("kT", HM * SEQ)])
        relu1 = two["Z"][:, 0:2048].rearrange("p (h k) -> p h k", h=HI)
        relu0 = two["Z"][:, 2048:3072].rearrange("p (h k) -> p h k", h=HI)
        kfull = two["Z"][:, 0:NB * HM * QK].rearrange("p (b h d) -> p b h d", b=NB, h=HM)
        sbt = two["Z"][:, 1152:1152 + HS * 384].rearrange("p (h k) -> p h k", h=HS)
        cn = two["X"][:, 0:NB * (QL + KVL)].rearrange("p (b c) -> p b c", b=NB)
        q7 = two["Y"][:, 0:NB * 7 * QK].rearrange("p (b h d) -> p b h d", b=NB, h=7)
        rt = two["Y"][:, 1344:1344 + 4 * 224].rearrange("p (i b h d) -> p i b h d", i=4, b=NB, h=7)
        ikd = two["Y"][:, 2048:2304].rearrange("p (b d) -> p b d", b=NB)
        pm = [two["X"][:, 1536:2304].rearrange("p (h k) -> p h k", h=HM),
              two["X"][:, 0:1536].rearrange("p (h k) -> p h k", h=HM)]
        pmT = [two["Y"][:, 1536:2304], two["Y"][:, 0:1536]]
        pd = [two["X"][:, 1280:1920].rearrange("p (h k) -> p h k", h=HD),
              two["X"][:, 0:1280].rearrange("p (h k) -> p h k", h=HD)]
        pdT = [two["Y"][:, 1280:1920], two["Y"][:, 0:1280]]
        iqT = two["iqT"].rearrange("p (t q) -> p t q", t=4)
        ikT = two["ikT"]
        work = [two["work"][:, 0:P], two["work"][:, P:3 * P]]
        dT = two["dT"].rearrange("p (t q) -> p t q", t=3)
        dkT = two["dkT"]
        dv = two["dv"].rearrange("p (b d) -> p b d", b=NB)
        sT = two["sT"].rearrange("p (t q) -> p t q", t=6)
        sv = two["sv"].rearrange("p (b c) -> p b c", b=NB)
        mv = two["mv"].rearrange("p (b h d) -> p b h d", b=NB, h=HM)
        qT = two["qT"].rearrange("p (h q) -> p h q", h=HM)
        kT = two["kT"].rearrange("p (h q) -> p h q", h=HM)

        three = carve([("pp", NB * D), ("sg", NB * D), ("hid", NB * FF_CHUNK), ("silu", NB * FF_CHUNK), ("pT", 2 * SEQ)])
        pp = three["pp"].rearrange("p (b c) -> p b c", b=NB)
        sg = three["sg"].rearrange("p (b c) -> p b c", b=NB)
        hid2 = three["hid"].rearrange("p (b c) -> p b c", b=NB)
        silu2 = three["silu"].rearrange("p (b c) -> p b c", b=NB)
        pT = three["pT"].rearrange("p (t q) -> p t q", t=2)

        skew = nc.dram_tensor("skew", (HD, P * 3 * P), F32, kind="Internal").ap()

        landed = [sem(f"landed{i}") for i in range(RAW_SLOTS)]
        names = """used hi_done lo_done in_consts in_vec in_x in_rows in_rel in_gain in_lora in_p in_skew out_skew
        masks_done init_p silu_c csb_done relb_ps toep_done relb_done mod_evac gain_row gain_ps mod_mid scaled
        pick_done sumsq var_done rstd_done h_ready xs_mid xs_ready xT_ps xh_ready xl_ready sig_done glu_done
        tap_ready tap_added diag_ready diag_used conv_first tile_done tile_biased conv_step mean_ps cent_done
        sq_done var_ps deviation ln_scale ln_done silu_done yh_done yl_done pw2_ps res_step w1_ps relu_done
        hid_done hidT_ps gh_done gl_done mlp_ps iqT_done ikd_done iw_done ikT_ps ikT_done isc_ps relu_i isc_step
        topk_step sel_done lora_sq lora_var lora_rstd cn_done kr_done cnT_ps dsa_evac q7_done kv_done sb_evac
        sv_evac rope_t rope_done kf_done qkT_ps qT_done kT_done m_sc m_max m_nm m_exp m_inv m_pT_ps m_pT m_o
        mix_m s_z s_abs c4_evac s_e s_ln s_sp s_zs s_w s_o mix_s d_sc d_b d_s d_nm d_exp d_inv d_pT_ps d_pT d_o
        mix_d wo_ps gu_ps silu_g hid_g dn_ps ph_done pl_done proj_ps proj_evac0 proj_evac1 gate_ps sig_g gmul
        outs""".split()
        S = {n: sem(n) for n in names}

        block = ctx.enter_context(nc.Block())

        def product(eng, stage, n=0):
            eng.wait_ge(S["used"], last_of(stage, n)["index"] + 1)

        def block_product(eng, first, value, b, stage, n=0):
            if b == 0:
                eng.wait_ge(S[first], value)
            else:
                product(eng, stage, n)

        EMBED_AT = 4

        SB_GROUPS = ((slice(0, 3), slice(5, 8)), (slice(3, 5), slice(0, 2)))

        MOD_BANK = [0, 2, 0, 2, 4, 6]

        NORMS = 3 + 3 * LAYERS + 1
        LAST = NORMS - 1

        def nval(n, b):
            return 2 * n + b + 1

        def deferred(n):
            return 3 < n < LAST and n % 3 != 0

        def hval(n, b):
            return 2 * (n - 1) + b + 1

        def xsval(n, b):
            return 2 * (n if n < 2 else n - 1) + b + 1

        def tval(t, b):
            return 2 * t + b + 1

        def norm_of(t):
            return t if t < 2 else 3 + 3 * ((t - 2) // 4) + (0, None, 1, 2)[(t - 2) % 4]

        def before_T(t):
            if t == 0:
                return None
            if t == 1:
                return last_of("pw2")
            layer, k = (t - 2) // 4, (t - 2) % 4
            if k == 0:
                return last_of("w1", MLP_CHUNKS - 1) if layer == 0 else last_of(("gate", layer - 1))
            return (None, last_of(("sv", layer)), last_of(("wo", layer)), last_of(("gu", layer), FF_CHUNKS - 1))[k]

        GAIN_ROWS = ["norm1_g", "norm2_g", "final_g"] + [f"{k}{l}" for l in range(LAYERS) for k in ("attn", "ffn", "ple")] + ["final"]

        @block.sync
        def _(sp):
            def weights(units):
                for u in units:
                    if u["index"] >= RAW_SLOTS:
                        old = UNITS[u["index"] - RAW_SLOTS]
                        if old["split"]:
                            sp.wait_ge(S["lo_done"], old["s"] + 1)
                        else:
                            sp.wait_ge(S["used"], old["index"] + 1)
                    n = u["kts"] * u["cols"]
                    src = stream[u["offset"]:u["offset"] + P * n].rearrange("(p n) -> p n", p=P)
                    sp.dma_start(raw[:, u["slot"], 0:n], src).then_inc(landed[u["slot"]], 16)

            def row(dst, name, s):
                sp.dma_start(dst, rows[name].partition_broadcast(P)).then_inc(S[s], 16)

            def gain_row(n):
                if n >= 2:
                    sp.wait_ge(S["xs_ready"] if n - 2 != 2 else S["h_ready"],
                               xsval(n - 2, 1) if n - 2 != 2 else hval(3, 1))
                row(gain[:, n % 2, :], GAIN_ROWS[n], "in_gain")

            def lora_row(layer):
                if layer:
                    sp.wait_ge(S["cn_done"], 4 * layer)
                row(lora_gain[:], f"lora{layer}", "in_lora")

            sp.dma_start(vec, vectors).then_inc(S["in_vec"], 16)
            weights(UNITS[0:1])
            sp.dma_start(rows_raw, rows["stack"]).then_inc(S["in_rows"], 16)
            sp.dma_start(table[:], consts[:, 0:C_HOT]).then_inc(S["in_consts"], 16)
            sp.dma_start(h[:], x.rearrange("(b p) d -> p b d", p=P)).then_inc(S["in_x"], 16)
            weights(UNITS[1:2])
            sp.dma_start(hot, consts[0:BUCKETS + 1, C_HOT:C_HOT + HOT]).then_inc(S["in_rel"], 16)
            sp.dma_start(rb, rel).then_inc(S["in_rel"], 16)
            first = units_of("pw1", 0)[0]["index"]
            weights(UNITS[2:first + 4])
            sp.wait_ge(S["toep_done"], 1)
            sp.dma_start(skew.rearrange("h (p d) -> p h d", p=P), toep).then_inc(S["out_skew"], 16)
            weights(UNITS[first + 4:first + 6])
            sp.wait_ge(S["out_skew"], 16)
            for slot, head in enumerate(ORDER5):
                src = skew[head, P - 1:P - 1 + P * (3 * P - 1)].rearrange("(p d) -> p d", p=P)[:, 0:2 * P]
                sp.dma_start(bias[:, slot, :], src).then_inc(S["in_skew"], 16)
            first += 6
            at = units_of(("mod", 2), 0)[0]["index"]
            weights(UNITS[first:at])
            gain_row(1)
            end = units_of("w1", 1)[0]["index"]
            weights(UNITS[at:end])
            gain_row(2)
            at, end = end, units_of(("mla", 0))[0]["index"]
            weights(UNITS[at:end])
            for layer in range(LAYERS):
                n = 3 + 3 * layer
                gain_row(n)
                lora_row(layer)
                at, end = end, units_of(("wo", layer))[0]["index"]
                weights(UNITS[at:end])
                gain_row(n + 1)
                at, end = end, units_of(("gu", layer), 2)[0]["index"]
                weights(UNITS[at:end])
                gain_row(n + 2)
                sp.wait_ge(S["mix_d"], 2 * layer + 2)
                sp.dma_start(pT, p_t[layer].rearrange("(t p) q -> p t q", p=P)).then_inc(S["in_p"], 16)
                at = end
                end = units_of(("mla", layer + 1))[0]["index"] if layer + 1 < LAYERS else len(UNITS)
                weights(UNITS[at:end])
            gain_row(LAST)
            for b in range(NB):
                sp.wait_ge(S["xs_ready"], xsval(LAST, b))
                sp.dma_start(out[b * P:(b + 1) * P, :], xs[:, b, :]).then_inc(S["outs"], 16)
            sp.wait_ge(S["outs"], 32)

        @block.scalar
        def _(act):
            fed = [0]

            def feed(unit, ahead=LOOKAHEAD):
                while fed[0] < min(unit["s"] + 1 + ahead, len(SPLIT)):
                    u = SPLIT[fed[0]]
                    act.wait_ge(landed[u["slot"]], u["landed"])
                    if u["s"] >= SPLIT_SLOTS:
                        act.wait_ge(S["used"], SPLIT[u["s"] - SPLIT_SLOTS]["index"] + 1)
                    n = u["kts"] * u["cols"]
                    nc.scalar.activation(hi[:, u["s"] % SPLIT_SLOTS, 0:n], raw[:, u["slot"], 0:n],
                                         ACT.Copy).then_inc(S["hi_done"], 1)
                    fed[0] += 1

            def squares(n):
                for b in range(NB):
                    if n:
                        act.wait_ge(S["h_ready"], hval(n, b))
                    else:
                        act.wait_ge(S["in_x"], 16)
                        act.wait_ge(S["init_p"], 2)
                    k = 2 * (n % 2) + b
                    dump = sg if deferred(n) else xs
                    nc.scalar.activation(dump[:, b, :], h[:, b, :], ACT.Square,
                                         accum_out=ss[:, k:k + 1]).then_inc(S["sumsq"], 1)

            def high_T(t):
                if before_T(t):
                    act.wait_ge(S["used"], before_T(t)["index"] + 1)
                for b in range(NB):
                    bank = 4 + 2 * b
                    act.wait_ge(S["xT_ps"], tval(t, b))
                    nc.scalar.activation(xh[:, :, b * P:(b + 1) * P],
                                         ps[:, bank:bank + 2, :].rearrange("p a (k m) -> p (a k) m", k=4),
                                         ACT.Copy).then_inc(S["xh_ready"], 1)

            act.wait_ge(S["in_vec"], 16)
            nc.scalar.activation(vec[:, V_C:V_C + KT], vec[:, V_C:V_C + KT], ACT.Silu).then_inc(S["silu_c"], 1)
            squares(0)
            act.wait_ge(S["gain_ps"], 1)
            nc.scalar.activation(gain[:, 0, :], ps[:, 4:6, :].rearrange("p a c -> p (a c)"), ACT.Copy).then_inc(S["gain_row"], 1)
            feed(units_of("pw1", 0)[0], 1)
            high_T(0)
            feed(units_of("pw1", 0)[0])
            act.wait_ge(S["relb_ps"], 1)
            nc.scalar.activation(toep.rearrange("p h d -> p (h d)"),
                                 ps[:, 0:4, :].rearrange("p a c -> p (a c)")[:, 0:HD * HOT], ACT.Copy).then_inc(S["toep_done"], 1)

            def tap_products(k):
                made = k - 1
                if k and made >= PRODUCTS:
                    act.wait_ge(S["tap_added"], made - PRODUCTS + 1)
                for i, f in enumerate(POOL_TILES):
                    src = upad[:, f, :, k:k + SEG]
                    dst = taps[:, made % PRODUCTS, i, :] if k else cv[:, f, :]
                    bias_ = vec[:, V_BDW + f:V_BDW + f + 1] if k == 0 else 0.0
                    ins = nc.scalar.activation(dst.rearrange("p (s t) -> p s t", s=SEGS), src, ACT.Identity,
                                               scale=dw[:, f, k:k + 1], bias=bias_)
                    ins.then_inc(S["tap_ready"] if k else S["conv_first"], 1)

            def diagonal(k):
                if k == 0:
                    act.wait_ge(S["xT_ps"], 2)
                if k >= DIAGONALS:
                    act.wait_ge(S["diag_used"], k - DIAGONALS + 1)
                nc.scalar.activation(diagonals[:, k % DIAGONALS, :], ident, ACT.Copy,
                                     scale=dw[:, PE_TILE, k:k + 1]).then_inc(S["diag_ready"], 1)

            def mod_copy(dst, v):
                product(act, ("mod", v), 3)
                nc.scalar.activation(dst, ps[:, MOD_BANK[v]:MOD_BANK[v] + 2, :].rearrange("p a c -> p (a c)"),
                                     ACT.Copy).then_inc(S["mod_evac"], 1)

            done = 0
            for f in range(KT):
                feed(units_of("pw1", f)[0], min(LOOKAHEAD, KT - 1 - f))
                product(act, "pw1", f)
                if f >= GATES:
                    act.wait_ge(S["glu_done"], f - GATES + 1)
                nc.scalar.activation(sig[:, f % GATES, :], ps[:, 4 + f % 4, SEQ:2 * SEQ], ACT.Sigmoid,
                                     bias=vec[:, V_BPW1 + KT + f:V_BPW1 + KT + f + 1]).then_inc(S["sig_done"], 1)
                if f >= POOL_TILES[-1]:
                    if f == POOL_TILES[-1]:
                        act.wait_ge(S["glu_done"], POOL_TILES[-1] + 1)
                        act.wait_ge(S["out_skew"], 16)
                    for k in range(done, done + 2):
                        tap_products(k)
                    done += 2
            made = 0
            for k in range(done, TAPS):
                tap_products(k)
                goal = min(TAPS, -(-TAPS * (k + 1 - done) // (TAPS - done)))
                for i in range(made, goal):
                    diagonal(i)
                made = goal
                if k == (done + TAPS) // 2:
                    mod_copy(one["g1"], 2)
            mod_copy(one["shift"], 3)
            act.wait_ge(S["tile_done"], 1)
            nc.scalar.activation(cv[:, PE_TILE, :], ps[:, 5, 0:SEQ], ACT.Identity,
                                 bias=vec[:, V_BDW + PE_TILE:V_BDW + PE_TILE + 1]).then_inc(S["tile_biased"], 1)
            for i in range(2):
                act.wait_ge(S["cent_done"], i + 1)
                half = slice(i * KT // 2, (i + 1) * KT // 2)
                nc.scalar.activation(sq[:, half, :], cv[:, half, :], ACT.Square).then_inc(S["sq_done"], 1)
            feed(units_of("pw2")[0], 0)
            act.wait_ge(S["var_ps"], 1)
            nc.scalar.activation(one["rs"], ps[:, 7, 0:SEQ], ACT.Sqrt, bias=epsilon[:]).then_inc(S["deviation"], 1)
            feed(units_of("pw2")[0], 1)
            act.wait_ge(S["used"], last_of("pw1", KT - 1)["index"] + 1)
            for i in range(KT // 2):
                act.wait_ge(S["ln_done"], i + 1)
                for f in (2 * i, 2 * i + 1):
                    nc.scalar.activation(sq[:, f, :], cv[:, f, :], ACT.Silu, scale=vec[:, V_LNG + f:V_LNG + f + 1],
                                         bias=vec[:, V_LNB + f:V_LNB + f + 1]).then_inc(S["silu_done"], 1)
                act.wait_ge(S["silu_done"], 2 * (i + 1))
                pair = slice(2 * i, 2 * i + 2)
                nc.scalar.activation(xh[:, pair, :], sq[:, pair, :], ACT.Copy).then_inc(S["yh_done"], 1)
            feed(last_of("pw2"), 0)
            squares(1)
            feed(last_of("w1", 0), 0)
            mod_copy(one["g2"], 5)
            high_T(1)
            for j in range(MLP_CHUNKS):
                feed(last_of("w1", j))
                for b in range(NB):
                    block_product(act, "w1_ps", j + 1, b, "w1", j)
                    if j:
                        act.wait_ge(S["hidT_ps"], 2 * (j - 1) + b + 1)
                    nc.scalar.activation(hid1[:, b, :], ps[:, 4 + b, :], ACT.Relu).then_inc(S["relu_done"], 1)
                    act.wait_ge(S["relu_done"], 2 * j + b + 1)
                    nc.scalar.activation(hid1[:, b, :], hid1[:, b, :], ACT.Square).then_inc(S["hid_done"], 1)
                if j:
                    feed(last_of("w2", j - 1))
                    act.wait_ge(S["used"], last_of("w2", j - 1)["index"] + 1)
                for b in range(NB):
                    act.wait_ge(S["hidT_ps"], 2 * j + b + 1)
                    nc.scalar.activation(gh[:, 0:4, b * P:(b + 1) * P], ps[:, 6 + b, :].rearrange("p (k m) -> p k m", k=4),
                                         ACT.Copy).then_inc(S["gh_done"], 1)
            feed(last_of("w2", MLP_CHUNKS - 1))
            squares(2)

            ghv = 2 * MLP_CHUNKS
            for layer in range(LAYERS):
                n, t = 3 + 3 * layer, 2 + 4 * layer
                squares(n)
                feed(units_of(("mla", layer))[0])
                high_T(t)
                feed(last_of(("mla", layer)))
                product(act, ("mla", layer))
                for b in range(NB):
                    nc.scalar.activation(cn[:, b, 0:QL], ps[:, 2 * b, 0:QL], ACT.Square,
                                         accum_out=lss[:, b, 0:1]).then_inc(S["lora_sq"], 1)
                    nc.scalar.activation(cn[:, b, QL:QL + KVL], ps[:, 2 * b + 1, 0:KVL], ACT.Square,
                                         accum_out=lss[:, b, 1:2]).then_inc(S["lora_sq"], 1)
                for b in range(NB):
                    nc.scalar.activation(q7[:, b, HM, NOPE:QK], ps[:, 2 * b + 1, KVL:KVL + ROPE],
                                         ACT.Copy).then_inc(S["kr_done"], 1)
                feed(last_of(("idx", layer)))
                last_g = last_of("w2", MLP_CHUNKS - 1) if layer == 0 else last_of(("proj", layer - 1))
                act.wait_ge(S["used"], last_g["index"] + 1)
                act.wait_ge(S["cnT_ps"], layer + 1)
                nc.scalar.activation(gh[:].rearrange("p k m -> p (k m)"), ps[:, 0:3, :].rearrange("p a c -> p (a c)")[:, 0:5 * SEQ],
                                     ACT.Copy).then_inc(S["gh_done"], 1)
                ghv += 1
                product(act, ("idx", layer))
                nc.scalar.activation(iqT, ps[:, 4:6, :].rearrange("p a (t q) -> p (a t) q", t=2),
                                     ACT.Copy).then_inc(S["iqT_done"], 1)
                act.wait_ge(S["ikT_ps"], layer + 1)
                nc.scalar.activation(ikT, ps[:, 3, 0:SEQ], ACT.Copy).then_inc(S["ikT_done"], 1)
                feed(last_of(("dsa", layer)))
                product(act, ("dsa", layer))
                nc.scalar.activation(dT[:, 0:2, :], ps[:, 6, :].rearrange("p (t q) -> p t q", t=2),
                                     ACT.Copy).then_inc(S["dsa_evac"], 1)
                nc.scalar.activation(dT[0:DH, 2, :], ps[0:DH, 7, 0:SEQ], ACT.Copy).then_inc(S["dsa_evac"], 1)
                nc.scalar.activation(dkT[DH:P, :], ps[DH:P, 7, 0:SEQ], ACT.Copy).then_inc(S["dsa_evac"], 1)
                nc.scalar.activation(dkT[0:DH, :], ps[DH:P, 7, 0:SEQ], ACT.Copy).then_inc(S["dsa_evac"], 1)
                nc.scalar.activation(dv, ps[:, 7, SEQ:SEQ + 2 * DH].rearrange("p (b d) -> p b d", b=NB),
                                     ACT.Copy).then_inc(S["dsa_evac"], 1)
                product(act, ("uq", layer))
                for b in range(NB):
                    nc.scalar.activation(q7[:, b, 0:HM, :].rearrange("p h d -> p (h d)").rearrange("p (a c) -> p a c", a=2),
                                         ps[:, 2 * b:2 * b + 2, 0:UQ_COLS // 2], ACT.Copy).then_inc(S["q7_done"], 1)
                act.wait_ge(S["isc_ps"], 2 * layer + 1)
                nc.scalar.activation(relu1, ps[:, 4:8, :].rearrange("p a (t q) -> p (a t) q", t=2), ACT.Relu,
                                     scale=DH ** -0.5).then_inc(S["relu_i"], 1)
                feed(last_of(("uq", layer)))
                act.wait_ge(S["isc_ps"], 2 * layer + 2)
                nc.scalar.activation(relu0, ps[:, 4:6, :].rearrange("p a (t q) -> p (a t) q", t=4), ACT.Relu,
                                     scale=DH ** -0.5).then_inc(S["relu_i"], 1)
                feed(last_of(("ukv", layer)))
                feed(last_of(("sb", layer)), 1)
                act.wait_ge(S["rope_done"], 2 * layer + 2)
                act.wait_ge(S["kv_done"], 4 * layer + 4)
                for b in range(NB):
                    nc.scalar.activation(kfull[:, b, :, NOPE:QK], q7[:, b, HM:HM + 1, NOPE:QK].broadcast_to([P, HM, ROPE]),
                                         ACT.Copy).then_inc(S["kf_done"], 1)
                feed(last_of(("sb", layer)))
                product(act, ("sb", layer))
                nc.scalar.activation(sT[:, 0:2, :], ps[:, 6, :].rearrange("p (t q) -> p t q", t=2), ACT.Copy,
                                     scale=DH ** -0.5).then_inc(S["sb_evac"], 1)
                nc.scalar.activation(sT[:, 2:4, :], ps[:, 7, :].rearrange("p (t q) -> p t q", t=2),
                                     ACT.Copy).then_inc(S["sb_evac"], 1)
                act.wait_ge(S["qkT_ps"], 2 * layer + 1)
                nc.scalar.activation(qT[0:QK].rearrange("p h q -> p (h q)"), ps[0:QK, 0:3, :].rearrange("p a c -> p (a c)"),
                                     ACT.Copy).then_inc(S["qT_done"], 1)
                feed(last_of(("sv", layer)), 1)
                for i, b in enumerate((1, 0)):
                    act.wait_ge(S["m_nm"], 2 * layer + i + 1)
                    for hh in range(HM):
                        src = (ps[:, 0:3, :].rearrange("p a (t k) -> p (a t) k", t=2)[:, hh, :] if b else
                               ps[:, 3:5, :].rearrange("p a (t k) -> p (a t) k", t=4)[:, hh, :])
                        k = HM * b + hh
                        nc.scalar.activation(pm[b][:, hh, :], src, ACT.Exp, scale=QK ** -0.5, bias=neg_max[:, k:k + 1],
                                             accum_out=row_sum[:, k:k + 1]).then_inc(S["m_exp"], 1)
                product(act, ("sv", layer))
                nc.scalar.activation(sT[0:DH, 4, :], ps[0:DH, 6, 0:SEQ], ACT.Copy, scale=DH ** -0.5).then_inc(S["c4_evac"], 1)
                nc.scalar.activation(sT[0:DH, 5, :], ps[DH:P, 6, 0:SEQ], ACT.Copy).then_inc(S["c4_evac"], 1)
                feed(last_of(("sv", layer)))
                for g, (heads, banks) in enumerate(SB_GROUPS):
                    at = len(SB_GROUPS) * layer + g + 1
                    act.wait_ge(S["s_z"], at)
                    nc.scalar.activation(sbt[:, heads, :], ps[:, banks, 0:3 * P], ACT.Abs).then_inc(S["s_abs"], 1)
                    act.wait_ge(S["s_abs"], at)
                    nc.scalar.activation(sbt[:, heads, :], sbt[:, heads, :], ACT.Exp, scale=-1.0).then_inc(S["s_e"], 1)
                    act.wait_ge(S["s_e"], at)
                    nc.scalar.activation(sbt[:, heads, :], sbt[:, heads, :], ACT.Ln, bias=1.0).then_inc(S["s_ln"], 1)
                for g, (heads, banks) in enumerate(SB_GROUPS):
                    act.wait_ge(S["s_zs"], len(SB_GROUPS) * layer + g + 1)
                    nc.scalar.activation(sbt[:, heads, :], ps[:, banks, 0:3 * P], ACT.Exp).then_inc(S["s_w"], 1)
                for i, b in enumerate((1, 0)):
                    act.wait_ge(S["d_nm"], 2 * layer + i + 1)
                    for k in range(HD):
                        c, head = HD * b + k, HD * b + ORDER5[k]
                        nc.scalar.activation(pd[b][:, k, :], pd[b][:, k, :], ACT.Exp, bias=neg_max[:, c:c + 1],
                                             accum_out=row_sum[:, head:head + 1]).then_inc(S["d_exp"], 1)
                act.wait_ge(S["d_pT_ps"], 2 * layer + 1)
                nc.scalar.activation(pdT[1], ps[:, 2:5, :].rearrange("p a c -> p (a c)")[:, 0:2 * HD * P],
                                     ACT.Copy).then_inc(S["d_pT"], 1)
                high_T(t + 1)
                feed(last_of(("wo", layer)))
                squares(n + 1)
                high_T(t + 2)
                for j in range(FF_CHUNKS):
                    feed(last_of(("gu", layer), j))
                    for b in range(NB):
                        k = FF_CHUNKS * layer + j
                        block_product(act, "gu_ps", k + 1, b, ("gu", layer), j)
                        if k:
                            act.wait_ge(S["hid_g"], 2 * (k - 1) + b + 1)
                        act.wait_ge(S["rstd_done"], nval(n + 1, b))
                        scale = rstd[:, 2 * ((n + 1) % 2) + b:2 * ((n + 1) % 2) + b + 1]
                        nc.scalar.activation(silu2[:, b, :], ps[:, 4 + b, 0:FF_CHUNK], ACT.Silu,
                                             scale=scale).then_inc(S["silu_g"], 1)
                    if j:
                        feed(last_of(("dn", layer), j - 1))
                        if j == EMBED_AT:
                            act.wait_ge(S["in_p"], 16 * (layer + 1))
                            act.wait_ge(S["used"], last_of(("ukv", layer))["index"] + 1)
                            nc.scalar.activation(gh[:, 2:4, :], pT, ACT.Copy).then_inc(S["ph_done"], 1)
                        act.wait_ge(S["used"], last_of(("dn", layer), j - 1)["index"] + 1)
                    else:
                        act.wait_ge(S["used"], last_of(("ukv", layer))["index"] + 1)
                    for b in range(NB):
                        act.wait_ge(S["hidT_ps"], 2 * (MLP_CHUNKS + FF_CHUNKS * layer + j) + b + 1)
                        nc.scalar.activation(gh[:, 0:2, b * P:(b + 1) * P],
                                             ps[:, 6 + b, 0:2 * P].rearrange("p (k m) -> p k m", k=2),
                                             ACT.Copy).then_inc(S["gh_done"], 1)
                feed(last_of(("dn", layer), FF_CHUNKS - 1))
                squares(n + 2)
                feed(last_of(("proj", layer)))
                act.wait_ge(S["proj_ps"], layer + 1)
                nc.scalar.activation(pp[:, 0, :], ps[:, 4:6, :].rearrange("p a c -> p (a c)"), ACT.Copy).then_inc(S["proj_evac0"], 1)
                high_T(t + 3)
                feed(last_of(("gate", layer)))
                for b in range(NB):
                    block_product(act, "gate_ps", layer + 1, b, ("gate", layer))
                    act.wait_ge(S["rstd_done"], nval(n + 2, b))
                    k = 2 * ((n + 2) % 2) + b
                    nc.scalar.activation(sg[:, b, :], ps[:, 2 * b:2 * b + 2, :].rearrange("p a c -> p (a c)"),
                                         ACT.Sigmoid, scale=rstd[:, k:k + 1]).then_inc(S["sig_g"], 1)
            squares(LAST)

        @block.gpsimd
        def _(pool):
            nc.gpsimd.memset(pow_half[:], -0.5).then_inc(S["init_p"], 1)
            nc.gpsimd.memset(neg_ones[:], -1.0).then_inc(S["init_p"], 1)
            nc.gpsimd.memset(one["ones"], 1.0 / D).then_inc(S["init_p"], 1)
            nc.gpsimd.memset(epsilon[:], EPS).then_inc(S["init_p"], 1)
            nc.gpsimd.memset(upad, 0.0).then_inc(S["init_p"], 1)
            pool.wait_ge(S["init_p"], 5)

            def rstds(n):
                for b in range(NB):
                    k = 2 * (n % 2) + b
                    pool.wait_ge(S["sumsq"], nval(n, b))
                    nc.gpsimd.tensor_scalar(var[:, k:k + 1], ss[:, k:k + 1], 1.0 / D, EPS, ALU.mult,
                                            ALU.add).then_inc(S["var_done"], 1)
                    pool.wait_ge(S["var_done"], nval(n, b))
                    nc.gpsimd.tensor_tensor(rstd[:, k:k + 1], var[:, k:k + 1], pow_half[:, 0:1],
                                            ALU.pow).then_inc(S["rstd_done"], 1)

            rstds(0)
            acc = cv[:, POOL_TILES[0]:POOL_TILES[-1] + 1, :]
            pool.wait_ge(S["conv_first"], len(POOL_TILES))
            for k in range(1, TAPS):
                pool.wait_ge(S["tap_ready"], len(POOL_TILES) * k)
                if k > 1:
                    pool.wait_ge(S["tap_added"], k - 1)
                nc.gpsimd.tensor_tensor(acc, acc, taps[:, (k - 1) % PRODUCTS], ALU.add).then_inc(S["tap_added"], 1)
            rstds(1)
            rstds(2)
            for layer in range(LAYERS):
                n = 3 + 3 * layer
                rstds(n)
                pool.wait_ge(S["lora_sq"], 4 * layer + 4)
                nc.gpsimd.tensor_scalar(lvar[:, :, 0], lss[:, :, 0], 1.0 / QL, EPS, ALU.mult, ALU.add).then_inc(S["lora_var"], 1)
                nc.gpsimd.tensor_scalar(lvar[:, :, 1], lss[:, :, 1], 1.0 / KVL, EPS, ALU.mult, ALU.add).then_inc(S["lora_var"], 1)
                pool.wait_ge(S["lora_var"], 2 * layer + 2)
                nc.gpsimd.tensor_tensor(lrstd[:].rearrange("p b c -> p (b c)"), lvar[:].rearrange("p b c -> p (b c)"),
                                        pow_half[:], ALU.pow).then_inc(S["lora_rstd"], 1)
                rstds(n + 1)
                rstds(n + 2)
            rstds(LAST)

        @block.vector
        def _(dve):
            fed = [0]

            def feed(unit, ahead=LOOKAHEAD):
                while fed[0] < min(unit["s"] + 1 + ahead, len(SPLIT)):
                    u = SPLIT[fed[0]]
                    n = u["kts"] * u["cols"]
                    slot = u["s"] % SPLIT_SLOTS
                    dve.wait_ge(S["hi_done"], u["s"] + 1)
                    nc.vector.tensor_tensor(lo[:, slot, 0:n], raw[:, u["slot"], 0:n], hi[:, slot, 0:n].bitcast(F32),
                                            ALU.subtract).then_inc(S["lo_done"], 1)
                    fed[0] += 1

            def normalise(n):
                for b in range(NB):
                    k = 2 * (n % 2) + b
                    dve.wait_ge(S["in_gain"], 16 * n)
                    dve.wait_ge(S["rstd_done"], nval(n, b))
                    dst = h if n == 2 else xs
                    i = nc.vector.scalar_tensor_tensor(out=dst[:, b, :], in0=h[:, b, :], scalar=rstd[:, k:k + 1],
                                                       in1=gain[:, n % 2, :], op0=ALU.mult, op1=ALU.mult)
                    if n == 1:
                        i.then_inc(S["xs_mid"], 1)
                        dve.wait_ge(S["xs_mid"], b + 1)
                        i = nc.vector.tensor_tensor(xs[:, b, :], xs[:, b, :], one["shift"], ALU.add)
                    i.then_inc(S["h_ready"] if n == 2 else S["xs_ready"], 1)

            def low_T(t):
                for b in range(NB):
                    bank = 4 + 2 * b
                    dve.wait_ge(S["xh_ready"], tval(t, b))
                    sl = slice(b * P, (b + 1) * P)
                    nc.vector.tensor_tensor(xl[:, :, sl], ps[:, bank:bank + 2, :].rearrange("p a (k m) -> p (a k) m", k=4),
                                            xh[:, :, sl].bitcast(F32), ALU.subtract).then_inc(S["xl_ready"], 1)

            def mod_gain(v, n):
                product(dve, ("mod", v), 3)
                src = ps[:, MOD_BANK[v]:MOD_BANK[v] + 2, :].rearrange("p a c -> p (a c)")
                nc.vector.scalar_tensor_tensor(out=gain[:, n, :], in0=src, scalar=1.0, in1=gain[:, n, :], op0=ALU.add,
                                               op1=ALU.mult).then_inc(S["mod_mid"], 1)
                dve.wait_ge(S["mod_mid"], n + 1)

            dve.wait_ge(S["silu_c"], 1)
            nc.vector.tensor_copy(csb, vec[:, V_C:V_C + KT].rearrange("p (k a) -> p k a", a=1).broadcast_to([P, KT, P]))\
                .then_inc(S["csb_done"], 1)
            n = len(ROWS)
            dve.wait_ge(S["in_rows"], 16)
            nc.vector.tensor_copy(brows, rows_raw).then_inc(S["pick_done"], 1)
            dve.wait_ge(S["pick_done"], 1)
            low_rows = slice(LOW_ROW, LOW_ROW + n)
            nc.vector.tensor_tensor(brows[low_rows], rows_raw[low_rows], brows[low_rows].bitcast(F32),
                                    ALU.subtract).then_inc(S["pick_done"], 1)
            dve.wait_ge(S["in_consts"], 16)
            first_ones, second_ones = (ident[0:LOW_ROW + n, c:c + n].rearrange("p (i a) -> p i a", a=1)
                                       .broadcast_to([LOW_ROW + n, n, P]) for c in (0, LOW_ROW))
            nc.vector.tensor_tensor(pick, first_ones, second_ones, ALU.add).then_inc(S["pick_done"], 1)
            for dst, c in ((ident16[:], C_ID), (masks16[:, 0, :], C_CAUSAL), (masks16[:, 1, :], C_STRICT)):
                nc.vector.tensor_copy(dst, table[:, c:c + P]).then_inc(S["masks_done"], 1)
            dve.wait_ge(S["in_rel"], 32)
            nc.vector.tensor_copy(rbb, rb.rearrange("p (h a) -> p h a", a=1).broadcast_to([BUCKETS + 1, HD, P]))\
                .then_inc(S["relb_done"], 1)
            dve.wait_ge(S["gain_row"], 1)
            mod_gain(0, 0)
            for b in range(NB):
                dve.wait_ge(S["rstd_done"], nval(0, b))
                nc.vector.scalar_tensor_tensor(out=xs[:, b, :], in0=h[:, b, :], scalar=rstd[:, b:b + 1],
                                               in1=gain[:, 0, :], op0=ALU.mult, op1=ALU.mult).then_inc(S["scaled"], 1)
            feed(units_of("pw1", 0)[0], 1)
            product(dve, ("mod", 1), 3)
            for b in range(NB):
                dve.wait_ge(S["scaled"], b + 1)
                src = ps[:, MOD_BANK[1]:MOD_BANK[1] + 2, :].rearrange("p a c -> p (a c)")
                nc.vector.tensor_tensor(xs[:, b, :], xs[:, b, :], src, ALU.add).then_inc(S["xs_ready"], 1)
            low_T(0)

            def gate_values(f):
                feed(units_of("pw1", f)[0], min(LOOKAHEAD, KT - 1 - f))
                dve.wait_ge(S["sig_done"], f + 1)
                nc.vector.scalar_tensor_tensor(out=upad[:, f, :, HALO:HALO + SEG],
                                               in0=ps[:, 4 + f % 4, 0:SEQ].rearrange("p (s t) -> p s t", s=SEGS),
                                               scalar=vec[:, V_BPW1 + f:V_BPW1 + f + 1],
                                               in1=sig[:, f % GATES, :].rearrange("p (s t) -> p s t", s=SEGS),
                                               op0=ALU.add, op1=ALU.mult).then_inc(S["glu_done"], 1)

            steps = [0]

            def convolve(g, k0, k1):
                for k in range(k0, k1):
                    for f in DVE_GROUPS[g]:
                        acc = cv[:, f, :].rearrange("p (s t) -> p s t", s=SEGS)
                        src = upad[:, f, :, k:k + SEG]
                        if k == 0:
                            dve.wait_ge(S["glu_done"], f + 1)
                            ins = nc.vector.tensor_scalar(acc, src, dw[:, f, 0:1], vec[:, V_BDW + f:V_BDW + f + 1],
                                                          ALU.mult, ALU.add)
                        else:
                            dve.wait_ge(S["conv_step"], steps[0] - len(DVE_GROUPS[g]) + 1)
                            ins = nc.vector.scalar_tensor_tensor(out=acc, in0=src, scalar=dw[:, f, k:k + 1], in1=acc,
                                                                 op0=ALU.mult, op1=ALU.add)
                        ins.then_inc(S["conv_step"], 1)
                        steps[0] += 1

            done = 0
            for f in range(KT):
                gate_values(f)
                if DVE_GROUPS[0][-1] <= f < KT - 1:
                    convolve(0, done, done + 3)
                    done += 3
            convolve(0, done, TAPS)
            convolve(1, 0, TAPS)
            dve.wait_ge(S["mean_ps"], 1)
            for i in range(2):
                half = cv[:, i * KT // 2:(i + 1) * KT // 2, :]
                mean = ps[:, 6, 0:SEQ].rearrange("p (a t) -> p a t", a=1).broadcast_to([P, KT // 2, SEQ])
                nc.vector.tensor_tensor(half, half, mean, ALU.subtract).then_inc(S["cent_done"], 1)
            feed(units_of("pw2")[0], 0)
            dve.wait_ge(S["deviation"], 1)
            nc.vector.reciprocal(one["rs"], one["rs"]).then_inc(S["ln_scale"], 1)
            dve.wait_ge(S["ln_scale"], 1)

            def low_silu(i):
                pair = slice(2 * i, 2 * i + 2)
                dve.wait_ge(S["yh_done"], i + 1)
                nc.vector.tensor_tensor(xl[:, pair, :], sq[:, pair, :], xh[:, pair, :].bitcast(F32),
                                        ALU.subtract).then_inc(S["yl_done"], 1)

            for i in range(KT // 2):
                pair = cv[:, 2 * i:2 * i + 2, :]
                nc.vector.tensor_tensor(pair, pair, one["rs"].rearrange("p (a t) -> p a t", a=1).broadcast_to([P, 2, SEQ]),
                                        ALU.mult).then_inc(S["ln_done"], 1)
                if i:
                    low_silu(i - 1)
            low_silu(KT // 2 - 1)
            dve.wait_ge(S["in_gain"], 16)
            mod_gain(4, 1)
            feed(last_of("pw2"), 0)

            rstep = [0]

            def residual(done, value, stage, index, scale_row, n=None):
                for b in range(NB):
                    block_product(dve, done, value, b, stage, index)
                    src = ps[:, 2 * b:2 * b + 2, :].rearrange("p a c -> p (a c)")
                    if scale_row is None:
                        nc.vector.tensor_tensor(h[:, b, :], src, h[:, b, :], ALU.add).then_inc(S["h_ready"], 1)
                        dve.wait_ge(S["h_ready"], hval(n, b))
                        dve.wait_ge(S["in_gain"], 16 * n)
                        nc.vector.tensor_tensor(xs[:, b, :], h[:, b, :], gain[:, n % 2, :], ALU.mult).then_inc(S["xs_ready"], 1)
                    else:
                        nc.vector.tensor_tensor(xs[:, b, :], src, scale_row, ALU.mult).then_inc(S["res_step"], 1)
                        rstep[0] += 1
                        dve.wait_ge(S["res_step"], rstep[0])
                        nc.vector.tensor_tensor(h[:, b, :], xs[:, b, :], h[:, b, :], ALU.add).then_inc(S["h_ready"], 1)

            dve.wait_ge(S["mod_evac"], 1)
            residual("pw2_ps", 1, "pw2", 0, one["g1"])
            dve.wait_ge(S["mod_evac"], 2)
            normalise(1)
            feed(units_of("w1", 0)[0], 0)
            low_T(1)
            for j in range(MLP_CHUNKS):
                feed(last_of("w1", j))
                if j:
                    feed(last_of("w2", j - 1))
                for b in range(NB):
                    sl = slice(b * P, (b + 1) * P)
                    dve.wait_ge(S["gh_done"], 2 * j + b + 1)
                    nc.vector.tensor_tensor(gl[:, 0:4, sl], ps[:, 6 + b, :].rearrange("p (k m) -> p k m", k=4),
                                            gh[:, 0:4, sl].bitcast(F32), ALU.subtract).then_inc(S["gl_done"], 1)
            feed(last_of("w2", MLP_CHUNKS - 1))
            dve.wait_ge(S["mod_evac"], 3)
            residual("mlp_ps", 1, "w2", MLP_CHUNKS - 1, one["g2"])
            normalise(2)

            for layer in range(LAYERS):
                n, t = 3 + 3 * layer, 2 + 4 * layer
                ghv = 2 * MLP_CHUNKS + (1 + 2 * FF_CHUNKS) * layer
                normalise(n)
                feed(last_of(("mla", layer)), -2)
                low_T(t)
                feed(last_of(("mla", layer)))
                dve.wait_ge(S["lora_rstd"], layer + 1)
                dve.wait_ge(S["in_lora"], 16 * (layer + 1))
                dve.wait_ge(S["kr_done"], 2 * layer + 2)
                for b in range(NB):
                    for c, (a, z) in enumerate(((0, QL), (QL, QL + KVL))):
                        nc.vector.scalar_tensor_tensor(out=cn[:, b, a:z], in0=ps[:, 2 * b + c, 0:z - a],
                                                       scalar=lrstd[:, b, c:c + 1], in1=lora_gain[:, a:z],
                                                       op0=ALU.mult, op1=ALU.mult).then_inc(S["cn_done"], 1)
                feed(last_of(("idx", layer)))
                product(dve, ("idx", layer))
                for c in range(2):
                    nc.vector.tensor_copy(ikd[:, :, c * DH:(c + 1) * DH], ps[:, 6:8, 0:DH]).then_inc(S["ikd_done"], 1)
                nc.vector.tensor_scalar(iw[:], ps[:, 6:8, DH:DH + HI], HI ** -0.5, None, ALU.mult).then_inc(S["iw_done"], 1)
                dve.wait_ge(S["gh_done"], ghv + 1)
                nc.vector.tensor_tensor(gl[:].rearrange("p k m -> p (k m)"),
                                        ps[:, 0:3, :].rearrange("p a c -> p (a c)")[:, 0:5 * SEQ],
                                        gh[:].rearrange("p k m -> p (k m)").bitcast(F32), ALU.subtract).then_inc(S["gl_done"], 1)
                feed(last_of(("dsa", layer)))
                feed(last_of(("uq", layer)))

                istep = [16 * layer]
                tstep = [2 * NB * layer * (TOPK // 8)]

                def index_scores(b):
                    r, order = ((relu1, ORDER8) if b else (relu0, ORDER8_B0))
                    dve.wait_ge(S["relu_i"], 2 * layer + (1 if b else 2))
                    if b:
                        dve.wait_ge(S["iw_done"], layer + 1)
                    for k in range(HI):
                        if k:
                            dve.wait_ge(S["isc_step"], istep[0])
                        head = order[k]
                        in1 = work[b] if k else (cmask if b else cmask[:, P:])
                        nc.vector.scalar_tensor_tensor(out=work[b], in0=r[:, k, :], scalar=iw[:, b, head:head + 1],
                                                       in1=in1, op0=ALU.mult, op1=ALU.add).then_inc(S["isc_step"], 1)
                        istep[0] += 1
                    dve.wait_ge(S["isc_step"], istep[0])

                def top_keys(r0, r1):
                    for r in range(r0, r1):
                        for b in (1, 0):
                            if r:
                                dve.wait_ge(S["topk_step"], tstep[0] - 1)
                            nc.vector.max(top8[:, b, :], work[b]).then_inc(S["topk_step"], 1)
                            tstep[0] += 1
                        for b in (1, 0):
                            dve.wait_ge(S["topk_step"], tstep[0] - 1)
                            nc.vector.match_replace(work[b], top8[:, b, :], work[b], TAKEN).then_inc(S["topk_step"], 1)
                            tstep[0] += 1

                index_scores(1)
                feed(last_of(("ukv", layer)))
                index_scores(0)
                product(dve, ("ukv", layer))
                for b in range(NB):
                    src = ps[:, 2 * b:2 * b + 2, 0:UKV_COLS // 2].rearrange("p a (h d) -> p a h d", h=3)
                    nc.vector.tensor_copy(mv[:, b, :, :].rearrange("p (a h) d -> p a h d", a=2),
                                          src[:, :, :, NOPE:NOPE + VD]).then_inc(S["kv_done"], 1)
                    nc.vector.tensor_copy(kfull[:, b, :, 0:NOPE].rearrange("p (a h) d -> p a h d", a=2),
                                          src[:, :, :, 0:NOPE]).then_inc(S["kv_done"], 1)
                dve.wait_ge(S["q7_done"], 2 * layer + 2)
                dve.wait_ge(S["kr_done"], 2 * layer + 2)
                x1 = q7[:, :, :, NOPE:NOPE + HALF]
                x2 = q7[:, :, :, NOPE + HALF:QK]
                co = cosines.rearrange("p b (a d) -> p b a d", a=1).broadcast_to([P, NB, 7, HALF])
                si = sines.rearrange("p b (a d) -> p b a d", a=1).broadcast_to([P, NB, 7, HALF])
                for i, (xx, cs) in enumerate(((x1, co), (x2, si), (x1, si), (x2, co))):
                    nc.vector.tensor_tensor(rt[:, i], xx, cs, ALU.mult).then_inc(S["rope_t"], 1)
                dve.wait_ge(S["rope_t"], 4 * layer + 4)
                nc.vector.tensor_tensor(x1, rt[:, 0], rt[:, 1], ALU.subtract).then_inc(S["rope_done"], 1)
                nc.vector.tensor_tensor(x2, rt[:, 2], rt[:, 3], ALU.add).then_inc(S["rope_done"], 1)
                feed(last_of(("sb", layer)), 1)
                top_keys(0, 2)
                feed(last_of(("sb", layer)))
                dve.wait_ge(S["qkT_ps"], 2 * layer + 2)
                nc.vector.tensor_copy(kT[0:QK].rearrange("p h q -> p (h q)"),
                                      ps[0:QK, 3:6, :].rearrange("p a c -> p (a c)")).then_inc(S["kT_done"], 1)
                feed(last_of(("sv", layer)), 1)
                for i, b in enumerate((1, 0)):
                    dve.wait_ge(S["m_sc"], 2 * layer + i + 1)
                    src = (ps[:, 0:3, :].rearrange("p a (t k) -> p (a t) k", t=2) if b else
                           ps[:, 3:5, :].rearrange("p a (t k) -> p (a t) k", t=4)[:, 0:HM, :])
                    nc.vector.tensor_reduce(row_max[:, HM * b:HM * (b + 1)], src, AX.X, ALU.max).then_inc(S["m_max"], 1)
                    dve.wait_ge(S["m_max"], 2 * layer + i + 1)
                    nc.vector.tensor_scalar(neg_max[:, HM * b:HM * (b + 1)], row_max[:, HM * b:HM * (b + 1)],
                                            -QK ** -0.5, None, ALU.mult).then_inc(S["m_nm"], 1)
                top_keys(2, 5)
                product(dve, ("sv", layer))
                nc.vector.tensor_copy(sv[:, 0, :], ps[:, 7, 0:SV]).then_inc(S["sv_evac"], 1)
                nc.vector.tensor_copy(sv[:, 1, 0:3 * DH], ps[:, 7, SV:512]).then_inc(S["sv_evac"], 1)
                dve.wait_ge(S["c4_evac"], 2 * layer + 2)
                nc.vector.tensor_copy(sv[:, 1, 3 * DH:SV], ps[:, 6, SEQ:SEQ + 2 * DH]).then_inc(S["sv_evac"], 1)
                dve.wait_ge(S["m_pT_ps"], 2 * layer + 1)
                nc.vector.tensor_copy(pmT[1], ps[:, 0:3, :].rearrange("p a c -> p (a c)")).then_inc(S["m_pT"], 1)
                top_keys(5, 6)
                dve.wait_ge(S["m_pT_ps"], 2 * layer + 2)
                nc.vector.tensor_copy(pmT[0], ps[:, 3:5, :].rearrange("p a c -> p (a c)")[:, 0:HM * P]).then_inc(S["m_pT"], 1)
                dve.wait_ge(S["m_exp"], 2 * HM * (layer + 1))
                nc.vector.reciprocal(row_inv[:], row_sum[:]).then_inc(S["m_inv"], 1)
                dve.wait_ge(S["m_inv"], layer + 1)
                top_keys(6, 7)

                def mix_out(name, o, banks, at, heads, inv, between=None):
                    for i, b in enumerate((1, 0)):
                        if i and between:
                            between()
                        dve.wait_ge(S[o], 2 * layer + i + 1)
                        dst = xs[:, b, at:at + heads * DH].rearrange("p (h d) -> p h d", h=heads)
                        src = ps[:, banks[b], 0:heads * DH].rearrange("p (h d) -> p h d", h=heads)
                        if inv is None:
                            nc.vector.tensor_copy(dst, src).then_inc(S[name], 1)
                        else:
                            r = row_inv[:, heads * b:heads * (b + 1)].rearrange("p (h a) -> p h a", a=1)
                            nc.vector.tensor_tensor(dst, src, r.broadcast_to([P, heads, DH]), ALU.mult).then_inc(S[name], 1)

                mix_out("mix_m", "m_o", [3, 2], 0, HM, True, between=lambda: top_keys(7, TOPK // 8))

                def softplus(g):
                    heads, banks = SB_GROUPS[g]
                    dve.wait_ge(S["s_ln"], len(SB_GROUPS) * layer + g + 1)
                    nc.vector.scalar_tensor_tensor(out=sbt[:, heads, :], in0=ps[:, banks, 0:3 * P], scalar=0.0,
                                                   in1=sbt[:, heads, :], op0=ALU.max, op1=ALU.add).then_inc(S["s_sp"], 1)

                softplus(0)
                for b in (1, 0):
                    dve.wait_ge(S["topk_step"], tstep[0] - (1 if b else 0))
                    nc.vector.tensor_scalar(work[b], work[b], 0.5 * TAKEN, NEG, ALU.is_gt, ALU.mult).then_inc(S["sel_done"], 1)
                softplus(1)

                def dsa_scores(i, b):
                    nk = P * (b + 1)
                    dve.wait_ge(S["d_sc"], 2 * layer + i + 1)
                    bank = 2 if b else 5
                    src = ps[:, bank:bank + 3, :].rearrange("p a (t k) -> p (a t) k", t=2)[:, 0:HD, 0:nk]
                    bs = bias[:, :, 0:2 * P] if b else bias[:, :, P:2 * P]
                    nc.vector.scalar_tensor_tensor(out=pd[b], in0=src, scalar=DH ** -0.5, in1=bs, op0=ALU.mult,
                                                   op1=ALU.add).then_inc(S["d_b"], 1)
                    dve.wait_ge(S["d_b"], 2 * layer + i + 1)
                    dve.wait_ge(S["sel_done"], 2 * layer + 2)
                    chosen = work[b].rearrange("p (a k) -> p a k", a=1).broadcast_to([P, HD, nk])
                    nc.vector.tensor_tensor(pd[b], pd[b], chosen, ALU.add).then_inc(S["d_s"], 1)
                    dve.wait_ge(S["d_s"], 2 * layer + i + 1)
                    nc.vector.tensor_reduce(neg_max[:, HD * b:HD * (b + 1)], pd[b], AX.X, ALU.max,
                                            negate=True).then_inc(S["d_nm"], 1)

                dsa_scores(0, 1)
                dsa_scores(1, 0)
                mix_out("mix_s", "s_o", [1, 0], (HM + HD) * DH, HS, None)
                dve.wait_ge(S["d_exp"], 2 * HD * (layer + 1))
                nc.vector.reciprocal(row_inv[:, 0:2 * HD], row_sum[:, 0:2 * HD]).then_inc(S["d_inv"], 1)
                dve.wait_ge(S["d_pT_ps"], 2 * layer + 2)
                nc.vector.tensor_copy(pdT[0], ps[:, 5:7, :].rearrange("p a c -> p (a c)")[:, 0:HD * P]).then_inc(S["d_pT"], 1)
                dve.wait_ge(S["d_inv"], layer + 1)
                mix_out("mix_d", "d_o", [2, 7], HM * DH, HD, True)
                feed(last_of(("wo", layer)), -2)
                low_T(t + 1)
                feed(last_of(("wo", layer)))
                residual("wo_ps", layer + 1, ("wo", layer), 0, None, n + 1)
                low_T(t + 2)
                for j in range(FF_CHUNKS):
                    feed(last_of(("gu", layer), j))
                    for b in range(NB):
                        k = FF_CHUNKS * layer + j
                        dve.wait_ge(S["silu_g"], 2 * k + b + 1)
                        if j:
                            dve.wait_ge(S["hidT_ps"], 2 * (MLP_CHUNKS + k - 1) + b + 1)
                        scale = rstd[:, 2 * ((n + 1) % 2) + b:2 * ((n + 1) % 2) + b + 1]
                        nc.vector.scalar_tensor_tensor(out=hid2[:, b, :], in0=ps[:, 4 + b, FF_CHUNK:2 * FF_CHUNK],
                                                       scalar=scale, in1=silu2[:, b, :], op0=ALU.mult,
                                                       op1=ALU.mult).then_inc(S["hid_g"], 1)
                    if j:
                        feed(last_of(("dn", layer), j - 1))
                        if j == EMBED_AT:
                            dve.wait_ge(S["ph_done"], layer + 1)
                            nc.vector.tensor_tensor(gl[:, 2:4, :], pT, gh[:, 2:4, :].bitcast(F32),
                                                    ALU.subtract).then_inc(S["pl_done"], 1)
                    for b in range(NB):
                        sl = slice(b * P, (b + 1) * P)
                        dve.wait_ge(S["gh_done"], ghv + 1 + 2 * j + b + 1)
                        nc.vector.tensor_tensor(gl[:, 0:2, sl], ps[:, 6 + b, 0:2 * P].rearrange("p (k m) -> p k m", k=2),
                                                gh[:, 0:2, sl].bitcast(F32), ALU.subtract).then_inc(S["gl_done"], 1)
                feed(last_of(("dn", layer), FF_CHUNKS - 1))
                residual("dn_ps", layer + 1, ("dn", layer), FF_CHUNKS - 1, None, n + 2)
                product(dve, ("proj", layer))
                nc.vector.tensor_copy(pp[:, 1, :], ps[:, 6:8, :].rearrange("p a c -> p (a c)")).then_inc(S["proj_evac1"], 1)
                low_T(t + 3)
                feed(last_of(("gate", layer)))
                for b in range(NB):
                    dve.wait_ge(S["sig_g"], 2 * layer + b + 1)
                    dve.wait_ge(S[f"proj_evac{b}"], layer + 1)
                    nc.vector.tensor_tensor(sg[:, b, :], sg[:, b, :], pp[:, b, :], ALU.mult).then_inc(S["gmul"], 1)
                    dve.wait_ge(S["gmul"], 2 * layer + b + 1)
                    nc.vector.tensor_tensor(h[:, b, :], h[:, b, :], sg[:, b, :], ALU.add).then_inc(S["h_ready"], 1)
            normalise(LAST)

        @block.tensor
        def _(pe):
            def used(ins, u):
                ins.then_inc(S["used"], 1)

            def parts(u):
                n = u["kts"] * u["cols"]
                s = u["s"] % SPLIT_SLOTS
                pe.wait_ge(S["lo_done"], u["s"] + 1)
                return (hi[:, s, 0:n].rearrange("p (k c) -> p k c", k=u["kts"]),
                        lo[:, s, 0:n].rearrange("p (k c) -> p k c", k=u["kts"]))

            def three(out, ah, al, wh, wl, start, stop, skip=False, activation_first=True):
                ins = None
                passes = ((ah, wh), (al, wh), (ah, wl))
                for i, (a, w) in enumerate(passes):
                    l, r = (a, w) if activation_first else (w, a)
                    ins = nc.tensor.matmul(out, l, r, start=start and i == 0, stop=stop and i == 2,
                                           skip_group_check=skip)
                return ins

            def token_major(units, ah, al, columns, place, done=None, opened=False, waits=None):
                k_total = sum(u["kts"] for u in units)
                for u in units:
                    wh, wl = parts(u)
                    for b in range(NB):
                        if waits:
                            waits(u, b)
                        sl = slice(b * P, (b + 1) * P)
                        for k in range(u["kts"]):
                            kk = u["k0"] + k
                            for i, c in enumerate(columns):
                                ins = three(place(b, i), ah[:, kk, sl], al[:, kk, sl], wh[:, k, c], wl[:, k, c],
                                            start=kk == 0 and not opened, stop=kk == k_total - 1)
                        if u is units[-1] and done and b == 0:
                            done(ins)
                    used(ins, u)

            def transposes_T(t, before=None):
                norm = norm_of(t) if t >= 2 and (t - 2) % 4 != 1 or t < 2 else None
                for b in range(NB):
                    bank = 4 + 2 * b
                    if norm is not None:
                        pe.wait_ge(S["xs_ready"], xsval(norm, b))
                    if before:
                        before(b)
                    for k in range(KT):
                        ins = nc.tensor.transpose(ps[:, bank + k // 4, (k % 4) * P:(k % 4 + 1) * P],
                                                  xs[:, b, k * P:(k + 1) * P], ident)
                    ins.then_inc(S["xT_ps"], 1)

            def xT(t):
                def waits(u, b):
                    if u["part"] == 0:
                        pe.wait_ge(S["xl_ready"], tval(t, b))
                return waits

            def mod_vector(v, q0=0, q1=4):
                bank = MOD_BANK[v]
                for q in range(q0, q1):
                    u = units_of(("mod", v), q)[0]
                    pe.wait_ge(landed[u["slot"]], u["landed"])
                    w = raw[:, u["slot"], :].rearrange("p (k c) -> p k c", k=KT)
                    dst = ps[:, bank + q // 2, (q % 2) * 256:(q % 2 + 1) * 256]
                    for k in range(KT):
                        nc.tensor.matmul(dst, csb[:, k, :], w[:, k, :], start=(k == 0), stop=False)
                    if v == 0 and q == 0:
                        pe.wait_ge(S["pick_done"], 3)
                    ins = nc.tensor.matmul(dst, pick[:, v, :], brows[:, q * 256:(q + 1) * 256], start=False, stop=True)
                    used(ins, u)

            pe.wait_ge(S["csb_done"], 1)
            mod_vector(0, 0, 1)
            for i in range(2):
                ins = nc.tensor.matmul(ps[:, 4 + i, :], pick[:, ROWS.index("norm1_g"), :], brows[:, i * 512:(i + 1) * 512],
                                       start=True, stop=True)
            ins.then_inc(S["gain_ps"], 1)
            mod_vector(0, 1, 4)
            mod_vector(1)
            transposes_T(0)
            pe.wait_ge(S["relb_done"], 1)
            for head in range(HD):
                at = 0
                while at < HOT:
                    bank, c = (head * HOT + at) // 512, (head * HOT + at) % 512
                    n = min(HOT - at, 512 - c)
                    ins = nc.tensor.matmul(ps[:, bank, c:c + n], rbb[:, head, :], hot[:, at:at + n], start=True, stop=True)
                    at += n
            ins.then_inc(S["relb_ps"], 1)
            for f in range(KT):
                u = units_of("pw1", f)[0]
                wh, wl = parts(u)
                if f == 0:
                    pe.wait_ge(S["xl_ready"], tval(0, 1))
                if f >= 4:
                    pe.wait_ge(S["glu_done"], f - 3)
                for k in range(KT):
                    for c in range(2):
                        cs = slice(c * P, (c + 1) * P)
                        out_ = ps[:, 4 + f % 4, c * SEQ:(c + 1) * SEQ]
                        for i, (a, w) in enumerate(((xh, wh), (xl, wh), (xh, wl))):
                            ins = nc.tensor.matmul(out_, w[:, k, cs], a[:, k, :], start=(k == 0 and c == 0 and i == 0),
                                                   stop=(k == KT - 1 and i == 2), skip_group_check=True)
                used(ins, u)
            pe.wait_ge(S["toep_done"], 1)
            mod_vector(2)

            def tile_taps(k0, k1):
                for k in range(k0, k1):
                    pe.wait_ge(S["diag_ready"], k + 1)
                    ins = nc.tensor.matmul(ps[:, 5, 0:SEQ], diagonals[:, k % DIAGONALS, :], upad[:, PE_TILE, :, k:k + SEG],
                                           start=(k == 0), stop=(k == TAPS - 1))
                    ins.then_inc(S["diag_used"] if k < TAPS - 1 else S["tile_done"], 1)

            pe.wait_ge(S["glu_done"], KT)
            tile_taps(0, DIAGONALS)
            mod_vector(3)
            mod_vector(4, 0, 2)
            tile_taps(DIAGONALS, TAPS)
            pe.wait_ge(S["init_p"], 5)
            order = DVE_GROUPS[0] + POOL_TILES + (PE_TILE,) + DVE_GROUPS[1]
            for i, f in enumerate(order):
                if f == PE_TILE:
                    pe.wait_ge(S["tile_biased"], 1)
                elif f in POOL_TILES:
                    pe.wait_ge(S["tap_added"], TAPS - 1)
                else:
                    pe.wait_ge(S["conv_step"], TAPS * (2 if f in DVE_GROUPS[0] else 4))
                ins = nc.tensor.matmul(ps[:, 6, 0:SEQ], one["ones"], cv[:, f, :], start=(i == 0), stop=(i == KT - 1))
            ins.then_inc(S["mean_ps"], 1)
            mod_vector(4, 2, 3)
            for f in range(KT):
                pe.wait_ge(S["sq_done"], 1 + f // (KT // 2))
                ins = nc.tensor.matmul(ps[:, 7, 0:SEQ], one["ones"], sq[:, f, :], start=(f == 0), stop=(f == KT - 1))
            ins.then_inc(S["var_ps"], 1)
            mod_vector(4, 3, 4)
            halves = [slice(0, 512), slice(512, 1024)]
            pe.wait_ge(S["mod_evac"], 2)
            for b in range(NB):
                for i, c in enumerate(halves):
                    nc.tensor.matmul(ps[:, 2 * b + i, :], pick[:, ROWS.index("b_pw2"), :], brows[:, c], start=True, stop=False)
            token_major(units_of("pw2"), xh, xl, halves, lambda b, i: ps[:, 2 * b + i, :],
                        done=lambda ins: ins.then_inc(S["pw2_ps"], 1), opened=True,
                        waits=lambda u, b: pe.wait_ge(S["yl_done"], u["part"] + 1))
            mod_vector(5)
            pe.wait_ge(S["mod_evac"], 3)
            transposes_T(1)
            def w2_product(j):
                pe.wait_ge(S["gl_done"], 2 * j + 2)
                units = units_of("w2", j)
                for u in units:
                    wh, wl = parts(u)
                    for b in range(NB):
                        sl = slice(b * P, (b + 1) * P)
                        for k in range(u["kts"]):
                            kk = u["k0"] + k
                            for i, c in enumerate(halves):
                                ins = three(ps[:, 2 * b + i, :], gh[:, kk, sl], gl[:, kk, sl], wh[:, k, c], wl[:, k, c],
                                            start=(j == 0 and kk == 0), stop=(j == MLP_CHUNKS - 1 and kk == 3))
                        if j == MLP_CHUNKS - 1 and u is units[-1] and b == 0:
                            ins.then_inc(S["mlp_ps"], 1)
                    used(ins, u)

            for j in range(MLP_CHUNKS):
                xw = xT(1)

                def waits(u, b, j=j):
                    if j == 0:
                        xw(u, b)
                    if j and u["part"] == 0:
                        pe.wait_ge(S["relu_done"], 2 * (j - 1) + b + 1)

                token_major(units_of("w1", j), xh, xl, [slice(0, MLP_CHUNK)], lambda b, i: ps[:, 4 + b, :],
                            done=lambda ins: ins.then_inc(S["w1_ps"], 1), waits=waits)
                if j:
                    w2_product(j - 1)
                for b in range(NB):
                    pe.wait_ge(S["hid_done"], 2 * j + b + 1)
                    if j:
                        pe.wait_ge(S["gl_done"], 2 * (j - 1) + b + 1)
                    for k in range(4):
                        ins = nc.tensor.transpose(ps[:, 6 + b, k * P:(k + 1) * P], hid1[:, b, k * P:(k + 1) * P], ident)
                    ins.then_inc(S["hidT_ps"], 1)
            w2_product(MLP_CHUNKS - 1)

            for layer in range(LAYERS):
                t = 2 + 4 * layer
                glv = 2 * MLP_CHUNKS + (1 + 2 * FF_CHUNKS) * layer
                transposes_T(t)
                units = units_of(("mla", layer))
                for u in units:
                    wh, wl = parts(u)
                    for b in range(NB):
                        if u["part"] == 0:
                            pe.wait_ge(S["xl_ready"], tval(t, b))
                        sl = slice(b * P, (b + 1) * P)
                        for k in range(u["kts"]):
                            kk = u["k0"] + k
                            for i, c in enumerate((slice(0, QL), slice(QL, MLA_COLS))):
                                ins = three(ps[:, 2 * b + i, 0:c.stop - c.start], xh[:, kk, sl], xl[:, kk, sl],
                                            wh[:, k, c], wl[:, k, c], start=kk == 0, stop=kk == KT - 1)
                    used(ins, u)
                for u in units_of(("idx", layer)):
                    wh, wl = parts(u)
                    for k in range(u["kts"]):
                        kk = u["k0"] + k
                        for c in range(4):
                            cs = slice(c * P, (c + 1) * P)
                            for i, (a, w) in enumerate(((xh, wh), (xl, wh), (xh, wl))):
                                nc.tensor.matmul(ps[:, 4 + c // 2, (c % 2) * SEQ:(c % 2 + 1) * SEQ], w[:, k, cs], a[:, kk, :],
                                                 start=(kk == 0 and c % 2 == 0 and i == 0), stop=(kk == KT - 1 and i == 2),
                                                 skip_group_check=True)
                        for b in range(NB):
                            sl = slice(b * P, (b + 1) * P)
                            ins = three(ps[:, 6 + b, 0:DH + HI], xh[:, kk, sl], xl[:, kk, sl], wh[:, k, 512:IDX_COLS],
                                        wl[:, k, 512:IDX_COLS], start=kk == 0, stop=kk == KT - 1)
                    used(ins, u)
                pe.wait_ge(S["cn_done"], 4 * layer + 4)
                for k in range(5):
                    for b in range(NB):
                        at = k * SEQ + b * P
                        ins = nc.tensor.transpose(ps[:, at // 512, at % 512:at % 512 + P], cn[:, b, k * P:(k + 1) * P], ident)
                ins.then_inc(S["cnT_ps"], 1)
                pe.wait_ge(S["ikd_done"], 2 * layer + 2)
                for b in range(NB):
                    ins = nc.tensor.transpose(ps[:, 3, b * P:(b + 1) * P], ikd[:, b, :], ident)
                ins.then_inc(S["ikT_ps"], 1)
                pe.wait_ge(S["iw_done"], layer + 1)
                units = units_of(("dsa", layer))
                for u in units:
                    wh, wl = parts(u)
                    for k in range(u["kts"]):
                        kk = u["k0"] + k
                        for c in range(3):
                            cs = slice(c * P, (c + 1) * P)
                            for i, (a, w) in enumerate(((xh, wh), (xl, wh), (xh, wl))):
                                nc.tensor.matmul(ps[:, 6 + c // 2, (c % 2) * SEQ:(c % 2 + 1) * SEQ], w[:, k, cs], a[:, kk, :],
                                                 start=(kk == 0 and c % 2 == 0 and i == 0), stop=(kk == KT - 1 and i == 2),
                                                 skip_group_check=True)
                        for b in range(NB):
                            sl = slice(b * P, (b + 1) * P)
                            for i, (a, w) in enumerate(((xh, wh), (xl, wh), (xh, wl))):
                                ins = nc.tensor.matmul(ps[:, 7, SEQ + b * DH:SEQ + (b + 1) * DH], a[:, kk, sl],
                                                       w[:, k, 3 * P:DSA_COLS], start=False,
                                                       stop=(kk == KT - 1 and i == 2), skip_group_check=True)
                    used(ins, u)

                def lora_product(stage, cols, k0):
                    u = units_of((stage, layer))[0]
                    wh, wl = parts(u)
                    for b in range(NB):
                        sl = slice(b * P, (b + 1) * P)
                        for k in range(u["kts"]):
                            for i in range(2):
                                c = slice(i * cols // 2, (i + 1) * cols // 2)
                                ins = three(ps[:, 2 * b + i, 0:cols // 2], gh[:, k0 + k, sl], gl[:, k0 + k, sl],
                                            wh[:, k, c], wl[:, k, c], start=k == 0, stop=k == u["kts"] - 1)
                    used(ins, u)

                pe.wait_ge(S["gl_done"], glv + 1)
                pe.wait_ge(S["ikT_done"], layer + 1)
                lora_product("uq", UQ_COLS, 0)
                pe.wait_ge(S["iqT_done"], layer + 1)
                pe.wait_ge(S["dsa_evac"], 5 * (layer + 1))
                for slot, head in enumerate(ORDER8):
                    r = slice(DH * (head % 2), DH * (head % 2) + DH)
                    ins = nc.tensor.matmul(ps[:, 4 + slot // 2, (slot % 2) * SEQ:(slot % 2 + 1) * SEQ], iqT[r, head // 2, P:2 * P],
                                           ikT[r, :], start=True, stop=True)
                ins.then_inc(S["isc_ps"], 1)
                pe.wait_ge(S["q7_done"], 2 * layer + 2)
                lora_product("ukv", UKV_COLS, 3)
                pe.wait_ge(S["relu_i"], 2 * layer + 1)
                for slot, head in enumerate(ORDER8_B0):
                    r = slice(DH * (head % 2), DH * (head % 2) + DH)
                    ins = nc.tensor.matmul(ps[:, 4 + slot // 4, (slot % 4) * P:(slot % 4 + 1) * P], iqT[r, head // 2, 0:P],
                                           ikT[r, 0:P], start=True, stop=True)
                ins.then_inc(S["isc_ps"], 1)
                for u in units_of(("sb", layer)):
                    wh, wl = parts(u)
                    for k in range(u["kts"]):
                        kk = u["k0"] + k
                        for c in range(4):
                            cs = slice(c * P, (c + 1) * P)
                            for i, (a, w) in enumerate(((xh, wh), (xl, wh), (xh, wl))):
                                ins = nc.tensor.matmul(ps[:, 6 + c // 2, (c % 2) * SEQ:(c % 2 + 1) * SEQ], w[:, k, cs], a[:, kk, :],
                                                       start=(kk == 0 and c % 2 == 0 and i == 0),
                                                       stop=(kk == KT - 1 and i == 2), skip_group_check=True)
                    used(ins, u)
                pe.wait_ge(S["rope_done"], 2 * layer + 2)
                pe.wait_ge(S["kv_done"], 4 * layer + 4)
                for hh in range(HM):
                    for b in range(NB):
                        at = hh * SEQ + b * P
                        ins = nc.tensor.transpose(ps[0:QK, at // 512, at % 512:at % 512 + P], q7[:, b, hh, :], ident)
                ins.then_inc(S["qkT_ps"], 1)
                pe.wait_ge(S["kf_done"], 2 * layer + 2)
                pe.wait_ge(S["relu_i"], 2 * layer + 2)
                for hh in range(HM):
                    for b in range(NB):
                        at = hh * SEQ + b * P
                        ins = nc.tensor.transpose(ps[0:QK, 3 + at // 512, at % 512:at % 512 + P], kfull[:, b, hh, :], ident)
                ins.then_inc(S["qkT_ps"], 1)

                def values_unit(part):
                    u = units_of(("sv", layer))[part]
                    wh, wl = parts(u)
                    places = ((0, 7, 0, 0, SV), (1, 7, SV, 0, 3 * DH), (1, 6, SEQ, 3 * DH, SV))
                    for k in range(u["kts"]):
                        kk = u["k0"] + k
                        for i, (a, w) in enumerate(((xh, wh), (xl, wh), (xh, wl))):
                            nc.tensor.matmul(ps[:, 6, 0:SEQ], w[:, k, SV:SV_COLS], a[:, kk, :], start=(kk == 0 and i == 0),
                                             stop=(kk == KT - 1 and i == 2), skip_group_check=True)
                            for b, bank, at, c0, c1 in places:
                                ins = nc.tensor.matmul(ps[:, bank, at:at + c1 - c0], a[:, kk, b * P:(b + 1) * P], w[:, k, c0:c1],
                                                       start=(kk == 0 and i == 0 and b == 0),
                                                       stop=(kk == KT - 1 and i == 2), skip_group_check=True)
                    used(ins, u)

                pe.wait_ge(S["sb_evac"], 2 * (layer + 1))
                values_unit(0)
                if layer == 0:
                    pe.wait_ge(S["masks_done"], 3)
                pe.wait_ge(S["qT_done"], layer + 1)
                pe.wait_ge(S["kT_done"], layer + 1)
                for b in (1, 0):
                    nk = P * (b + 1)
                    for hh in range(HM):
                        at = hh * nk
                        bank = (0 if b else 3) + at // 512
                        nc.tensor.matmul(ps[:, bank, at % 512:at % 512 + nk], qT[0:QK, hh, b * P:(b + 1) * P], kT[0:QK, hh, 0:nk],
                                         start=True, stop=False, skip_group_check=True)
                        at += nk - P
                        ins = nc.tensor.matmul(ps[:, bank, at % 512:at % 512 + P], ident16[:], masks16[:, 0, :],
                                               start=False, stop=True, skip_group_check=True)
                    ins.then_inc(S["m_sc"], 1)
                values_unit(1)
                pe.wait_ge(S["m_exp"], 2 * HM * layer + HM)
                for hh in range(HM):
                    for k in range(2):
                        at = (2 * hh + k) * P
                        ins = nc.tensor.transpose(ps[:, at // 512, at % 512:at % 512 + P], pm[1][:, hh, k * P:(k + 1) * P], ident)
                ins.then_inc(S["m_pT_ps"], 1)

                rows_of = [(slice(0, DH), 0, 2), (slice(DH, P), 0, 2), (slice(0, DH), 1, 3), (slice(DH, P), 1, 3),
                           (slice(0, DH), 4, 5)]

                def group_heads(g):
                    heads, banks = SB_GROUPS[g]
                    return [(hh, banks.start + hh - heads.start) for hh in range(heads.start, heads.stop)]

                def logits(g):
                    for hh, bank in group_heads(g):
                        r, tq, tk = rows_of[hh]
                        nc.tensor.matmul(ps[:, bank, 0:2 * P], sT[r, tk, 0:P], sT[r, tq, :], start=True, stop=False,
                                         skip_group_check=True)
                        nc.tensor.matmul(ps[:, bank, 2 * P:3 * P], sT[r, tk, P:2 * P], sT[r, tq, P:2 * P], start=False,
                                         stop=False, skip_group_check=True)
                        for c in (0, 2):
                            ins = nc.tensor.matmul(ps[:, bank, c * P:(c + 1) * P], ident16[:], masks16[:, 1, :], start=False,
                                                   stop=True, skip_group_check=True)
                    ins.then_inc(S["s_z"], 1)

                def logit_sums(g):
                    pe.wait_ge(S["s_sp"], len(SB_GROUPS) * layer + g + 1)
                    for hh, bank in group_heads(g):
                        for dst, w, src in ((slice(0, P), tri, slice(0, P)), (slice(P, 2 * P), tri, slice(P, 2 * P)),
                                            (slice(P, 2 * P), neg_ones[:], slice(2 * P, 3 * P)),
                                            (slice(2 * P, 3 * P), tri, slice(2 * P, 3 * P))):
                            ins = nc.tensor.matmul(ps[:, bank, dst], w, sbt[:, hh, src], start=False, stop=True,
                                                   skip_group_check=True)
                    ins.then_inc(S["s_zs"], 1)

                pe.wait_ge(S["sv_evac"], 3 * (layer + 1))
                pe.wait_ge(S["c4_evac"], 2 * (layer + 1))
                logits(0)
                pe.wait_ge(S["m_exp"], 2 * HM * (layer + 1))
                for hh in range(HM):
                    at = hh * P
                    ins = nc.tensor.transpose(ps[:, 3 + at // 512, at % 512:at % 512 + P], pm[0][:, hh, :], ident)
                ins.then_inc(S["m_pT_ps"], 1)
                pe.wait_ge(S["m_pT"], 2 * layer + 1)
                v = pmT[1].rearrange("p (h k q) -> p h k q", h=HM, k=2)
                for hh in range(HM):
                    for k in range(2):
                        ins = nc.tensor.matmul(ps[:, 2, hh * VD:(hh + 1) * VD], v[:, hh, k, :], mv[:, k, hh, :],
                                               start=k == 0, stop=k == 1)
                ins.then_inc(S["m_o"], 1)
                logits(1)
                pe.wait_ge(S["m_pT"], 2 * layer + 2)
                for hh in range(HM):
                    ins = nc.tensor.matmul(ps[:, 3, hh * VD:(hh + 1) * VD], pmT[0][:, hh * P:(hh + 1) * P], mv[:, 0, hh, :],
                                           start=True, stop=True)
                ins.then_inc(S["m_o"], 1)
                logit_sums(0)

                def dsa_logits(b):
                    nk = P * (b + 1)
                    for slot, head in enumerate(ORDER5):
                        r = slice(DH * (head % 2), DH * (head % 2) + DH)
                        ins = nc.tensor.matmul(ps[:, (2 if b else 5) + slot // 2, (slot % 2) * SEQ:(slot % 2) * SEQ + nk],
                                               dT[r, head // 2, b * P:(b + 1) * P], dkT[r, 0:nk], start=True, stop=True)
                    ins.then_inc(S["d_sc"], 1)

                pe.wait_ge(S["mix_m"], 2 * layer + 2)
                dsa_logits(1)
                logit_sums(1)
                pe.wait_ge(S["s_w"], len(SB_GROUPS) * (layer + 1))
                dsa_logits(0)
                for b in (1, 0):
                    for hh in range(HS):
                        o = ps[:, 1 - b, hh * DH:(hh + 1) * DH]
                        if b:
                            nc.tensor.matmul(o, sbt[:, hh, P:2 * P], sv[:, 0, hh * DH:(hh + 1) * DH], start=True, stop=False)
                            ins = nc.tensor.matmul(o, sbt[:, hh, 2 * P:3 * P], sv[:, 1, hh * DH:(hh + 1) * DH], start=False, stop=True)
                        else:
                            ins = nc.tensor.matmul(o, sbt[:, hh, 0:P], sv[:, 0, hh * DH:(hh + 1) * DH], start=True, stop=True)
                    ins.then_inc(S["s_o"], 1)
                pe.wait_ge(S["d_exp"], 2 * HD * layer + HD)
                for slot in range(HD):
                    for k in range(2):
                        at = (2 * slot + k) * P
                        ins = nc.tensor.transpose(ps[:, 2 + at // 512, at % 512:at % 512 + P], pd[1][:, slot, k * P:(k + 1) * P], ident)
                ins.then_inc(S["d_pT_ps"], 1)
                pe.wait_ge(S["d_exp"], 2 * HD * (layer + 1))
                for slot in range(HD):
                    at = slot * P
                    ins = nc.tensor.transpose(ps[:, 5 + at // 512, at % 512:at % 512 + P], pd[0][:, slot, :], ident)
                ins.then_inc(S["d_pT_ps"], 1)
                pe.wait_ge(S["d_pT"], 2 * layer + 2)
                for b in (1, 0):
                    for slot, head in enumerate(ORDER5):
                        o = ps[:, 7 if b else 2, head * DH:(head + 1) * DH]
                        nkt = b + 1
                        for k in range(nkt):
                            at = (nkt * slot + k) * P
                            ins = nc.tensor.matmul(o, pdT[b][:, at:at + P], dv[:, k, :], start=k == 0, stop=k == nkt - 1)
                    ins.then_inc(S["d_o"], 1)
                pe.wait_ge(S["mix_s"], 2 * layer + 2)
                pe.wait_ge(S["mix_d"], 2 * layer + 2)
                transposes_T(t + 1)
                token_major(units_of(("wo", layer)), xh, xl, halves, lambda b, i: ps[:, 2 * b + i, :],
                            done=lambda ins: ins.then_inc(S["wo_ps"], 1), waits=xT(t + 1))
                transposes_T(t + 2)

                def dn_product(j):
                    pe.wait_ge(S["gl_done"], glv + 1 + 2 * (j + 1))
                    u = units_of(("dn", layer), j)[0]
                    wh, wl = parts(u)
                    final = j == FF_CHUNKS - 1
                    for b in range(NB):
                        sl = slice(b * P, (b + 1) * P)
                        for k in range(u["kts"]):
                            for i, c in enumerate(halves):
                                ins = three(ps[:, 2 * b + i, :], gh[:, k, sl], gl[:, k, sl], wh[:, k, c], wl[:, k, c],
                                            start=(j == 0 and k == 0), stop=final and k == 1)
                        if final and b == 0:
                            ins.then_inc(S["dn_ps"], 1)
                    used(ins, u)

                for j in range(FF_CHUNKS):
                    xw = xT(t + 2)
                    k_ = FF_CHUNKS * layer + j

                    def waits(u, b, j=j, k_=k_):
                        if j == 0:
                            xw(u, b)
                        elif u["part"] == 0:
                            pe.wait_ge(S["hid_g"], 2 * (k_ - 1) + b + 1)

                    token_major(units_of(("gu", layer), j), xh, xl, [slice(0, 512)], lambda b, i: ps[:, 4 + b, :],
                                done=lambda ins: ins.then_inc(S["gu_ps"], 1), waits=waits)
                    if j == 1:
                        pe.wait_ge(S["h_ready"], hval(4 + 3 * layer, 1))
                    if j:
                        dn_product(j - 1)
                    for b in range(NB):
                        pe.wait_ge(S["hid_g"], 2 * k_ + b + 1)
                        if j:
                            pe.wait_ge(S["gl_done"], glv + 1 + 2 * (j - 1) + b + 1)
                        for k in range(2):
                            ins = nc.tensor.transpose(ps[:, 6 + b, k * P:(k + 1) * P], hid2[:, b, k * P:(k + 1) * P], ident)
                        ins.then_inc(S["hidT_ps"], 1)
                dn_product(FF_CHUNKS - 1)
                pe.wait_ge(S["pl_done"], layer + 1)
                u = units_of(("proj", layer))[0]
                wh, wl = parts(u)
                for b in range(NB):
                    sl = slice(b * P, (b + 1) * P)
                    for k in range(2):
                        for i, c in enumerate(halves):
                            ins = three(ps[:, 4 + 2 * b + i, :], gh[:, 2 + k, sl], gl[:, 2 + k, sl], wh[:, k, c], wl[:, k, c],
                                        start=k == 0, stop=k == 1)
                    if b == 0:
                        ins.then_inc(S["proj_ps"], 1)
                used(ins, u)
                transposes_T(t + 3, before=lambda b: pe.wait_ge(S[f"proj_evac{b}"], layer + 1))
                xw3 = xT(t + 3)

                token_major(units_of(("gate", layer)), xh, xl, halves, lambda b, i: ps[:, 2 * b + i, :],
                            done=lambda ins: ins.then_inc(S["gate_ps"], 1), waits=xw3)


def bucket_table():
    d = (2 * P - 1 - np.arange(HOT)).astype(np.int64)
    exact = BUCKETS // 2
    dd = np.maximum(d, 1).astype(np.float32)
    large = exact + (np.log(dd / np.float32(exact)) / np.float32(np.log(MAX_DIST / exact)) * (BUCKETS - exact)).astype(np.int32)
    bucket = np.where(d < exact, d, np.minimum(large, BUCKETS - 1))
    table = np.zeros((P, HOT), np.float32)
    for i in range(HOT):
        if d[i] >= 0:
            table[bucket[i], i] = 1.0
        else:
            table[BUCKETS, i] = NEG
    return table


def constants():
    c = np.zeros((P, C_END), np.float32)
    a, b = np.arange(P)[:, None], np.arange(P)[None, :]
    c[:, C_ID:C_ID + P] = a == b
    c[:, C_TRI:C_TRI + P] = -1.0 * (a >= b)
    c[:, C_CAUSAL:C_CAUSAL + P] = np.where(b > a, NEG, 0.0)
    c[:, C_STRICT:C_STRICT + P] = np.where(a >= b, NEG, 0.0)
    inv = np.float32(10000.0) ** (-np.arange(HALF, dtype=np.float32) / np.float32(HALF))
    ang = np.arange(SEQ, dtype=np.float32)[:, None] * inv[None, :]
    for tab, at in ((np.cos(ang), C_COS), (np.sin(ang), C_SIN)):
        c[:, at:at + NB * HALF] = tab.astype(np.float32).reshape(NB, P, HALF).transpose(1, 0, 2).reshape(P, NB * HALF)
    c[:, C_HOT:] = bucket_table()
    return c


def lay_out(inputs):
    g = lambda n: np.ascontiguousarray(inputs[n])
    flat = np.empty(STREAM, np.float32)

    def put(stage, n, w):
        for u in units_of(stage, n):
            part = w[u["k0"] * P:(u["k0"] + u["kts"]) * P]
            assert part.shape[1] == u["cols"]
            flat[u["offset"]:u["offset"] + part.size] = part.reshape(u["kts"], P, u["cols"]).transpose(1, 0, 2).reshape(-1)

    wm = g("w_mod")[0]
    order = [1, 0, 2, 3, 4, 5]
    for v, src in enumerate(order):
        for q in range(4):
            put(("mod", v), q, wm[:, src * D + q * 256:src * D + (q + 1) * 256])
    pw1 = g("conv_w_pw1")[0]
    for f in range(KT):
        put("pw1", f, np.concatenate([pw1[:, f * P:(f + 1) * P], pw1[:, D + f * P:D + (f + 1) * P]], 1))
    put("pw2", 0, g("conv_w_pw2")[0])
    w1, w2 = g("mlp_w1")[0], g("mlp_w2")[0]
    for j in range(MLP_CHUNKS):
        put("w1", j, w1[:, j * MLP_CHUNK:(j + 1) * MLP_CHUNK])
        put("w2", j, w2[j * MLP_CHUNK:(j + 1) * MLP_CHUNK])
    for layer in range(LAYERS):
        w = g("w_in_2")[layer]
        at = np.cumsum([0, QL, KVL, ROPE, HD * DH, DH, DH, HI * DH, DH, HI, HS * DH, HS * DH, HS * DH])
        put(("idx", layer), 0, w[:, at[6]:at[9]])
        put(("mla", layer), 0, w[:, at[0]:at[3]])
        put(("dsa", layer), 0, w[:, at[3]:at[6]])
        q, k = at[9], at[10]
        half = (HS - 1) * DH
        put(("sb", layer), 0, np.concatenate([w[:, q:q + half], w[:, k:k + half]], 1))
        put(("sv", layer), 0, np.concatenate([w[:, at[11]:at[12]], w[:, q + half:q + SV], w[:, k + half:k + SV]], 1))
        put(("uq", layer), 0, g("mla_w_uq_2")[layer])
        put(("ukv", layer), 0, g("mla_w_ukv_2")[layer])
        put(("wo", layer), 0, g("w_o_2")[layer])
        wg, wu, wd = g("w_gate_2")[layer], g("w_up_2")[layer], g("w_down_2")[layer]
        for j in range(FF_CHUNKS):
            c = slice(j * FF_CHUNK, (j + 1) * FF_CHUNK)
            put(("gu", layer), j, np.concatenate([wg[:, c], wu[:, c]], 1))
            put(("dn", layer), j, wd[c])
        put(("proj", layer), 0, g("w_ple_proj_2")[layer])
        put(("gate", layer), 0, g("w_ple_gate_2")[layer])

    cols = lambda v: v.reshape(-1, P).T
    vectors = np.concatenate([cols(g("c")[0]), cols(g("conv_b_pw1")[0]), cols(g("conv_b_dw")[0]), cols(g("conv_ln_g")[0]),
                              cols(g("conv_ln_b")[0]),
                              g("conv_w_dw")[0].reshape(TAPS, KT, P).transpose(2, 1, 0).reshape(P, KT * TAPS)], 1)
    bm = g("b_mod")[0]
    stack = {f"b_mod{i}": bm[i * D:(i + 1) * D] for i in range(6)}
    stack.update(b_pw2=g("conv_b_pw2")[0], norm1_g=g("norm1_g")[0])
    table = np.zeros((LOW_ROW + len(ROWS), D), np.float32)
    for i, n in enumerate(ROWS):
        table[i] = table[LOW_ROW + i] = stack[n]
    rows = dict(stack=table, norm2_g=g("norm2_g")[0], final_g=g("final_g"),
                final=g("final_norm_2"))
    for l in range(LAYERS):
        rows[f"attn{l}"] = g("attn_norm_2")[l]
        rows[f"ffn{l}"] = g("ffn_norm_2")[l]
        rows[f"ple{l}"] = g("ple_norm_2")[l]
        rows[f"lora{l}"] = np.concatenate([g("mla_q_norm_2")[l], g("mla_kv_norm_2")[l]])
    rel = np.concatenate([g("rel_bias_2"), np.ones((1, HD), np.float32)], 0)
    arrays = dict(stream=flat, x=g("x")[0], p_t=np.ascontiguousarray(g("p_2")[:, 0].transpose(0, 2, 1)),
                  vectors=np.ascontiguousarray(vectors), rel=rel, consts=constants())
    for k, v in rows.items():
        arrays["row_" + k] = np.ascontiguousarray(v)
    return arrays


def kernel(**inputs):
    import concourse.bacc as bacc
    from concourse.bass_utils import run_bass_kernel_spmd as run

    nc = bacc.Bacc("TRN2", target_bir_lowering=False, num_devices=1)
    arrays = lay_out(inputs)
    aps = {n: nc.dram_tensor(n, a.shape, mybir.dt.from_np(a.dtype), kind="ExternalInput").ap() for n, a in arrays.items()}
    rows = {n[4:]: ap for n, ap in aps.items() if n.startswith("row_")}
    out = nc.dram_tensor("out", (SEQ, D), F32, kind="ExternalOutput").ap()
    build(nc, aps["stream"], aps["x"], aps["p_t"], aps["vectors"], rows, aps["rel"], aps["consts"], out)
    r = run(nc, [arrays], core_ids=[0])
    return r.results[0]["out"].reshape(1, SEQ, D)
```
